# Optimizing a Trainium2 kernel written in Bass

```python
import jax
import jax.numpy as jnp
from jax import lax
import numpy as np
import math
import jax, jax.numpy as jnp

D_MODEL = 1024
BATCH = 1
SEQ = 512
DEPTH = 1

CTX_LEN = 256
GRID_W = 64
D_MIX = D_MODEL
HEAD_DIM = 64
D_POOL = D_MIX // 4
D_RWKV = (D_MIX - D_POOL) // 2
D_HGRN = D_MIX - D_POOL - D_RWKV
POOL_WINDOWS = (2, 4, 8, 16)
N_POOL_GROUPS = len(POOL_WINDOWS)
POOL_GROUP = D_POOL // N_POOL_GROUPS
H_RWKV = D_RWKV // HEAD_DIM
H_HGRN = D_HGRN // HEAD_DIM
LORA_W = 64
LORA_A = 64
N_DIR = 2
HGRN_CHUNK = 32
D_RWKV_IN = 3 * D_RWKV + N_DIR * (LORA_W + LORA_A)
D_IN = D_POOL + D_RWKV_IN + 2 * D_HGRN + N_DIR * D_HGRN + D_MIX
ALPHA = float((2 * DEPTH) ** 0.25)
BETA = float((8 * DEPTH) ** -0.25)
LN_EPS = 1e-5
GN_EPS = 64e-5
RMS_EPS = 1e-6


def _layer_norm(x):
    xf = x.astype(jnp.float32)
    mu = jnp.mean(xf, axis=-1, keepdims=True)
    var = jnp.mean(jnp.square(xf - mu), axis=-1, keepdims=True)
    return (xf - mu) * lax.rsqrt(var + LN_EPS)

def _heads(z):
    return z.reshape(z.shape[:-1] + (z.shape[-1] // HEAD_DIM, HEAD_DIM))

def _split_proj(p):
    o0 = D_POOL
    o1 = o0 + D_RWKV_IN
    o2 = o1 + 2 * D_HGRN + N_DIR * D_HGRN
    return p[..., :o0], p[..., o0:o1], p[..., o1:o2], p[..., o2:]

def _centred_mean(u, axis, window):
    n = u.shape[axis]
    left = window // 2
    right = window - 1 - left
    t = jnp.arange(n)
    lo = jnp.maximum(t - left, 0)
    hi = jnp.minimum(t + right, n - 1) + 1
    pad = [(0, 0)] * u.ndim
    pad[axis] = (1, 0)
    cs = jnp.pad(jnp.cumsum(u, axis=axis), pad)
    total = jnp.take(cs, hi, axis=axis) - jnp.take(cs, lo, axis=axis)
    shape = [1] * u.ndim
    shape[axis] = n
    count = (hi - lo).astype(jnp.float32).reshape(shape)
    return total / count

def _pool_branch(u, grid, pool_w, pool_scale):
    b, n, _ = u.shape
    uf = u.astype(jnp.float32)
    if grid:
        rows = n // GRID_W
        uf = uf.reshape(b, rows, GRID_W, D_POOL)
        axis = 2
    else:
        axis = 1
    groups = []
    for g, win in enumerate(POOL_WINDOWS):
        ch = uf[..., g * POOL_GROUP:(g + 1) * POOL_GROUP]
        groups.append(_centred_mean(ch, axis, win) - ch)
    pooled = jnp.stack(groups, axis=-2)
    mixed = jnp.einsum('...gi,gio->...go', pooled, pool_w)
    return mixed.reshape(b, n, D_POOL) * pool_scale

def _shift3(u, w):
    up = jnp.pad(u, ((0, 0), (1, 1), (0, 0)))
    return w[0] * up[:, :-2] + w[1] * up[:, 1:-1] + w[2] * up[:, 2:]

def _rwkv_dir_inputs(u, d, w0, w_up, a0, a_up, k_k, k_a):
    r = u[..., :D_RWKV]
    k = u[..., D_RWKV:2 * D_RWKV]
    v = u[..., 2 * D_RWKV:3 * D_RWKV]
    o = 3 * D_RWKV
    xw = u[..., o + d * LORA_W:o + (d + 1) * LORA_W]
    o2 = o + N_DIR * LORA_W
    xa = u[..., o2 + d * LORA_A:o2 + (d + 1) * LORA_A]
    w_log = -jax.nn.softplus(-(w0[d] + jnp.tanh(xw) @ w_up[d])) - 0.5
    decay = jnp.exp(-jnp.exp(w_log))
    a = jax.nn.sigmoid(a0[d] + xa @ a_up[d])
    kk = _heads(k * k_k)
    kk = kk * lax.rsqrt(jnp.sum(kk * kk, axis=-1, keepdims=True) + 1e-12)
    k_mod = k * (1.0 + (a - 1.0) * k_a)
    return (_heads(r), _heads(decay), _heads(k_mod), _heads(v), kk, _heads(a))

def _rwkv_bonus(ins, r_k_d):
    r, k_mod, v = ins[0], ins[2], ins[3]
    return jnp.sum(r * k_mod * r_k_d, axis=-1, keepdims=True) * v

def _rwkv_scan(state, ins, emit):
    r, w, k, v, kk, a = (jnp.moveaxis(z, 1, 0) for z in ins)
    xs = (w, k, v, kk, a, r) if emit else (w, k, v, kk, a)

    def step(S, inp):
        w_t, k_t, v_t, kk_t, a_t = inp[:5]
        sa = jnp.einsum('bhvk,bhk->bhv', S, kk_t)
        S = (S * w_t[:, :, None, :] - sa[..., None] * (kk_t * a_t)[:, :, None, :]
             + v_t[..., None] * k_t[:, :, None, :])
        y = jnp.einsum('bhvk,bhk->bhv', S, inp[5]) if emit else None
        return S, y

    state, ys = lax.scan(step, state, xs)
    return state, (jnp.moveaxis(ys, 0, 1) if emit else None)

def _rwkv_readout(y, bonus, gn_g, gn_b):
    mu = jnp.mean(y, axis=-1, keepdims=True)
    var = jnp.mean(jnp.square(y - mu), axis=-1, keepdims=True)
    yn = (y - mu) * lax.rsqrt(var + GN_EPS) * gn_g.reshape(H_RWKV, HEAD_DIM) + gn_b.reshape(H_RWKV, HEAD_DIM)
    out = yn + bonus
    return out.reshape(out.shape[:-2] + (D_RWKV,))

def _rwkv_branch(u_ctx, u_lat, w0, w_up, a0, a_up, k_k, k_a, r_k, gn_g, gn_b, emit_ctx):
    b = u_lat.shape[0]
    y_ctx, y_lat, bonus_ctx, bonus_lat = 0.0, 0.0, 0.0, 0.0
    for d in range(N_DIR):
        ins_c = _rwkv_dir_inputs(u_ctx, d, w0, w_up, a0, a_up, k_k, k_a)
        ins_l = _rwkv_dir_inputs(u_lat, d, w0, w_up, a0, a_up, k_k, k_a)
        bonus_lat = bonus_lat + _rwkv_bonus(ins_l, r_k[d])
        if emit_ctx:
            bonus_ctx = bonus_ctx + _rwkv_bonus(ins_c, r_k[d])
        if d == 1:
            ins_c = tuple(jnp.flip(z, axis=1) for z in ins_c)
            ins_l = tuple(jnp.flip(z, axis=1) for z in ins_l)
        s0 = jnp.zeros((b, H_RWKV, HEAD_DIM, HEAD_DIM), jnp.float32)
        s_c, yc = _rwkv_scan(s0, ins_c, emit_ctx)
        _, yl = _rwkv_scan(s_c, ins_l, True)
        if d == 1:
            yl = jnp.flip(yl, axis=1)
            if emit_ctx:
                yc = jnp.flip(yc, axis=1)
        y_lat = y_lat + yl
        if emit_ctx:
            y_ctx = y_ctx + yc
    out_lat = _rwkv_readout(y_lat, bonus_lat, gn_g, gn_b)
    out_ctx = _rwkv_readout(y_ctx, bonus_ctx, gn_g, gn_b) if emit_ctx else None
    return out_ctx, out_lat

def _hgrn_dir_inputs(fh, d, lb_d):
    q = fh[..., :D_HGRN]
    i = fh[..., D_HGRN:2 * D_HGRN]
    z = fh[..., (2 + d) * D_HGRN:(3 + d) * D_HGRN]
    logf = jnp.logaddexp(jnp.log(lb_d), jnp.log1p(-lb_d) + jax.nn.log_sigmoid(z))
    k = (1.0 - lb_d) * jax.nn.sigmoid(-z)
    return (_heads(k), _heads(i), _heads(logf), _heads(q))

def _hgrn_scan(state, ins, emit):
    k, i, logf, q = ins
    b, n, h, dk = k.shape
    nc = n // HGRN_CHUNK

    def chunks(z):
        return z.reshape(b, nc, HGRN_CHUNK, h, dk).transpose(1, 0, 3, 2, 4)

    causal = jnp.tril(jnp.ones((HGRN_CHUNK, HGRN_CHUNK), dtype=bool))[:, :, None]

    def step(S, inp):
        k_c, i_c, lf_c = inp[:3]
        g = jnp.cumsum(lf_c, axis=2)
        g_last = g[:, :, -1:, :]
        if emit:
            q_c = inp[3]
            inter = jnp.einsum('bhtk,bhkv->bhtv', q_c * jnp.exp(g), S)
            rel = jnp.exp(jnp.where(causal, g[:, :, :, None, :] - g[:, :, None, :, :], -jnp.inf))
            scores = jnp.einsum('bhtk,bhsk,bhtsk->bhts', q_c, k_c, rel)
            o = inter + jnp.einsum('bhts,bhsv->bhtv', scores, i_c)
        else:
            o = None
        S = (jnp.exp(g_last[:, :, 0, :])[..., None] * S
             + jnp.einsum('bhsk,bhsv->bhkv', k_c * jnp.exp(g_last - g), i_c))
        return S, o

    xs = (chunks(k), chunks(i), chunks(logf), chunks(q)) if emit else (chunks(k), chunks(i), chunks(logf))
    state, o = lax.scan(step, state, xs)
    if emit:
        o = o.transpose(1, 0, 3, 2, 4).reshape(b, n, h, dk)
    return state, o

def _rms_heads(o, norm_g):
    on = o * lax.rsqrt(jnp.mean(o * o, axis=-1, keepdims=True) + RMS_EPS) * norm_g.reshape(H_HGRN, HEAD_DIM)
    return on.reshape(on.shape[:-2] + (D_HGRN,))

def _hgrn_branch(fh_ctx, fh_lat, lb, norm_g, emit_ctx):
    b = fh_lat.shape[0]
    o_ctx, o_lat = 0.0, 0.0
    for d in range(N_DIR):
        ins_c = _hgrn_dir_inputs(fh_ctx, d, lb[d])
        ins_l = _hgrn_dir_inputs(fh_lat, d, lb[d])
        if d == 1:
            ins_c = tuple(jnp.flip(z, axis=1) for z in ins_c)
            ins_l = tuple(jnp.flip(z, axis=1) for z in ins_l)
        s0 = jnp.zeros((b, H_HGRN, HEAD_DIM, HEAD_DIM), jnp.float32)
        s_c, oc = _hgrn_scan(s0, ins_c, emit_ctx)
        _, ol = _hgrn_scan(s_c, ins_l, True)
        if d == 1:
            ol = jnp.flip(ol, axis=1)
            if emit_ctx:
                oc = jnp.flip(oc, axis=1)
        o_lat = o_lat + ol
        if emit_ctx:
            o_ctx = o_ctx + oc
    out_ctx = _rms_heads(o_ctx, norm_g) if emit_ctx else None
    return out_ctx, _rms_heads(o_lat, norm_g)

def first_inputs(seed: int = 0) -> dict:
    key = jax.random.key(seed)
    ks = jax.random.split(key, 24)
    f32 = jnp.float32

    def nrm(k, shape, scale):
        return scale * jax.random.normal(k, shape, f32)

    return {
        "x": nrm(ks[0], (BATCH, SEQ, D_MODEL), 1.0),
        "c": nrm(ks[1], (BATCH, D_MODEL), 1.0),
        "ctx": nrm(ks[2], (BATCH, CTX_LEN, D_MODEL), 1.0),
        "c_ctx": nrm(ks[3], (D_MODEL,), 1.0),
        "mod_w": nrm(ks[4], (DEPTH, D_MODEL, 3 * D_MODEL), D_MODEL ** -0.5),
        "mod_b": nrm(ks[5], (DEPTH, 3 * D_MODEL), 0.02),
        "w_in": nrm(ks[6], (DEPTH, D_MODEL, D_IN), D_MODEL ** -0.5),
        "rwkv_shift": jnp.array([0.25, 0.5, 0.25], f32)[None, :, None] + nrm(ks[7], (DEPTH, 3, D_RWKV_IN), 0.05),
        "pool_w": nrm(ks[8], (DEPTH, N_POOL_GROUPS, POOL_GROUP, POOL_GROUP), POOL_GROUP ** -0.5),
        "pool_scale": 1.0 + nrm(ks[9], (DEPTH, D_POOL), 0.1),
        "rwkv_w0": jax.random.uniform(ks[10], (DEPTH, N_DIR, D_RWKV), f32, minval=-5.0, maxval=-0.5),
        "rwkv_w_up": nrm(ks[11], (DEPTH, N_DIR, LORA_W, D_RWKV), 0.5 * LORA_W ** -0.5),
        "rwkv_a0": nrm(ks[12], (DEPTH, N_DIR, D_RWKV), 0.1),
        "rwkv_a_up": nrm(ks[13], (DEPTH, N_DIR, LORA_A, D_RWKV), LORA_A ** -0.5),
        "rwkv_k_k": 0.85 + nrm(ks[14], (DEPTH, D_RWKV), 0.05),
        "rwkv_k_a": 1.0 + nrm(ks[15], (DEPTH, D_RWKV), 0.05),
        "rwkv_r_k": nrm(ks[16], (DEPTH, N_DIR, H_RWKV, HEAD_DIM), 0.1),
        "rwkv_gn_g": 1.0 + nrm(ks[17], (DEPTH, D_RWKV), 0.05),
        "rwkv_gn_b": nrm(ks[18], (DEPTH, D_RWKV), 0.02),
        "hgrn_lb_logits": nrm(ks[19], (N_DIR, DEPTH, D_HGRN), 0.5),
        "hgrn_norm_g": 1.0 + nrm(ks[20], (DEPTH, D_HGRN), 0.05),
        "w_out": nrm(ks[21], (DEPTH, D_MIX, D_MODEL), BETA * D_MIX ** -0.5),
        "ln_g": 1.0 + nrm(ks[22], (DEPTH, D_MODEL), 0.05),
        "ln_b": nrm(ks[23], (DEPTH, D_MODEL), 0.02),
    }

def first_block(x, c, ctx, c_ctx, mod_w, mod_b, w_in, rwkv_shift, pool_w, pool_scale,
              rwkv_w0, rwkv_w_up, rwkv_a0, rwkv_a_up, rwkv_k_k, rwkv_k_a, rwkv_r_k,
              rwkv_gn_g, rwkv_gn_b, hgrn_lb_logits, hgrn_norm_g, w_out, ln_g, ln_b):
    out_dtype = x.dtype
    lb_w = jax.nn.softmax(hgrn_lb_logits.astype(jnp.float32), axis=1)
    lb_all = jnp.maximum(jnp.cumsum(lb_w, axis=1) - lb_w[:, :1], 0.0)
    h_x = x.astype(jnp.float32)
    h_ctx = ctx.astype(jnp.float32)
    for l in range(DEPTH):
        last = l == DEPTH - 1
        mod_lat = jax.nn.silu(c.astype(jnp.float32)) @ mod_w[l] + mod_b[l]
        mod_c = jax.nn.silu(c_ctx.astype(jnp.float32)) @ mod_w[l] + mod_b[l]
        sh_l, sc_l, gt_l = jnp.split(mod_lat, 3, axis=-1)
        sh_c, sc_c, gt_c = jnp.split(mod_c, 3, axis=-1)
        p_lat = (_layer_norm(h_x) * (1.0 + sc_l[:, None]) + sh_l[:, None]) @ w_in[l]
        p_ctx = (_layer_norm(h_ctx) * (1.0 + sc_c) + sh_c) @ w_in[l]
        pv_l, u_l, fh_l, g_l = _split_proj(p_lat)
        pv_c, u_c, fh_c, g_c = _split_proj(p_ctx)
        u_l = _shift3(u_l, rwkv_shift[l])
        u_c = _shift3(u_c, rwkv_shift[l])
        y_rc, y_rl = _rwkv_branch(u_c, u_l, rwkv_w0[l], rwkv_w_up[l], rwkv_a0[l], rwkv_a_up[l],
                                  rwkv_k_k[l], rwkv_k_a[l], rwkv_r_k[l], rwkv_gn_g[l], rwkv_gn_b[l],
                                  not last)
        o_hc, o_hl = _hgrn_branch(fh_c, fh_l, lb_all[:, l], hgrn_norm_g[l], not last)
        pool_l = _pool_branch(pv_l, True, pool_w[l], pool_scale[l])
        mix_l = jnp.concatenate([pool_l, y_rl, o_hl], axis=-1) * jax.nn.silu(g_l)
        new_x = _layer_norm(ALPHA * h_x + gt_l[:, None] * (mix_l @ w_out[l])) * ln_g[l] + ln_b[l]
        if not last:
            pool_c = _pool_branch(pv_c, False, pool_w[l], pool_scale[l])
            mix_c = jnp.concatenate([pool_c, y_rc, o_hc], axis=-1) * jax.nn.silu(g_c)
            h_ctx = _layer_norm(ALPHA * h_ctx + gt_c * (mix_c @ w_out[l])) * ln_g[l] + ln_b[l]
        h_x = new_x
    return h_x.astype(out_dtype)


DEPTH_2 = 2

N_EVEN = (DEPTH_2 + 1) // 2
N_ODD = DEPTH_2 // 2

A_GROUPS = 4
A_GROUP_DIM = 128
A_WIDTH = A_GROUPS * A_GROUP_DIM
A_CHUNK = 128
B_HEADS = 4
B_HEAD_DIM = 128
B_WIDTH = B_HEADS * B_HEAD_DIM
B_CONV = 3
GDN_CHUNK = 64
AB_SPLITS = (A_WIDTH, 2 * A_WIDTH, 2 * A_WIDTH + 3 * B_WIDTH, 2 * A_WIDTH + 4 * B_WIDTH,
             2 * A_WIDTH + 4 * B_WIDTH + 2 * B_HEADS)
AB_IN = 2 * A_WIDTH + 4 * B_WIDTH + 4 * B_HEADS
AB_MIX = A_WIDTH + B_WIDTH
C_HEADS = 8
C_NOPE = 128
C_ROPE = 64
C_VDIM = 128
C_Q_LORA = 384
C_KV_LORA = 256
C_IN = C_Q_LORA + C_KV_LORA + C_ROPE
Q_BLOCK = 128
ROPE_THETA = 10000.0
D_FF = 2816
FFN_CONV = 3
EPS = 1e-6


def rms_norm(x, g):
    xf = x.astype(jnp.float32)
    y = xf * lax.rsqrt(jnp.mean(xf * xf, axis=-1, keepdims=True) + EPS)
    return (y * g.astype(jnp.float32)).astype(x.dtype)

def layer_norm(x, g, b):
    xf = x.astype(jnp.float32)
    mu = jnp.mean(xf, axis=-1, keepdims=True)
    var = jnp.mean(jnp.square(xf - mu), axis=-1, keepdims=True)
    y = (xf - mu) * lax.rsqrt(var + EPS) * g.astype(jnp.float32) + b.astype(jnp.float32)
    return y.astype(x.dtype)

def modulate(h, shift, scale):
    return h * (1 + scale) + shift

def ada_mod(cond, w, b):
    m = (jax.nn.silu(cond) @ w + b)[..., None, :]
    return jnp.split(m, 6, axis=-1)

def dwconv(x, w):
    k = w.shape[0]
    return lax.conv_general_dilated(x, w[:, None, :], (1,), [(k // 2, k // 2)],
                                    dimension_numbers=('NWC', 'WIO', 'NWC'),
                                    feature_group_count=x.shape[-1])

def axial_rope(n, rot_dim):
    rows = n // GRID_W
    row = jnp.repeat(jnp.arange(rows, dtype=jnp.float32), GRID_W)
    col = jnp.tile(jnp.arange(GRID_W, dtype=jnp.float32), rows)
    n_freq = rot_dim // 4
    inv = ROPE_THETA ** (-jnp.arange(n_freq, dtype=jnp.float32) / n_freq)
    ang = jnp.concatenate([row[:, None] * inv, col[:, None] * inv], axis=-1)
    return jnp.cos(ang), jnp.sin(ang)

def apply_rope(x, cos, sin):
    h = x.shape[-1] // 2
    x1, x2 = x[..., :h], x[..., h:]
    cos = cos.astype(x.dtype)
    sin = sin.astype(x.dtype)
    return jnp.concatenate([x1 * cos - x2 * sin, x2 * cos + x1 * sin], axis=-1)

def chunk_gmlp(u, v, ln_g, ln_b, ws, bs):
    u = jax.nn.gelu(u, approximate=False)
    v = layer_norm(jax.nn.gelu(v, approximate=False), ln_g, ln_b)
    bn, l, _ = v.shape
    vc = v.reshape(bn, l // A_CHUNK, A_CHUNK, A_GROUPS, A_GROUP_DIM)
    s = jnp.einsum('gij,bnjgd->bnigd', ws, vc) + bs.T[None, None, :, :, None]
    return u * s.reshape(bn, l, A_WIDTH)

def gdn_chunked(q, k, v, g, beta, s0):
    bn, l, h, dk = q.shape
    cs = GDN_CHUNK
    n = l // cs
    to_c = lambda t: t.reshape(bn, n, cs, h, t.shape[-1]).transpose(1, 0, 3, 2, 4)
    qc, kc, vc = to_c(q), to_c(k), to_c(v)
    gc = g.reshape(bn, n, cs, h).transpose(1, 0, 3, 2)
    bc = beta.reshape(bn, n, cs, h).transpose(1, 0, 3, 2)
    gcum = jnp.cumsum(gc, axis=-1)
    tri_incl = jnp.tril(jnp.ones((cs, cs), bool))
    tri_strict = jnp.tril(jnp.ones((cs, cs), bool), -1)
    diff = gcum[..., :, None] - gcum[..., None, :]
    decay = jnp.exp(jnp.where(tri_incl, diff, -jnp.inf))
    kb = kc * bc[..., None]
    vb = vc * bc[..., None]
    a_mat = jnp.where(tri_strict, jnp.einsum('nbhid,nbhjd->nbhij', kb, kc) * decay, 0.0)
    eye = jnp.eye(cs, dtype=jnp.float32)
    t_mat = lax.linalg.triangular_solve(eye + a_mat, jnp.broadcast_to(eye, a_mat.shape),
                                        left_side=True, lower=True, unit_diagonal=True)
    u = jnp.einsum('nbhij,nbhjd->nbhid', t_mat, vb)
    w = jnp.einsum('nbhij,nbhjd->nbhid', t_mat, kb * jnp.exp(gcum)[..., None])
    attn = jnp.einsum('nbhid,nbhjd->nbhij', qc, kc) * decay
    qg = qc * jnp.exp(gcum)[..., None]
    kdec = kc * jnp.exp(gcum[..., -1:] - gcum)[..., None]
    gend = jnp.exp(gcum[..., -1])

    def step(s, xs):
        u_i, w_i, qg_i, kd_i, at_i, ge_i = xs
        v_new = u_i - jnp.einsum('bhck,bhkv->bhcv', w_i, s)
        o_i = jnp.einsum('bhck,bhkv->bhcv', qg_i, s) + jnp.einsum('bhij,bhjv->bhiv', at_i, v_new)
        s = s * ge_i[..., None, None] + jnp.einsum('bhck,bhcv->bhkv', kd_i, v_new)
        return s, o_i

    s_fin, o = lax.scan(step, s0, (u, w, qg, kdec, attn, gend))
    o = o.transpose(1, 0, 3, 2, 4).reshape(bn, l, h, v.shape[-1])
    return o, s_fin

def gated_deltanet(qkv, gate, alpha_raw, beta_raw, conv_w, a_log, dt_bias, norm_g, s0_pair):
    bn, l, _ = qkv.shape
    hq = jax.nn.silu(dwconv(qkv, conv_w)).astype(jnp.float32)
    q, k, v = jnp.split(hq, 3, axis=-1)
    l2 = lambda t: t * lax.rsqrt(jnp.sum(t * t, axis=-1, keepdims=True) + EPS)
    q = l2(q.reshape(bn, l, B_HEADS, B_HEAD_DIM)) * (B_HEAD_DIM ** -0.5)
    k = l2(k.reshape(bn, l, B_HEADS, B_HEAD_DIM))
    v = v.reshape(bn, l, B_HEADS, B_HEAD_DIM)
    a = alpha_raw.astype(jnp.float32).reshape(bn, l, 2, B_HEADS)
    beta = jax.nn.sigmoid(beta_raw.astype(jnp.float32).reshape(bn, l, 2, B_HEADS))
    log_alpha = -jnp.exp(a_log.astype(jnp.float32)) * jax.nn.softplus(a + dt_bias.astype(jnp.float32))
    o_f, s_f = gdn_chunked(q, k, v, log_alpha[:, :, 0], beta[:, :, 0], s0_pair[0])
    flip = lambda t: jnp.flip(t, axis=1)
    o_b, s_b = gdn_chunked(flip(q), flip(k), flip(v), flip(log_alpha[:, :, 1]), flip(beta[:, :, 1]), s0_pair[1])
    o = o_f + flip(o_b)
    o = rms_norm(o, norm_g) * jax.nn.silu(gate.astype(jnp.float32).reshape(bn, l, B_HEADS, B_HEAD_DIM))
    return o.reshape(bn, l, B_WIDTH).astype(qkv.dtype), (s_f, s_b)

def ab_mixer(h_ctx, h_lat, w_in, a_ln_g, a_ln_b, a_ws, a_bs, conv_w, a_log, dt_bias, norm_g, w_out,
             need_ctx_out):
    def run(h, state0, want_out):
        a_u, a_v, qkv, gate, alpha_raw, beta_raw = jnp.split(h @ w_in, AB_SPLITS, axis=-1)
        y_b, state = gated_deltanet(qkv, gate, alpha_raw, beta_raw, conv_w, a_log, dt_bias, norm_g, state0)
        if not want_out:
            return None, state
        y_a = chunk_gmlp(a_u, a_v, a_ln_g, a_ln_b, a_ws, a_bs)
        return jnp.concatenate([y_a, y_b], axis=-1) @ w_out, state

    zero = jnp.zeros((h_ctx.shape[0], B_HEADS, B_HEAD_DIM, B_HEAD_DIM), jnp.float32)
    y_ctx, ctx_state = run(h_ctx, (zero, zero), need_ctx_out)
    y_lat, _ = run(h_lat, ctx_state, True)
    return y_ctx, y_lat

def block_attention(qn, qr, kn, kr, v):
    bn, l, h, _ = qn.shape
    nb = l // Q_BLOCK
    scale = (C_NOPE + C_ROPE) ** -0.5
    blocks = lambda t: t.reshape(bn, nb, Q_BLOCK, h, t.shape[-1]).transpose(1, 0, 2, 3, 4)

    def one(blk):
        qn_b, qr_b = blk
        s = jnp.einsum('bqhd,bkhd->bhqk', qn_b, kn) + jnp.einsum('bqhd,bkd->bhqk', qr_b, kr)
        p = jax.nn.softmax(s.astype(jnp.float32) * scale, axis=-1).astype(v.dtype)
        return jnp.einsum('bhqk,bkhd->bqhd', p, v)

    o = lax.map(one, (blocks(qn), blocks(qr)))
    return o.transpose(1, 0, 2, 3, 4).reshape(bn, l, h * v.shape[-1])

def mla_mixer(h_ctx, h_lat, w_in, q_norm_g, kv_norm_g, w_uq, w_ukv, w_out, need_ctx_out):
    n_lat = h_lat.shape[1]
    cos, sin = axial_rope(n_lat, C_ROPE)
    rot_q = lambda t: apply_rope(t, cos[:, None, :], sin[:, None, :])
    rot_k = lambda t: apply_rope(t, cos, sin)
    no_rot = lambda t: t

    def queries(cq, rot):
        bn, l, _ = cq.shape
        q = (rms_norm(cq, q_norm_g) @ w_uq).reshape(bn, l, C_HEADS, C_NOPE + C_ROPE)
        return q[..., :C_NOPE], rot(q[..., C_NOPE:])

    def keys(kv_part, rot):
        bn, l, _ = kv_part.shape
        ckv, kr = jnp.split(kv_part, [C_KV_LORA], axis=-1)
        kv = (rms_norm(ckv, kv_norm_g) @ w_ukv).reshape(bn, l, C_HEADS, C_NOPE + C_VDIM)
        return kv[..., :C_NOPE], rot(kr), kv[..., C_NOPE:]

    z_lat = h_lat @ w_in
    kn_l, kr_l, v_l = keys(z_lat[..., C_Q_LORA:], rot_k)
    qn_l, qr_l = queries(z_lat[..., :C_Q_LORA], rot_q)
    if need_ctx_out:
        z_ctx = h_ctx @ w_in
        kv_ctx = z_ctx[..., C_Q_LORA:]
    else:
        kv_ctx = h_ctx @ w_in[:, C_Q_LORA:]
    kn_c, kr_c, v_c = keys(kv_ctx, no_rot)
    kn = jnp.concatenate([kn_c, kn_l], axis=1)
    kr = jnp.concatenate([kr_c, kr_l], axis=1)
    v = jnp.concatenate([v_c, v_l], axis=1)
    y_lat = block_attention(qn_l, qr_l, kn, kr, v) @ w_out
    y_ctx = None
    if need_ctx_out:
        qn_c, qr_c = queries(z_ctx[..., :C_Q_LORA], no_rot)
        y_ctx = block_attention(qn_c, qr_c, kn_c, kr_c, v_c) @ w_out
    return y_ctx, y_lat

def conv_ffn(h, w_up, conv_w, w_down):
    g, u = jnp.split(dwconv(h @ w_up, conv_w), 2, axis=-1)
    return (jax.nn.silu(g) * u) @ w_down

def second_inputs(seed: int = 0) -> dict:
    key = jax.random.key(seed)
    ks = iter(jax.random.split(key, 32))
    nrm = lambda shape, s: jax.random.normal(next(ks), shape, jnp.float32) * s
    gain = lambda shape: 1.0 + nrm(shape, 0.02)
    d = D_MODEL
    a_log = jnp.log(jax.random.uniform(next(ks), (N_EVEN, 2, B_HEADS), jnp.float32, 1.0, 16.0))
    dt = jnp.exp(jax.random.uniform(next(ks), (N_EVEN, 2, B_HEADS), jnp.float32,
                                    math.log(1e-3), math.log(1e-1)))
    dt_bias = dt + jnp.log(-jnp.expm1(-dt))
    return {
        'x': nrm((BATCH, SEQ, d), 1.0),
        'c': nrm((BATCH, d), 1.0),
        'ctx': nrm((BATCH, CTX_LEN, d), 1.0),
        'c_ctx': nrm((d,), 1.0),
        'ada_w': nrm((DEPTH_2, d, 6 * d), d ** -0.5),
        'ada_b': nrm((DEPTH_2, 6 * d), 0.01),
        'norm1_g': gain((DEPTH_2, d)),
        'norm2_g': gain((DEPTH_2, d)),
        'ab_w_in': nrm((N_EVEN, d, AB_IN), d ** -0.5),
        'a_ln_g': gain((N_EVEN, A_WIDTH)),
        'a_ln_b': nrm((N_EVEN, A_WIDTH), 0.01),
        'a_ws': nrm((N_EVEN, A_GROUPS, A_CHUNK, A_CHUNK), 0.5 * A_CHUNK ** -0.5),
        'a_bs': 1.0 + nrm((N_EVEN, A_GROUPS, A_CHUNK), 0.1),
        'b_conv_w': nrm((N_EVEN, B_CONV, 3 * B_WIDTH), B_CONV ** -0.5),
        'b_a_log': a_log,
        'b_dt_bias': dt_bias,
        'b_norm_g': gain((N_EVEN, B_HEAD_DIM)),
        'ab_w_out': nrm((N_EVEN, AB_MIX, d), AB_MIX ** -0.5),
        'mla_w_in': nrm((N_ODD, d, C_IN), d ** -0.5),
        'mla_q_norm_g': gain((N_ODD, C_Q_LORA)),
        'mla_kv_norm_g': gain((N_ODD, C_KV_LORA)),
        'mla_w_uq': nrm((N_ODD, C_Q_LORA, C_HEADS * (C_NOPE + C_ROPE)), C_Q_LORA ** -0.5),
        'mla_w_ukv': nrm((N_ODD, C_KV_LORA, C_HEADS * (C_NOPE + C_VDIM)), C_KV_LORA ** -0.5),
        'mla_w_out': nrm((N_ODD, C_HEADS * C_VDIM, d), (C_HEADS * C_VDIM) ** -0.5),
        'ffn_w_up': nrm((DEPTH_2, d, 2 * D_FF), d ** -0.5),
        'ffn_conv_w': nrm((DEPTH_2, FFN_CONV, 2 * D_FF), FFN_CONV ** -0.5),
        'ffn_w_down': nrm((DEPTH_2, D_FF, d), D_FF ** -0.5),
        'final_g': gain((d,)),
    }

def second_block(x, c, ctx, c_ctx, ada_w, ada_b, norm1_g, norm2_g, ab_w_in, a_ln_g, a_ln_b, a_ws, a_bs,
              b_conv_w, b_a_log, b_dt_bias, b_norm_g, ab_w_out, mla_w_in, mla_q_norm_g, mla_kv_norm_g,
              mla_w_uq, mla_w_ukv, mla_w_out, ffn_w_up, ffn_conv_w, ffn_w_down, final_g):
    lat, cx = x, ctx
    for i in range(DEPTH_2):
        last = i == DEPTH_2 - 1
        j = i // 2
        sh1, sc1, g1, sh2, sc2, g2 = ada_mod(c, ada_w[i], ada_b[i])
        csh1, csc1, cg1, csh2, csc2, cg2 = ada_mod(c_ctx, ada_w[i], ada_b[i])
        h_lat = modulate(rms_norm(lat, norm1_g[i]), sh1, sc1)
        h_ctx = modulate(rms_norm(cx, norm1_g[i]), csh1, csc1)
        if i % 2 == 0:
            y_ctx, y_lat = ab_mixer(h_ctx, h_lat, ab_w_in[j], a_ln_g[j], a_ln_b[j], a_ws[j], a_bs[j],
                                    b_conv_w[j], b_a_log[j], b_dt_bias[j], b_norm_g[j], ab_w_out[j],
                                    not last)
        else:
            y_ctx, y_lat = mla_mixer(h_ctx, h_lat, mla_w_in[j], mla_q_norm_g[j], mla_kv_norm_g[j],
                                     mla_w_uq[j], mla_w_ukv[j], mla_w_out[j], not last)
        lat = lat + g1 * y_lat
        lat = lat + g2 * conv_ffn(modulate(rms_norm(lat, norm2_g[i]), sh2, sc2),
                                  ffn_w_up[i], ffn_conv_w[i], ffn_w_down[i])
        if not last:
            cx = cx + cg1 * y_ctx
            cx = cx + cg2 * conv_ffn(modulate(rms_norm(cx, norm2_g[i]), csh2, csc2),
                                     ffn_w_up[i], ffn_conv_w[i], ffn_w_down[i])
    return rms_norm(lat, final_g)


def setup_inputs(seed=0):
    out = dict(first_inputs(seed))
    for name, value in second_inputs(seed + 1).items():
        if name != "x":
            out[name + "_2"] = value
    return out


def reference(
    x, c, ctx, c_ctx, mod_w, mod_b, w_in, rwkv_shift, pool_w, pool_scale, rwkv_w0, rwkv_w_up,
    rwkv_a0, rwkv_a_up, rwkv_k_k, rwkv_k_a, rwkv_r_k, rwkv_gn_g, rwkv_gn_b, hgrn_lb_logits,
    hgrn_norm_g, w_out, ln_g, ln_b, c_2, ctx_2, c_ctx_2, ada_w_2, ada_b_2, norm1_g_2, norm2_g_2,
    ab_w_in_2, a_ln_g_2, a_ln_b_2, a_ws_2, a_bs_2, b_conv_w_2, b_a_log_2, b_dt_bias_2,
    b_norm_g_2, ab_w_out_2, mla_w_in_2, mla_q_norm_g_2, mla_kv_norm_g_2, mla_w_uq_2,
    mla_w_ukv_2, mla_w_out_2, ffn_w_up_2, ffn_conv_w_2, ffn_w_down_2, final_g_2,
):
    x = first_block(
        x, c, ctx, c_ctx, mod_w, mod_b, w_in, rwkv_shift, pool_w, pool_scale, rwkv_w0,
        rwkv_w_up, rwkv_a0, rwkv_a_up, rwkv_k_k, rwkv_k_a, rwkv_r_k, rwkv_gn_g, rwkv_gn_b,
        hgrn_lb_logits, hgrn_norm_g, w_out, ln_g, ln_b,
    )
    return second_block(
        x, c_2, ctx_2, c_ctx_2, ada_w_2, ada_b_2, norm1_g_2, norm2_g_2, ab_w_in_2, a_ln_g_2,
        a_ln_b_2, a_ws_2, a_bs_2, b_conv_w_2, b_a_log_2, b_dt_bias_2, b_norm_g_2, ab_w_out_2,
        mla_w_in_2, mla_q_norm_g_2, mla_kv_norm_g_2, mla_w_uq_2, mla_w_ukv_2, mla_w_out_2,
        ffn_w_up_2, ffn_conv_w_2, ffn_w_down_2, final_g_2,
    )


_drawn_inputs = setup_inputs


def setup_inputs(seed=0):
    import zlib

    import numpy as np

    out = dict(_drawn_inputs(seed))
    spreads = {}
    factors = {'mod_b': 3.302,
     'pool_scale': 3.834,
     'rwkv_w_up': 3.036,
     'rwkv_a0': 8.0,
     'rwkv_gn_g': 6.697,
     'rwkv_gn_b': 8.0,
     'hgrn_norm_g': 6.357,
     'ada_b_2': 2.745,
     'norm1_g_2': 4.426,
     'norm2_g_2': 3.226,
     'a_ln_g_2': 8.0,
     'a_ln_b_2': 27.29,
     'b_norm_g_2': 8.0,
     'mla_q_norm_g_2': 8.0,
     'mla_kv_norm_g_2': 8.0,
     'final_g_2': 8.055}
    for name, (base, spread) in spreads.items():
        noise = np.random.default_rng([zlib.crc32(name.encode()), seed]).standard_normal(out[name].shape)
        drawn = base * np.exp(spread * noise) if base else spread * noise
        out[name] = jnp.asarray(drawn.astype(out[name].dtype))
    for name, factor in factors.items():
        out[name] = (out[name] * factor).astype(out[name].dtype)
    return out
```

```python
from contextlib import ExitStack

import numpy as np

import concourse.bass as bass
from concourse import mybir

F32 = mybir.dt.float32
F32R = mybir.dt.float32r
ALU = mybir.AluOpType
ACT = mybir.ActivationFunctionType
AX = mybir.AxisListType

P = 128
D = 1024
KD = D // P
CTX, LAT = 256, 512
T = CTX + LAT
SEGS = ((0, CTX), (CTX, LAT))
LAT_ONLY = ((CTX, LAT),)
TT = T // P
CT = CTX // P


class Stage:

    def __init__(self, nc, name):
        self.nc, self.name = nc, name
        self.mem, self.sems = ExitStack(), []

    def __enter__(self):
        return self

    def sem(self, name):
        s = self.nc.alloc_semaphore(f"{self.name}_{name}")
        self.sems.append(s)
        return s

    def sbuf(self, name, shape, dt=F32):
        return self.mem.enter_context(self.nc.sbuf_tensor(f"{self.name}_{name}", shape, dt))

    def banks(self, name, n):
        return [self.mem.enter_context(self.nc.psum_tensor(f"{self.name}_{name}{i}", [P, 512], F32))
                for i in range(n)]

    def block(self):
        return self.mem.enter_context(self.nc.Block())

    def __exit__(self, *exc):
        self.mem.close()
        if exc[0] is None:
            self.nc.clear_and_free_semaphores(self.sems)
            self.nc.all_engine_barrier()
        return False


def tile_loop(eng, n, body):
    turns = (n - 1) // 2
    if turns > 1:
        with eng.Fori(0, turns) as t:
            body(2 * t, 0, False)
            body(2 * t + 1, 1, False)
    else:
        for i in range(2 * turns):
            body(i, i % 2, False)
    for i in range(2 * turns, n):
        body(i, i % 2, i == n - 1)


def dense(nc, name, w_tiles, n_tiles, kt, xh, xl, spans, evac_act=None, evac_dve=None, first=0, evac=None):
    st = Stage(nc, name)
    ns = len(spans)
    if evac is not None:
        evac_act, evac_dve = evac(st)
    w_loaded = [st.sem(f"w_loaded{j}") for j in range(2)]
    w_high = st.sem("w_high")
    w_low = st.sem("w_low")
    tile_done = st.sem("tile_done")
    act_done = st.sem("act_done")
    banks_free = st.banks_free = st.sem("banks_free")
    with st:
        stage = st.sbuf("stage", [P, 2, kt * P])
        wh = st.sbuf("wh", [P, 2, kt * P], F32R)
        wl = st.sbuf("wl", [P, 2, kt * P], F32R)
        ps = st.banks("ps", 2 * ns)
        block = st.block()

        @block.sync
        def _(sp):
            def load(i, slot, last):
                sp.wait_ge(w_low, i + 1)
                sp.dma_start(stage[:, slot, :], w_tiles[bass.ds(first + i, 1)].rearrange("a p f -> p (a f)")
                             ).then_inc(w_loaded[slot], 16)
            tile_loop(sp, n_tiles, load)

        @block.gpsimd
        def _(pool):
            pool.sem_inc(w_low, 2)

            def low(i, slot, last):
                pool.wait_ge(w_high, i + 1)
                nc.gpsimd.tensor_tensor(wl[:, slot, :], stage[:, slot, :], wh[:, slot, :].bitcast(F32),
                                        ALU.subtract).then_inc(w_low, 1)
            tile_loop(pool, n_tiles, low)

        @block.scalar
        def _(act):
            def high(i, slot):
                act.wait_ge(w_loaded[slot], 8 * i + (16 if slot == 0 else 8))
                act.wait_ge(tile_done, i + 1)
                nc.scalar.activation(wh[:, slot, :], stage[:, slot, :], ACT.Copy).then_inc(w_high, 1)

            high(0, 0)

            def step(i, slot, last):
                if not last:
                    high(i + 1, 1 - slot)
                if evac_act is not None:
                    act.wait_ge(tile_done, i + 3)
                    ins = evac_act(act, i, ps[slot * ns:slot * ns + ns], slot)
                    ins.then_inc(act_done if evac_dve is not None else banks_free, 1)
            if evac_act is not None and evac_dve is None:
                act.sem_inc(banks_free, 2)
            tile_loop(act, n_tiles, step)

        @block.vector
        def _(dve):
            if evac_dve is None:
                return
            dve.sem_inc(banks_free, 2)

            def step(i, slot, last):
                if evac_act is None:
                    dve.wait_ge(tile_done, i + 3)
                else:
                    dve.wait_ge(act_done, i + 1)
                evac_dve(dve, i, ps[slot * ns:slot * ns + ns], slot).then_inc(banks_free, 1)
            tile_loop(dve, n_tiles, step)

        @block.tensor
        def _(pe):
            pe.sem_inc(tile_done, 2)

            def products(i, slot, last):
                pe.wait_ge(w_low, i + 3)
                pe.wait_ge(banks_free, i + 1)
                for s, (t0, n) in enumerate(spans):
                    out = ps[slot * ns + s][:, :n]
                    for k in range(kt):
                        w_hi = wh[:, slot, k * P:(k + 1) * P]
                        w_lo = wl[:, slot, k * P:(k + 1) * P]
                        nc.tensor.matmul(out, w_hi, xh[:, k, t0:t0 + n], start=k == 0, stop=False)
                        nc.tensor.matmul(out, w_hi, xl[:, k, t0:t0 + n], start=False, stop=False)
                        done = nc.tensor.matmul(out, w_lo, xh[:, k, t0:t0 + n], start=False, stop=k == kt - 1)
                done.then_inc(tile_done, 1)
            tile_loop(pe, n_tiles, products)




def three_taps(nc, t, name, per_tap, dst, spans, shift=0):
    def make(st):
        before_ok = st.sem("tap_before")

        def tap(k, i):
            return t["cols"][:, bass.ds(COL[name][0] + k * per_tap + shift + i, 1)]

        def evac_act(act, i, ps, slot):
            for (t0, n), b in zip(spans, ps):
                ins = nc.scalar.activation(dst(i, t0, n), b[:, :n], ACT.Copy, scale=tap(1, i))
            return ins

        def evac_dve(dve, i, ps, slot):
            for (t0, n), b in zip(spans, ps):
                out = dst(i, t0 + 1, n - 1)
                nc.vector.scalar_tensor_tensor(out, b[:, :n - 1], tap(0, i), out, ALU.mult, ALU.add
                                               ).then_inc(before_ok, 1)
            dve.wait_ge(before_ok, len(spans) * i + len(spans))
            for (t0, n), b in zip(spans, ps):
                out = dst(i, t0, n - 1)
                ins = nc.vector.scalar_tensor_tensor(out, b[:, 1:n], tap(2, i), out, ALU.mult, ALU.add)
            return ins
        return evac_act, evac_dve
    return make


class Chain:

    def __init__(self, eng, sem):
        self.eng, self.sem, self.n = eng, sem, 0

    def __call__(self, ins):
        self.n += 1
        ins.then_inc(self.sem, 1)
        self.eng.wait_ge(self.sem, self.n)


def spread(ap, at, n):
    shape = list(ap.shape)
    shape.insert(at, n)
    return ap.unsqueeze(at).to_broadcast(shape)


def normed(nc, name, x, kt, spans, ones, eps, center, scale, shift, xh, xl, out=None):
    st = Stage(nc, name)
    ns = len(spans)
    centered = st.sem("centered")
    squared = st.sem("squared")
    mean = st.sem("mean")
    var = st.sem("var")
    var_eps = st.sem("var_eps")
    root = st.sem("root")
    rstd_ok = st.sem("rstd")
    xn_ok = st.sem("xn")
    high = st.sem("high")
    full = st.sem("full")
    low = st.sem("low")
    with st:
        tmax = max(n for _, n in spans)
        xc = st.sbuf("xc", [P, kt, T])
        sq = st.sbuf("sq", [P, kt, tmax])
        rs = st.sbuf("rs", [P, ns, tmax])
        rstd = st.sbuf("rstdt", [P, ns, tmax])
        mps = st.banks("mean", ns)
        vps = st.banks("var", ns)
        block = st.block()

        @block.tensor
        def _(pe):
            if center:
                for s, (t0, n) in enumerate(spans):
                    for k in range(kt):
                        done = nc.tensor.matmul(mps[s][:, :n], ones[:, :], x[:, k, t0:t0 + n],
                                                start=k == 0, stop=k == kt - 1)
                    done.then_inc(mean, 1)
            for s, (t0, n) in enumerate(spans):
                pe.wait_ge(squared, s + 1)
                for k in range(kt):
                    done = nc.tensor.matmul(vps[s][:, :n], ones[:, :], sq[:, k, :n],
                                            start=k == 0, stop=k == kt - 1)
                done.then_inc(var, 1)

        @block.scalar
        def _(act):
            for s, (t0, n) in enumerate(spans):
                if center:
                    act.wait_ge(centered, s + 1)
                if s:
                    act.wait_ge(var, s)
                src = xc if center else x
                nc.scalar.activation(sq[:, :, :n], src[:, :, t0:t0 + n], ACT.Square).then_inc(squared, 1)
            for s, (t0, n) in enumerate(spans):
                act.wait_ge(var_eps, s + 1)
                nc.scalar.activation(rs[:, s, :n], rs[:, s, :n], ACT.Sqrt).then_inc(root, 1)
            if out is None:
                for s, (t0, n) in enumerate(spans):
                    act.wait_ge(xn_ok, s + 1)
                    for k in range(kt):
                        nc.scalar.activation(xh[:, k, t0:t0 + n], xc[:, k, t0:t0 + n], ACT.Identity,
                                             scale=scale[s](k), bias=shift[s](k) if shift else 0.0
                                             ).then_inc(high, 1)

        @block.vector
        def _(dve):
            if center:
                for s, (t0, n) in enumerate(spans):
                    dve.wait_ge(mean, s + 1)
                    nc.vector.tensor_tensor(xc[:, :, t0:t0 + n], x[:, :, t0:t0 + n],
                                            spread(mps[s][:, :n], 1, kt), ALU.subtract).then_inc(centered, 1)
            for s, (t0, n) in enumerate(spans):
                dve.wait_ge(var, s + 1)
                nc.vector.tensor_scalar(rs[:, s, :n], vps[s][:, :n], eps, None, ALU.add).then_inc(var_eps, 1)
            for s, (t0, n) in enumerate(spans):
                dve.wait_ge(root, s + 1)
                nc.vector.reciprocal(rstd[:, s, :n], rs[:, s, :n]).then_inc(rstd_ok, 1)
                dve.wait_ge(rstd_ok, s + 1)
                src = xc if center else x
                nc.vector.tensor_tensor(xc[:, :, t0:t0 + n], src[:, :, t0:t0 + n],
                                        spread(rstd[:, s, :n], 1, kt), ALU.mult).then_inc(xn_ok, 1)
            for s, (t0, n) in enumerate(spans):
                dve.wait_ge(xn_ok, s + 1)
                for k in range(kt):
                    dst = xc if out is None else out
                    if out is None:
                        dve.wait_ge(high, s * kt + k + 1)
                    if shift:
                        ins = nc.vector.tensor_scalar(dst[:, k, t0:t0 + n], xc[:, k, t0:t0 + n],
                                                      scale[s](k), shift[s](k), ALU.mult, ALU.add)
                    else:
                        ins = nc.vector.tensor_scalar(dst[:, k, t0:t0 + n], xc[:, k, t0:t0 + n],
                                                      scale[s](k), None, ALU.mult)
                    ins.then_inc(full, 1)

        @block.gpsimd
        def _(pool):
            if out is None:
                for s, (t0, n) in enumerate(spans):
                    for k in range(kt):
                        pool.wait_ge(full, s * kt + k + 1)
                        nc.gpsimd.tensor_tensor(xl[:, k, t0:t0 + n], xc[:, k, t0:t0 + n],
                                                xh[:, k, t0:t0 + n].bitcast(F32), ALU.subtract).then_inc(low, 1)


def gemv_mods(nc, name, w_tiles, n_tiles, kt, vec, bias, mods, group=4):
    st = Stage(nc, name)
    loaded = [st.sem(f"loaded{j}") for j in range(2)]
    used = st.sem("used")
    added = st.sem("added")
    turns = n_tiles // group
    assert turns * group == n_tiles and turns % 2 == 0
    with st:
        w = st.sbuf("w", [P, 2, group, kt * P])
        ps = st.banks("ps", 2)
        block = st.block()

        @block.sync
        def _(sp):
            def load(i, slot, last):
                sp.wait_ge(used, i + 1)
                sp.dma_start(w[:, slot], w_tiles[bass.ds(group * i, group)].rearrange("a p f -> p a f")
                             ).then_inc(loaded[slot], 16)
            tile_loop(sp, turns, load)

        @block.tensor
        def _(pe):
            pe.sem_inc(used, 2)

            def products(i, slot, last):
                pe.wait_ge(loaded[slot], 8 * i + (16 if slot == 0 else 8))
                pe.wait_ge(added, i + 1)
                for g in range(group):
                    for k in range(kt):
                        done = nc.tensor.matmul(ps[slot][:, 2 * g:2 * g + 2], w[:, slot, g, k * P:(k + 1) * P],
                                                vec[:, k, :], start=k == 0, stop=k == kt - 1)
                done.then_inc(used, 1)
            tile_loop(pe, turns, products)

        @block.vector
        def _(dve):
            dve.sem_inc(added, 2)

            def add(i, slot, last):
                dve.wait_ge(used, i + 3)
                nc.vector.tensor_tensor(
                    mods[:, bass.ds(group * i, group), :],
                    ps[slot][:, :2 * group].rearrange("p (g j) -> p g j", j=2),
                    spread(bias[:, bass.ds(group * i, group)], 2, 2), ALU.add).then_inc(added, 1)
            tile_loop(dve, turns, add)



def tiles_of(w, n):
    k = w.shape[0]
    return np.ascontiguousarray(
        w[:, :n].reshape(k // P, P, n // P, P).transpose(2, 1, 0, 3).reshape(n // P, P, k))


def columns(v):
    v = np.asarray(v, np.float32).reshape(-1, P)
    return v.T


D_POOL, D_RWKV, D_HGRN = 256, 384, 384
NR = D_RWKV // P
N_RWKV_IN = 11
HD = 64
C = 64
NC = T // C
CC = CTX // C
O_POOL, O_RWKV, O_HGRN, O_GATE = 0, 2, 13, 25


def masks():
    j, t = np.arange(P)[:, None], np.arange(P)[None, :]
    same = j // C == t // C
    m = {"ident": (j == t), "heads": j // HD == t // HD,
         "strict0": same & (j < t), "strict1": same & (j > t),
         "incl0": same & (j <= t), "incl1": same & (j >= t)}
    for lv in range(6):
        s = 1 << lv
        half = (j // (2 * s) == t // (2 * s)) & (j // s != t // s)
        m[f"level{lv}_0"] = half & (j < t)
        m[f"level{lv}_1"] = half & (j > t)
    return m


MASKS = {name: i for i, name in enumerate(masks())}

PACKED = (
    ("c", KD), ("c_ctx", KD), ("c_2", KD), ("c_ctx_2", KD), ("mod_b", 24), ("ada_b_2", 96),
    ("rwkv_shift", 33), ("rwkv_w0", 6), ("rwkv_a0", 6), ("rwkv_k_k", 3), ("rwkv_k_a", 3), ("rwkv_r_k", 6),
    ("rwkv_gn_g", 3), ("rwkv_gn_b", 3), ("hgrn_lb_logits", 6), ("hgrn_norm_g", 3), ("pool_scale", 2),
    ("ln_g", KD), ("ln_b", KD), ("norm1_g_2", 16), ("norm2_g_2", 16), ("a_ln_g_2", 4), ("a_ln_b_2", 4),
    ("b_conv_w_2", 36), ("b_norm_g_2", 1), ("mla_q_norm_g_2", 3), ("mla_kv_norm_g_2", 2),
    ("ffn_conv_w_2", 264), ("final_g_2", KD),
)
COL = {}
for _name, _n in PACKED:
    COL[_name] = (sum(n for _, n in PACKED[:len(COL)]), _n)
N_COLS = sum(n for _, n in PACKED)

LOADS = {}


def lay_out(inputs):
    g = {k: np.asarray(v) for k, v in inputs.items()}
    g["ffn_conv_w_2"] = pairs_of(g["ffn_conv_w_2"])
    arrays = {
        "x": np.ascontiguousarray(g["x"][0].T.reshape(KD, P, LAT).transpose(1, 0, 2)),
        "ctx": np.ascontiguousarray(g["ctx"][0].T.reshape(KD, P, CTX).transpose(1, 0, 2)),
        "ctx_2": np.ascontiguousarray(g["ctx_2"][0].T.reshape(KD, P, CTX).transpose(1, 0, 2)),
        "columns": np.ascontiguousarray(np.concatenate([columns(g[name]) for name, _ in PACKED], 1)),
        "masks": np.ascontiguousarray(np.stack([m.astype(np.float32) for m in masks().values()], 1)),
        "mod_w": tiles_of(g["mod_w"][0], 3 * D),
        "w_up": g["rwkv_w_up"].reshape(P, D_RWKV), "a_up": g["rwkv_a_up"].reshape(P, D_RWKV),
        "pool_w": np.ascontiguousarray(g["pool_w"].reshape(2, P, 64).transpose(1, 0, 2)),
        "pool_counts": pool_counts(),
        "w_out": tiles_of(g["w_out"][0], D),
        "w_in": tiles_of(g["w_in"][0], 4224),
    }
    arrays.update(lay_out_second(g))
    assert arrays["columns"].shape == (P, N_COLS)
    return arrays


def pairs_of(w):
    v = w.reshape(w.shape[:-1] + (2, -1, P))
    return np.ascontiguousarray(np.moveaxis(v, -3, -2)).reshape(w.shape)


def lay_out_second(g):
    w = g["ab_w_in_2"][0]
    raw = w[:, 3072:3088].reshape(D, 2, 2, 4)
    ab = np.zeros((D, 4, 32), np.float32)
    ab[:, :, :4] = raw.reshape(D, 4, 4)
    rows = np.zeros((P, 2), np.float32)
    for d in range(2):
        rows[32 * d:32 * d + 4, 0] = g["b_a_log_2"][0, d]
        rows[32 * d:32 * d + 4, 1] = g["b_dt_bias_2"][0, d]
    w_mla, w_uq, w_ukv = g["mla_w_in_2"][0], g["mla_w_uq_2"][0].reshape(384, 8, 192), \
        g["mla_w_ukv_2"][0].reshape(256, 8, 256)
    table, swap = rope_tables()
    down = g["ffn_w_down_2"]
    return {
        "ada_w": np.concatenate([tiles_of(g["ada_w_2"][i], 6 * D) for i in range(2)]),
        "ab_w": tiles_of(np.concatenate([w[:, :3072], ab.reshape(D, P)], 1), 25 * P),
        "gdn_rows": rows,
        "a_ws": np.ascontiguousarray(g["a_ws_2"][0].transpose(2, 0, 1)),
        "a_bs": g["a_bs_2"][0],
        "ab_w_out": tiles_of(g["ab_w_out_2"][0], D),
        "mla_w": tiles_of(np.concatenate([w_mla, w_mla[:, 640:]], 1), 6 * P),
        "mla_uq": tiles_of(np.concatenate([w_uq[..., :128].reshape(384, -1), w_uq[..., 128:].reshape(384, -1)], 1), 12 * P),
        "mla_ukv": tiles_of(np.concatenate([w_ukv[..., :128].reshape(256, -1), w_ukv[..., 128:].reshape(256, -1)], 1), 16 * P),
        "mla_w_out": tiles_of(g["mla_w_out_2"][0], D),
        "rope_table": table, "rope_swap": swap,
        "ffn_up": np.concatenate([tiles_of(pairs_of(g["ffn_w_up_2"][i]), 44 * P) for i in range(2)]),
        "ffn_down": np.concatenate([tiles_of(down[i, h * 1408:(h + 1) * 1408], D) for i in range(2) for h in range(2)]),
    }


def setup(nc, d, mem):
    t = {}

    def keep(name, shape, dt=F32):
        t[name] = mem.enter_context(nc.sbuf_tensor(name, shape, dt))
        return t[name]

    cols = keep("cols", [P, N_COLS])
    mask = keep("mask", [P, len(MASKS), P])
    cond = keep("cond", [P, 2, KD, 2])
    over_d = keep("over_d", [P, P])
    turn = keep("turn", [P, T])
    with Stage(nc, "setup") as st:
        loaded = st.sem("loaded")
        ready = st.sem("ready")
        block = st.block()

        @block.sync
        def _(sp):
            sp.dma_start(cols[:, :], d["columns"]).then_inc(loaded, 16)
            sp.dma_start(mask[:, :, :], d["masks"]).then_inc(loaded, 16)
            sp.wait_ge(loaded, 32)

        @block.scalar
        def _(act):
            act.wait_ge(loaded, 32)
            for i, (lat, con) in enumerate((("c", "c_ctx"), ("c_2", "c_ctx_2"))):
                for j, name in enumerate((lat, con)):
                    o = COL[name][0]
                    nc.scalar.activation(cond[:, i, :, j], cols[:, o:o + KD], ACT.Silu)

        @block.vector
        def _(dve):
            nc.vector.memset(over_d[:, :], 1.0 / D).then_inc(ready, 1)
            nc.vector.memset(turn[:, :], 1.0).then_inc(ready, 1)
            dve.wait_ge(ready, 2)
            nc.vector.memset(turn[:, :].rearrange("p (c t) -> p c t", t=C)[:, :, 0:1], 0.0)
    return t


def col(t, name, i):
    o, n = COL[name]
    assert i < n
    return t["cols"][:, o + i:o + i + 1]


def cols_of(t, name):
    o, n = COL[name]
    return t["cols"][:, o:o + n]


def modulation(nc, t, name, tile0, scale_tiles, gains=()):
    mods = t[name]
    with Stage(nc, f"{name}_scale{tile0}") as st:
        chain_sem = st.sem("own")
        block = st.block()

        @block.vector
        def _(dve):
            own = Chain(dve, chain_sem)
            for n, s0 in enumerate(scale_tiles):
                part = mods[:, s0:s0 + KD, :]
                own(nc.vector.tensor_scalar(part, part, 1.0, None, ALU.add))
                if gains:
                    own(nc.vector.tensor_tensor(part, part, spread(gains[n], 2, 2), ALU.mult))


def load(nc, name, pairs):
    with Stage(nc, name) as st:
        loaded = st.sem("loaded")
        block = st.block()

        @block.sync
        def _(sp):
            for out, src in pairs:
                sp.dma_start(out, src).then_inc(loaded, 16)
            sp.wait_ge(loaded, 16 * len(pairs))





def chunk_order(d):
    return [*range(CC), *range(CC, NC)] if d == 0 else [*range(CC - 1, -1, -1), *range(NC - 1, CC - 1, -1)]


def to_tokens(nc, name, jobs, ident):
    with Stage(nc, name) as st:
        turned = st.sem("turned")
        read = [st.sem("read_act"), st.sem("read_dve")]
        ps = st.banks("ps", 4)
        block = st.block()

        @block.tensor
        def _(pe):
            for j, (sources, _) in enumerate(jobs):
                if j >= 4:
                    pe.wait_ge(read[j % 2], (j - 4) // 2 + 1)
                for f, src in enumerate(sources):
                    done = nc.tensor.transpose(ps[j % 4][:, f * P:(f + 1) * P], src, ident)
                done.then_inc(turned, 1)

        def read_out(eng, j, copy):
            sources, out = jobs[j]
            eng.wait_ge(turned, j + 1)
            copy(out, ps[j % 4][:, :len(sources) * P]).then_inc(read[j % 2], 1)

        @block.scalar
        def _(act):
            for j in range(0, len(jobs), 2):
                read_out(act, j, lambda o, i: nc.scalar.activation(o, i, ACT.Copy))

        @block.vector
        def _(dve):
            for j in range(1, len(jobs), 2):
                read_out(dve, j, lambda o, i: nc.vector.tensor_copy(o, i))



def seg(ap, s):
    t0, n = SEGS[s]
    return ap[:, :, t0:t0 + n]


def later_half(ap, d, s):
    v = ap.rearrange("p f (b h s) -> p (f b) h s", h=2, s=s)
    return v[:, :, 1 - d, :], v[:, :, d, :]


def hgrn_prepare(nc, t, d, p, w):
    with Stage(nc, f"hgrn{d}_prep") as st:
        z = p[:, 6 + 3 * d:9 + 3 * d, :]
        absz = st.sbuf("absz", [P, NR, T])
        soft = st.sbuf("soft", [P, NR, T])
        logf = st.sbuf("logf", [P, NR, T])
        g = [st.sbuf("g0", [P, NR, CTX]), w["g"]]
        e_qg = st.sbuf("e_qg", [P, NR, LAT])
        soft_ok = st.sem("softplus")
        logf_ok = st.sem("logf")
        lk_ok = st.sem("log_k")
        k_ok = st.sem("k")
        q_ok = st.sem("q")
        g_ok = st.sem("g")
        rest_ok = st.sem("rest")
        exp_ok = st.sem("exp")
        own = st.sem("own")
        block = st.block()

        @block.scalar
        def _(act):
            chain = Chain(act, own)
            chain(nc.scalar.activation(absz[:, :, :], z, ACT.Abs))
            chain(nc.scalar.activation(absz[:, :, :], absz[:, :, :], ACT.Exp, scale=-1.0))
            nc.scalar.activation(soft[:, :, :], absz[:, :, :], ACT.Ln, bias=1.0).then_inc(soft_ok, 1)
            if d == 0:
                nc.scalar.activation(w["q"][:, :, :], seg(p[:, 0:NR, :], 1), ACT.Copy).then_inc(q_ok, 1)
            for s in range(2):
                act.wait_ge(lk_ok, s + 1)
                nc.scalar.activation(w["k"][s][:, :, :], seg(absz, s), ACT.Exp).then_inc(k_ok, 1)
            for s in range(2):
                act.wait_ge(rest_ok, s + 1)
                nc.scalar.activation(seg(soft, s), seg(soft, s), ACT.Exp).then_inc(exp_ok, 1)
                ends = g[s][:, :, :].rearrange("p f (c t) -> p f c t", t=C)[:, :, :, (0 if d else C - 1)]
                c0, cn = SEGS[s][0] // C, SEGS[s][1] // C
                nc.scalar.activation(w["end"][:, :, c0:c0 + cn], ends, ACT.Exp)
            nc.scalar.activation(e_qg[:, :, :], g[1][:, :, :], ACT.Exp).then_inc(exp_ok, 1)

        @block.vector
        def _(dve):
            dve.wait_ge(soft_ok, 1)
            nc.vector.scalar_tensor_tensor(logf[:, :, :], z, 0.0, soft[:, :, :], ALU.min, ALU.subtract
                                           ).then_inc(logf_ok, 1)
            dve.wait_ge(logf_ok, 1)
            for s in range(2):
                nc.vector.tensor_tensor(seg(absz, s), seg(logf, s), seg(z, s), ALU.subtract).then_inc(lk_ok, 1)
            for s, (t0, n) in enumerate(SEGS):
                for f in range(NR):
                    src, dst = logf[:, f, t0:t0 + n], g[s][:, f, :]
                    if d:
                        src, dst = src[:, ::-1], dst[:, ::-1]
                    nc.vector.tensor_tensor_scan(dst, t["turn"][:, :n], src, 0.0, ALU.mult, ALU.add
                                                 ).then_inc(g_ok, 1)
            for s, (t0, n) in enumerate(SEGS):
                dve.wait_ge(g_ok, NR * (s + 1))
                for f in range(NR):
                    gv = g[s][:, f, :].rearrange("p (c t) -> p c t", t=C)
                    end = gv[:, :, (0 if d else C - 1)]
                    ins = nc.vector.tensor_tensor(soft[:, f, t0:t0 + n].rearrange("p (c t) -> p c t", t=C),
                                                  spread(end, 2, C), gv, ALU.subtract)
                ins.then_inc(rest_ok, 1)
            dve.wait_ge(k_ok, 2)
            for s in range(2):
                dve.wait_ge(exp_ok, s + 1)
                nc.vector.tensor_tensor(w["kh"][s][:, :, :], w["k"][s][:, :, :], seg(soft, s), ALU.mult)
            if d == 0:
                dve.wait_ge(q_ok, 1)
            dve.wait_ge(exp_ok, 3)
            nc.vector.tensor_tensor(w["qg"][:, :, :], w["q"][:, :, :], e_qg[:, :, :], ALU.mult)


def half(h):
    return slice(HD * (h % 2), HD * (h % 2) + HD)


def score_groups():
    return [[(i, 2 * f + parity) for f, i in pairs]
            for pairs in ([(f, i) for i in range(LAT // P)] for f in range(NR)) for parity in range(2)]


SCORE_AT = {tile: 4 * b + a for b, group in enumerate(score_groups()) for a, tile in enumerate(group)}


def hgrn_scores(nc, t, d, w):
    groups = score_groups()
    ng = len(groups)
    levels = list(range(6)) + ["diagonal"]
    scores, g = w["scores"], w["g"]
    with Stage(nc, f"hgrn{d}_scores") as st:
        diff = st.sbuf("diff", [P, 2, NR, LAT])
        e_lv = st.sbuf("e_lv", [P, 2, NR, LAT])
        ops = st.sbuf("ops", [P, 2, NR, LAT])
        diff_ok = st.sem("diff")
        elv_ok = st.sem("level_exp")
        hq_ok = st.sem("level_q")
        hk_ok = st.sem("level_k")
        cleared = st.sem("cleared")
        product = st.sem("product")
        picked = st.sem("picked")
        ps = st.banks("ps", 6)
        block = st.block()

        @block.scalar
        def _(act):
            for lv in range(6):
                act.wait_ge(diff_ok, lv + 1)
                if lv >= 2:
                    act.wait_ge(hq_ok, lv - 1)
                    act.wait_ge(hk_ok, lv - 1)
                later, earlier = later_half(e_lv[:, lv % 2], d, 1 << lv)
                dl, de = later_half(diff[:, lv % 2], d, 1 << lv)
                nc.scalar.activation(later, dl, ACT.Exp).then_inc(elv_ok, 1)
                nc.scalar.activation(earlier, de, ACT.Exp, scale=-1.0).then_inc(elv_ok, 1)

        @block.gpsimd
        def _(pool):
            nc.gpsimd.memset(scores[:, :, :], 0.0).then_inc(cleared, 1)
            for lv in range(6):
                pool.wait_ge(elv_ok, 2 * lv + 2)
                if lv >= 2:
                    pool.wait_ge(product, ng * (lv - 1))
                _, earlier = later_half(ops[:, lv % 2], d, 1 << lv)
                _, k = later_half(w["k"][1][:, :, :], d, 1 << lv)
                _, e = later_half(e_lv[:, lv % 2], d, 1 << lv)
                nc.gpsimd.tensor_tensor(earlier, k, e, ALU.mult).then_inc(hk_ok, 1)

        @block.vector
        def _(dve):
            def difference(lv):
                s = 1 << lv
                v = g[:, :, :].rearrange("p f (b h s) -> p (f b) h s", h=2, s=s)
                border = v[:, :, d, (0 if d else s - 1)]
                if lv >= 2:
                    dve.wait_ge(elv_ok, 2 * lv - 2)
                nc.vector.tensor_tensor(
                    diff[:, lv % 2].rearrange("p f (b e) -> p (f b) e", e=2 * s),
                    g[:, :, :].rearrange("p f (b e) -> p (f b) e", e=2 * s),
                    spread(border, 2, 2 * s), ALU.subtract).then_inc(diff_ok, 1)

            def queries(lv):
                dve.wait_ge(elv_ok, 2 * lv + 1)
                if lv >= 2:
                    dve.wait_ge(product, ng * (lv - 1))
                later, _ = later_half(ops[:, lv % 2], d, 1 << lv)
                q, _ = later_half(w["q"][:, :, :], d, 1 << lv)
                e, _ = later_half(e_lv[:, lv % 2], d, 1 << lv)
                nc.vector.tensor_tensor(later, q, e, ALU.mult).then_inc(hq_ok, 1)

            difference(0)
            difference(1)
            queries(0)
            dve.wait_ge(cleared, 1)
            for n, lv in enumerate(levels):
                if n + 1 < 6:
                    queries(n + 1)
                if n + 2 < 6:
                    difference(n + 2)
                m = MASKS["ident" if lv == "diagonal" else f"level{lv}_{d}"]
                for b in range(ng):
                    dve.wait_ge(product, ng * n + b + 1)
                    nc.vector.copy_predicated(
                        scores[:, 4 * b:4 * b + 4, :], spread(t["mask"][:, m, :], 1, 4).bitcast(mybir.dt.int32),
                        ps[b][:, :].rearrange("p (a t) -> p a t", t=P)).then_inc(picked, 1)

        @block.tensor
        def _(pe):
            for n, lv in enumerate(levels):
                if lv != "diagonal":
                    pe.wait_ge(hq_ok, lv + 1)
                    pe.wait_ge(hk_ok, lv + 1)
                left = w["k"][1] if lv == "diagonal" else ops[:, lv % 2]
                right = w["q"] if lv == "diagonal" else ops[:, lv % 2]
                for b in range(0, ng, 2):
                    if n:
                        pe.wait_ge(picked, ng * (n - 1) + b + 2)
                    for a in range(4):
                        for e in range(2):
                            i, h = groups[b + e][a]
                            tok = slice(i * P, (i + 1) * P)
                            done = nc.tensor.matmul(ps[b + e][:, a * P:(a + 1) * P], left[half(h), h // 2, tok],
                                                    right[half(h), h // 2, tok], start=True, stop=True)
                            if a == 3:
                                done.then_inc(product, 1)


def hgrn_states(nc, d, w, vt):
    with Stage(nc, f"hgrn{d}_states") as st:
        update = st.sem("update")
        added = st.sem("added")
        decayed = st.sem("decayed")
        tmp = st.sbuf("tmp", [P, NR, HD])
        ps = st.banks("ps", 4)
        block = st.block()
        order = chunk_order(d)
        states = w["states"]

        @block.tensor
        def _(pe):
            for n, c in enumerate(order[:-1]):
                if n >= 4:
                    pe.wait_ge(added, n - 3)
                tok = slice(C * (c % 2), C * (c % 2) + C)
                for h in range(6):
                    f = slice(HD * h, HD * h + HD)
                    done = nc.tensor.matmul(ps[n % 4][half(h), HD * (h // 2):HD * (h // 2) + HD],
                                            w["kht"][tok, c // 2, f], vt[tok, c // 2, f], start=True, stop=True)
                done.then_inc(update, 1)

        @block.vector
        def _(dve):
            nc.vector.memset(states[:, order[0]], 0.0).then_inc(decayed, 1)
            for n, c in enumerate(order[:-1]):
                dve.wait_ge(decayed, n + 1)
                if n:
                    dve.wait_ge(added, n)
                nc.vector.tensor_tensor(tmp[:, :, :], states[:, c], spread(w["end"][:, :, c], 2, HD), ALU.mult
                                        ).then_inc(decayed, 1)
                dve.wait_ge(decayed, n + 2)
                dve.wait_ge(update, n + 1)
                nc.vector.tensor_tensor(states[:, order[n + 1]], tmp[:, :, :],
                                        ps[n % 4][:, :NR * HD].rearrange("p (f v) -> p f v", v=HD), ALU.add
                                        ).then_inc(added, 1)


def hgrn_outputs(nc, d, w, vt, o):
    with Stage(nc, f"hgrn{d}_out") as st:
        summed = st.sem("summed")
        ps = st.banks("ps", NR)
        block = st.block()

        @block.tensor
        def _(pe):
            for f in range(NR):
                for i in range(LAT // P):
                    for h in (2 * f, 2 * f + 1):
                        hd = slice(HD * h, HD * h + HD)
                        nc.tensor.matmul(ps[f][half(h), i * P:(i + 1) * P], vt[:, CT + i, hd],
                                         w["scores"][:, SCORE_AT[i, h], :], start=True, stop=False)
                        for c in (2 * i, 2 * i + 1):
                            done = nc.tensor.matmul(ps[f][half(h), c * C:(c + 1) * C],
                                                    w["states"][half(h), CC + c, f, :],
                                                    w["qg"][half(h), f, c * C:(c + 1) * C],
                                                    start=False, stop=c % 2 == 1)
                done.then_inc(summed, 1)

        @block.vector
        def _(dve):
            for f in range(NR):
                dve.wait_ge(summed, f + 1)
                if d == 0:
                    nc.vector.tensor_copy(o[:, f, :], ps[f][:, :])
                else:
                    nc.vector.tensor_tensor(o[:, f, :], o[:, f, :], ps[f][:, :], ALU.add)


def head_rms(nc, t, o, gain):
    with Stage(nc, "hgrn_rms") as st:
        squared = st.sem("squared")
        mean = st.sem("mean")
        eps_ok = st.sem("eps")
        root = st.sem("root")
        inv = st.sem("inverse")
        gained = st.sem("gained")
        sq = st.sbuf("sq", [P, NR, LAT])
        ps = st.banks("ps", NR)
        block = st.block()

        @block.scalar
        def _(act):
            nc.scalar.activation(sq[:, :, :], o[:, :, :], ACT.Square).then_inc(squared, 1)
            act.wait_ge(eps_ok, NR)
            nc.scalar.activation(sq[:, :, :], sq[:, :, :], ACT.Sqrt).then_inc(root, 1)

        @block.tensor
        def _(pe):
            pe.wait_ge(squared, 1)
            for f in range(NR):
                nc.tensor.matmul(ps[f][:, :], t["mask"][:, MASKS["heads"], :], sq[:, f, :],
                                 start=True, stop=True).then_inc(mean, 1)

        @block.vector
        def _(dve):
            for f in range(NR):
                dve.wait_ge(mean, NR)
                nc.vector.tensor_scalar(sq[:, f, :], ps[f][:, :], 1.0 / HD, 1e-6, ALU.mult, ALU.add).then_inc(eps_ok, 1)
            for f in range(NR):
                nc.vector.tensor_scalar(o[:, f, :], o[:, f, :], gain(f), None, ALU.mult).then_inc(gained, 1)
            dve.wait_ge(root, 1)
            nc.vector.reciprocal(sq[:, :, :], sq[:, :, :]).then_inc(inv, 1)
            dve.wait_ge(inv, 1)
            dve.wait_ge(gained, NR)
            nc.vector.tensor_tensor(o[:, :, :], o[:, :, :], sq[:, :, :], ALU.mult)


def hgrn(nc, t, p, o, mem):
    def buf(name, shape):
        return mem.enter_context(nc.sbuf_tensor(f"hg_{name}", shape, F32))

    ident = t["mask"][:, MASKS["ident"], :]
    vt = buf("vt", [P, TT, D_HGRN])
    to_tokens(nc, "hgrn_vt", [([p[:, 3 + f, i * P:(i + 1) * P] for f in range(NR)], vt[:, i, :])
                              for i in range(TT)], ident)
    w = {
        "q": buf("q", [P, NR, LAT]),
        "k": [buf(f"k{s}", [P, NR, n]) for s, (_, n) in enumerate(SEGS)],
        "kh": [buf(f"kh{s}", [P, NR, n]) for s, (_, n) in enumerate(SEGS)],
        "qg": buf("qg", [P, NR, LAT]), "g": buf("g", [P, NR, LAT]), "end": buf("end", [P, NR, NC]),
    }
    for d in range(2):
        hgrn_prepare(nc, t, d, p, w)
        with ExitStack() as late:
            w["scores"] = late.enter_context(nc.sbuf_tensor(f"hg_scores_{d}", [P, 24, P], F32))
            hgrn_scores(nc, t, d, w)
            w["kht"] = late.enter_context(nc.sbuf_tensor(f"hg_kht_{d}", [P, TT, D_HGRN], F32))
            w["states"] = late.enter_context(nc.sbuf_tensor(f"hg_states_{d}", [P, NC, NR, HD], F32))
            tok = [(0, i) for i in range(CT)] + [(1, i) for i in range(LAT // P)]
            to_tokens(nc, f"hgrn{d}_kht",
                      [([w["kh"][s][:, f, i * P:(i + 1) * P] for f in range(NR)], w["kht"][:, n, :])
                       for n, (s, i) in enumerate(tok)], ident)
            hgrn_states(nc, d, w, vt)
            hgrn_outputs(nc, d, w, vt, o)
    head_rms(nc, t, o, lambda f: col(t, "hgrn_norm_g", f))



def inverses(nc, t, name, lt, xt, groups, d):
    g_slots = 3
    waves = [groups[a:a + g_slots] for a in range(0, len(groups), g_slots)]
    flat = [(w, lv, g) for w, wave in enumerate(waves) for lv in range(6) for g in range(len(wave))]
    at_mask = {key: n for n, key in enumerate(flat)}
    at_merge = {key: n for n, key in enumerate(k for k in flat if k[1] >= 1)}
    at_turn = {key: n for n, key in enumerate(k for k in flat if k[1] < 5)}
    at_init = {key[::2]: n for n, key in enumerate(k for k in flat if k[1] == 0)}
    ident = t["mask"][:, MASKS["ident"], :]
    with Stage(nc, name) as st:
        ct = st.sbuf("ct", [P, g_slots, 4, P])
        x = st.sbuf("x", [P, g_slots, 4, P])
        xs = st.sbuf("xs", [P, g_slots, 4, P])
        cx = st.sbuf("cx", [P, g_slots, 4, P])
        masked = st.sem("masked")
        first = st.sem("first")
        product1 = st.sem("product1")
        copied = st.sem("copied")
        product2 = st.sem("product2")
        added = st.sem("added")
        turned = st.sem("turned")
        kept = st.sem("kept")
        bank_a = st.banks("a", g_slots)
        bank_b = st.banks("b", g_slots)
        block = st.block()

        def four(bank):
            return bank[:, :].rearrange("p (a t) -> p a t", t=P)

        @block.gpsimd
        def _(pool):
            for w, lv, g in flat:
                if lv == 0 and w:
                    pool.wait_ge(product1, at_merge[w - 1, 5, g] + 1)
                if lv == 1:
                    pool.wait_ge(first, at_init[w, g] + 1)
                if lv >= 2:
                    pool.wait_ge(product1, at_merge[w, lv - 1, g] + 1)
                m = t["mask"][:, MASKS[f"level{lv}_{d}"], :]
                nc.gpsimd.tensor_tensor(ct[:, g], lt[:, waves[w][g], :], spread(m, 1, 4), ALU.mult
                                        ).then_inc(masked, 1)

        @block.vector
        def _(dve):
            for w, wave in enumerate(waves):
                for g in range(len(wave)):
                    dve.wait_ge(masked, at_mask[w, 0, g] + 1)
                    if w:
                        dve.wait_ge(added, at_merge[w - 1, 5, g] + 1)
                    nc.vector.tensor_tensor(xs[:, g], ct[:, g], spread(ident, 1, 4), ALU.add).then_inc(first, 1)
                for lv in range(1, 6):
                    for g in range(len(wave)):
                        dve.wait_ge(product2, at_merge[w, lv, g] + 1)
                        if lv < 5:
                            ins = nc.vector.tensor_tensor(x[:, g], x[:, g], four(bank_b[g]), ALU.add)
                        else:
                            ins = nc.vector.tensor_tensor(xt[:, wave[g], :], xs[:, g], four(bank_b[g]), ALU.add)
                        ins.then_inc(added, 1)

        @block.scalar
        def _(act):
            for w, wave in enumerate(waves):
                for g in range(len(wave)):
                    act.wait_ge(turned, at_turn[w, 0, g] + 1)
                    nc.scalar.activation(x[:, g], four(bank_a[g]), ACT.Copy).then_inc(kept, 1)
                for lv in range(1, 6):
                    for g in range(len(wave)):
                        act.wait_ge(product1, at_merge[w, lv, g] + 1)
                        nc.scalar.activation(cx[:, g], four(bank_a[g]), ACT.Copy).then_inc(copied, 1)
                    for g in range(len(wave)):
                        if lv < 5:
                            act.wait_ge(turned, at_turn[w, lv, g] + 1)
                            nc.scalar.activation(xs[:, g], four(bank_a[g]), ACT.Copy).then_inc(kept, 1)

        @block.tensor
        def _(pe):
            def turn(src, g):
                for a in range(4):
                    done = nc.tensor.transpose(bank_a[g][:, a * P:(a + 1) * P], src[:, g, a, :], ident)
                done.then_inc(turned, 1)

            for w, wave in enumerate(waves):
                for g in range(len(wave)):
                    pe.wait_ge(first, at_init[w, g] + 1)
                    turn(xs, g)
                for lv in range(1, 6):
                    for g in range(len(wave)):
                        pe.wait_ge(masked, at_mask[w, lv, g] + 1)
                        pe.wait_ge(kept, at_turn[w, lv - 1, g] + 1)
                        for a in range(4):
                            done = nc.tensor.matmul(bank_a[g][:, a * P:(a + 1) * P], ct[:, g, a, :],
                                                    x[:, g, a, :], start=True, stop=True)
                        done.then_inc(product1, 1)
                    for g in range(len(wave)):
                        pe.wait_ge(copied, at_merge[w, lv, g] + 1)
                        for a in range(4):
                            left, right = (xs, cx) if lv < 5 else (cx, xs)
                            done = nc.tensor.matmul(bank_b[g][:, a * P:(a + 1) * P], left[:, g, a, :],
                                                    right[:, g, a, :], start=True, stop=True)
                        done.then_inc(product2, 1)
                    for g in range(len(wave)):
                        if lv < 5:
                            pe.wait_ge(added, at_merge[w, lv, g] + 1)
                            turn(x, g)



DECAY = float(np.exp(-0.5))


def rwkv_common(nc, t, u, kk, th):
    with Stage(nc, "rwkv_common") as st:
        sq = st.sbuf("sq", [P, NR, T])
        scaled = st.sem("scaled")
        squared = st.sem("squared")
        summed = st.sem("summed")
        eps_ok = st.sem("eps")
        root = st.sem("root")
        inv = st.sem("inverse")
        ps = st.banks("ps", 2 * NR)
        block = st.block()

        @block.vector
        def _(dve):
            for f in range(NR):
                nc.vector.tensor_scalar(kk[:, f, :], u[:, 3 + f, :], col(t, "rwkv_k_k", f), None, ALU.mult
                                        ).then_inc(scaled, 1)
            for f in range(NR):
                for s, (t0, n) in enumerate(SEGS):
                    dve.wait_ge(summed, 2 * f + s + 1)
                    nc.vector.tensor_scalar(sq[:, f, t0:t0 + n], ps[2 * f + s][:, :n], 1e-12, None, ALU.add
                                            ).then_inc(eps_ok, 1)
            dve.wait_ge(root, 1)
            nc.vector.reciprocal(sq[:, :, :], sq[:, :, :]).then_inc(inv, 1)
            dve.wait_ge(inv, 1)
            nc.vector.tensor_tensor(kk[:, :, :], kk[:, :, :], sq[:, :, :], ALU.mult)

        @block.scalar
        def _(act):
            nc.scalar.activation(th[:, :], u[:, 9, :], ACT.Tanh)
            act.wait_ge(scaled, NR)
            nc.scalar.activation(sq[:, :, :], kk[:, :, :], ACT.Square).then_inc(squared, 1)
            act.wait_ge(eps_ok, 2 * NR)
            nc.scalar.activation(sq[:, :, :], sq[:, :, :], ACT.Sqrt).then_inc(root, 1)

        @block.tensor
        def _(pe):
            pe.wait_ge(squared, 1)
            for f in range(NR):
                for s, (t0, n) in enumerate(SEGS):
                    nc.tensor.matmul(ps[2 * f + s][:, :n], t["mask"][:, MASKS["heads"], :], sq[:, f, t0:t0 + n],
                                     start=True, stop=True).then_inc(summed, 1)


def rwkv_prepare(nc, t, d, u, w):
    with Stage(nc, f"rwkv{d}_prep") as st:
        sg = st.sbuf("sg", [P, NR, T])
        gs = st.sbuf("gs", [P, NR, T])
        a = st.sbuf("a", [P, NR, T])
        km = st.sbuf("km", [P, NR, T])
        inv, rest, incl = w["bt"], w["bh"], w["rt"]
        lora = st.sem("lora")
        gate_ok = st.sem("gate")
        scanned = st.sem("scanned")
        excl_ok = st.sem("exclusive")
        rest_ok = st.sem("rest")
        exp_ok = st.sem("exp")
        bn_ok = st.sem("bn")
        km_ok = st.sem("km")
        kh_ok = st.sem("kh")
        own = st.sem("own")
        ps = st.banks("ps", 8)
        block = st.block()
        jobs = [(wh, f, s) for wh in range(2) for f in range(NR) for s in range(2)]
        rank = slice(64 * d, 64 * d + 64)

        @block.tensor
        def _(pe):
            for n, (wh, f, s) in enumerate(jobs):
                t0, tn = SEGS[s]
                if n >= 8:
                    pe.wait_ge(gate_ok, n - 7)
                up = t["a_up" if wh else "w_up"][rank, f * P:(f + 1) * P]
                src = u[rank, 10, t0:t0 + tn] if wh else t["th"][rank, t0:t0 + tn]
                nc.tensor.matmul(ps[n % 8][:, :tn], up, src, start=True, stop=True).then_inc(lora, 1)

        @block.scalar
        def _(act):
            for n, (wh, f, s) in enumerate(jobs):
                t0, tn = SEGS[s]
                act.wait_ge(lora, n + 1)
                nc.scalar.activation((a if wh else sg)[:, f, t0:t0 + tn], ps[n % 8][:, :tn], ACT.Sigmoid,
                                     bias=col(t, "rwkv_a0" if wh else "rwkv_w0", 3 * d + f)).then_inc(gate_ok, 1)
            act.wait_ge(scanned, NR)
            nc.scalar.activation(inv[:, :, :], gs[:, :, :], ACT.Exp, scale=DECAY).then_inc(exp_ok, 1)
            act.wait_ge(excl_ok, 1)
            nc.scalar.activation(sg[:, :, :], sg[:, :, :], ACT.Exp, scale=-DECAY).then_inc(exp_ok, 1)
            act.wait_ge(rest_ok, 1)
            nc.scalar.activation(rest[:, :, :], rest[:, :, :], ACT.Exp, scale=-DECAY).then_inc(exp_ok, 1)
            nc.scalar.activation(incl[:, :, :], seg(gs, 1), ACT.Exp, scale=-DECAY).then_inc(exp_ok, 1)
            ends = gs[:, :, :].rearrange("p f (c t) -> p f c t", t=C)[:, :, :, (0 if d else C - 1)]
            nc.scalar.activation(w["end"][:, :, :], ends, ACT.Exp, scale=-DECAY)

        @block.vector
        def _(dve):
            chain = Chain(dve, own)
            chain(nc.vector.tensor_scalar(t["one_ka"][:, :], cols_of(t, "rwkv_k_a"), -1.0, 1.0, ALU.mult, ALU.add))
            dve.wait_ge(gate_ok, 2 * NR)
            for f in range(NR):
                src, dst = sg[:, f, :], gs[:, f, :]
                if d:
                    src, dst = src[:, ::-1], dst[:, ::-1]
                nc.vector.tensor_tensor_scan(dst, t["turn"][:, :], src, 0.0, ALU.mult, ALU.add).then_inc(scanned, 1)
            dve.wait_ge(scanned, NR)
            nc.vector.tensor_tensor(sg[:, :, :], gs[:, :, :], sg[:, :, :], ALU.subtract).then_inc(excl_ok, 1)
            for f in range(NR):
                gv = gs[:, f, :].rearrange("p (c t) -> p c t", t=C)
                ins = nc.vector.tensor_tensor(rest[:, f, :].rearrange("p (c t) -> p c t", t=C),
                                              spread(gv[:, :, (0 if d else C - 1)], 2, C), gv, ALU.subtract)
            ins.then_inc(rest_ok, 1)
            dve.wait_ge(gate_ok, 4 * NR)
            for f in range(NR):
                ins = nc.vector.tensor_scalar(km[:, f, :], a[:, f, :], col(t, "rwkv_k_a", f),
                                              t["one_ka"][:, f:f + 1], ALU.mult, ALU.add)
            chain(ins)
            nc.vector.tensor_tensor(km[:, :, :], km[:, :, :], u[:, 3:6, :], ALU.mult).then_inc(km_ok, 1)
            nc.vector.scalar_tensor_tensor(a[:, :, :], a[:, :, :], -1.0, w["kk"][:, :, :], ALU.mult, ALU.mult
                                           ).then_inc(bn_ok, 1)
            dve.wait_ge(km_ok, 1)
            dve.wait_ge(bn_ok, 1)
            for f in range(NR):
                rk = col(t, "rwkv_r_k", 3 * d + f)
                if d == 0:
                    nc.vector.tensor_scalar(w["bonus"][:, f, :], km[:, f, CTX:], rk, None, ALU.mult)
                else:
                    nc.vector.scalar_tensor_tensor(w["bonus"][:, f, :], km[:, f, CTX:], rk, w["bonus"][:, f, :],
                                                   ALU.mult, ALU.add)
            dve.wait_ge(exp_ok, 1)
            chain(nc.vector.tensor_tensor(w["kt"][:, :, :], km[:, :, :], inv[:, :, :], ALU.mult))
            nc.vector.tensor_tensor(w["bt"][:, :, :], a[:, :, :], inv[:, :, :], ALU.mult)
            dve.wait_ge(exp_ok, 2)
            nc.vector.tensor_tensor(w["at"][:, :, :], w["kk"][:, :, :], sg[:, :, :], ALU.mult)
            dve.wait_ge(exp_ok, 4)
            nc.vector.tensor_tensor(w["rt"][:, :, :], seg(u[:, 0:3, :], 1), incl[:, :, :], ALU.mult)

        @block.gpsimd
        def _(pool):
            pool.wait_ge(km_ok, 1)
            pool.wait_ge(bn_ok, 1)
            pool.wait_ge(exp_ok, 3)
            nc.gpsimd.tensor_tensor(w["kh"][:, :, :], km[:, :, :], rest[:, :, :], ALU.mult).then_inc(kh_ok, 1)
            pool.wait_ge(kh_ok, 1)
            nc.gpsimd.tensor_tensor(w["bh"][:, :, :], a[:, :, :], rest[:, :, :], ALU.mult)


RWKV_TILES = [(i, h) for i in range(TT) for h in range(6)]


def rwkv_grams(nc, t, d, w, y):
    with Stage(nc, f"rwkv{d}_grams") as st:
        gram = st.sem("gram")
        masked = st.sem("masked")
        used = st.sem("used")
        lkv_read = st.sem("lkv_read")
        lk = st.sbuf("lk", [P, 4, 2, P])
        ps = st.banks("g", 3)
        lps = st.banks("l", 2)
        yps = st.banks("y", NR)
        block = st.block()
        strict = t["mask"][:, MASKS[f"strict{d}"], :]
        incl = t["mask"][:, MASKS[f"incl{d}"], :]
        n_tiles = len(RWKV_TILES)

        @block.tensor
        def _(pe):
            def grams(n):
                i, h = RWKV_TILES[n]
                tok = slice(i * P, (i + 1) * P)
                f = h // 2
                if n >= 3:
                    pe.wait_ge(masked, n - 2)
                elif n:
                    pass
                for e, left in enumerate((w["bt"], w["kt"])):
                    done = nc.tensor.matmul(ps[n % 3][:, e * P:(e + 1) * P], left[half(h), f, tok],
                                            w["at"][half(h), f, tok], start=True, stop=True)
                    if i >= CT:
                        lat = slice((i - CT) * P, (i - CT + 1) * P)
                        done = nc.tensor.matmul(ps[n % 3][:, (2 + e) * P:(3 + e) * P], left[half(h), f, tok],
                                                w["rt"][half(h), f, lat], start=True, stop=True)
                done.then_inc(gram, 1)

            def uses(n):
                i, h = RWKV_TILES[n]
                hd = slice(HD * h, HD * h + HD)
                pe.wait_ge(masked, n + 1)
                if h == 0 and i >= 2:
                    pe.wait_ge(lkv_read, i - 1)
                done = nc.tensor.matmul(lps[i % 2][:, hd], lk[:, n % 4, 0, :], w["vt"][:, i, hd],
                                        start=True, stop=True)
                if i >= CT:
                    done = nc.tensor.matmul(yps[h // 2][half(h), (i - CT) * P:(i - CT + 1) * P], w["vt"][:, i, hd],
                                            lk[:, n % 4, 1, :], start=True, stop=True)
                done.then_inc(used, 1)

            for n in range(n_tiles):
                grams(n)
                if n:
                    uses(n - 1)
            uses(n_tiles - 1)

        @block.vector
        def _(dve):
            for n, (i, h) in enumerate(RWKV_TILES):
                dve.wait_ge(gram, n + 1)
                if n >= 4:
                    dve.wait_ge(used, n - 3)
                bank = ps[n % 3]
                nc.vector.tensor_tensor(w["lt"][:, n, :], bank[:, 0:P], strict, ALU.mult)
                ins = nc.vector.tensor_tensor(lk[:, n % 4, 0, :], bank[:, P:2 * P], strict, ALU.mult)
                if i >= CT:
                    m = n - CT * 6
                    nc.vector.tensor_tensor(w["arb"][:, m, :], bank[:, 2 * P:3 * P], incl, ALU.mult)
                    ins = nc.vector.tensor_tensor(lk[:, n % 4, 1, :], bank[:, 3 * P:4 * P], incl, ALU.mult)
                ins.then_inc(masked, 1)
            dve.wait_ge(used, n_tiles)
            for f in range(NR):
                if d == 0:
                    nc.vector.tensor_copy(y[:, f, :], yps[f][:, :])
                else:
                    nc.vector.tensor_tensor(y[:, f, :], y[:, f, :], yps[f][:, :], ALU.add)

        @block.scalar
        def _(act):
            for i in range(TT):
                act.wait_ge(used, 6 * i + 6)
                nc.scalar.activation(w["lkv"][:, i, :], lps[i % 2][:, :D_RWKV], ACT.Copy).then_inc(lkv_read, 1)


def rwkv_solve(nc, d, w):
    with Stage(nc, f"rwkv{d}_solve") as st:
        m1_ok = st.sem("m1")
        m2_ok = st.sem("m2")
        m1_read = st.sem("m1_read")
        m2_read = st.sem("m2_read")
        a_ps = st.banks("a", 2)
        b_ps = st.banks("b", 2)
        block = st.block()

        @block.tensor
        def _(pe):
            for i in range(TT):
                if i >= 2:
                    pe.wait_ge(m1_read, i - 1)
                    pe.wait_ge(m2_read, i - 1)
                for h in range(6):
                    hd = slice(HD * h, HD * h + HD)
                    xt = w["xt"][:, 6 * i + h, :]
                    last1 = nc.tensor.matmul(a_ps[i % 2][half(h), (h // 2) * P:(h // 2 + 1) * P], w["att"][:, i, hd],
                                             xt, start=True, stop=True)
                    if h == 5:
                        last1.then_inc(m1_ok, 1)
                    last2 = nc.tensor.matmul(b_ps[i % 2][:, hd], xt, w["lkv"][:, i, hd], start=True, stop=True)
                last2.then_inc(m2_ok, 1)

        @block.scalar
        def _(act):
            for i in range(TT):
                act.wait_ge(m1_ok, i + 1)
                nc.scalar.activation(w["m1t"][:, :, i * P:(i + 1) * P],
                                     a_ps[i % 2][:, :NR * P].rearrange("p (f t) -> p f t", t=P), ACT.Copy
                                     ).then_inc(m1_read, 1)

        @block.vector
        def _(dve):
            for i in range(TT):
                dve.wait_ge(m2_ok, i + 1)
                nc.vector.tensor_copy(w["m2"][:, i, :], b_ps[i % 2][:, :D_RWKV]).then_inc(m2_read, 1)


def rwkv_states(nc, d, w):
    with Stage(nc, f"rwkv{d}_states") as st:
        sa_ps_ok = st.sem("sa_product")
        sa_ok = st.sem("sa")
        decayed = st.sem("decayed")
        update = st.sem("update")
        state_ok = st.sem("state")
        tmp = st.sbuf("tmp", [P, 2, NR, HD])
        even = st.banks("even", 2)
        odd = st.banks("odd", 2)
        ups = st.banks("up", 2)
        block = st.block()
        order = chunk_order(d)
        states, sa = w["states"], w["sa"]

        @block.tensor
        def _(pe):
            for n, c in enumerate(order):
                tok, i = slice(C * (c % 2), C * (c % 2) + C), c // 2
                pe.wait_ge(state_ok, n + 1)
                for h in range(6):
                    bank = (even, odd)[h % 2][n % 2]
                    done = nc.tensor.matmul(bank[tok, HD * (h // 2):HD * (h // 2) + HD],
                                            w["m1t"][half(h), h // 2, c * C:(c + 1) * C],
                                            states[half(h), c, h // 2, :], start=True, stop=True)
                done.then_inc(sa_ps_ok, 1)
                if n == NC - 1:
                    break
                pe.wait_ge(sa_ok, n + 1)
                for h in range(6):
                    hd = slice(HD * h, HD * h + HD)
                    out = ups[n % 2][half(h), HD * (h // 2):HD * (h // 2) + HD]
                    nc.tensor.matmul(out, w["kht"][tok, i, hd], w["vt"][tok, i, hd], start=True, stop=False)
                    done = nc.tensor.matmul(out, w["bht"][tok, i, hd], sa[tok, i, hd], start=False, stop=True)
                done.then_inc(update, 1)

        @block.gpsimd
        def _(pool):
            for n, c in enumerate(order[:-1]):
                pool.wait_ge(state_ok, n + 1)
                nc.gpsimd.tensor_tensor(tmp[:, n % 2], states[:, c], spread(w["end"][:, :, c], 2, HD), ALU.mult
                                        ).then_inc(decayed, 1)

        @block.vector
        def _(dve):
            nc.vector.memset(states[:, order[0]], 0.0).then_inc(state_ok, 1)
            for n, c in enumerate(order):
                tok, i = slice(C * (c % 2), C * (c % 2) + C), c // 2
                dve.wait_ge(sa_ps_ok, n + 1)
                for e, bank in enumerate((even[n % 2], odd[n % 2])):
                    def pairs(ap):
                        return ap.rearrange("p (f e v) -> p f e v", e=2, v=HD)[:, :, e, :]
                    ins = nc.vector.tensor_tensor(pairs(sa[tok, i, :]), pairs(w["m2"][tok, i, :]),
                                                  bank[tok, :NR * HD].rearrange("p (f v) -> p f v", v=HD), ALU.add)
                ins.then_inc(sa_ok, 1)
                if n == NC - 1:
                    break
                dve.wait_ge(decayed, n + 1)
                dve.wait_ge(update, n + 1)
                nc.vector.tensor_tensor(states[:, order[n + 1]], tmp[:, n % 2],
                                        ups[n % 2][:, :NR * HD].rearrange("p (f v) -> p f v", v=HD), ALU.add
                                        ).then_inc(state_ok, 1)


def rwkv_outputs(nc, d, w, y):
    with Stage(nc, f"rwkv{d}_out") as st:
        summed = st.sem("summed")
        ps = st.banks("ps", NR)
        block = st.block()

        @block.tensor
        def _(pe):
            for f in range(NR):
                for i in range(LAT // P):
                    for h in (2 * f, 2 * f + 1):
                        hd = slice(HD * h, HD * h + HD)
                        nc.tensor.matmul(ps[f][half(h), i * P:(i + 1) * P], w["sa"][:, CT + i, hd],
                                         w["arb"][:, 6 * i + h, :], start=True, stop=False)
                        for c in (2 * i, 2 * i + 1):
                            done = nc.tensor.matmul(ps[f][half(h), c * C:(c + 1) * C],
                                                    w["states"][half(h), CC + c, f, :],
                                                    w["rt"][half(h), f, c * C:(c + 1) * C],
                                                    start=False, stop=c % 2 == 1)
                done.then_inc(summed, 1)

        @block.vector
        def _(dve):
            for f in range(NR):
                dve.wait_ge(summed, f + 1)
                nc.vector.tensor_tensor(y[:, f, :], y[:, f, :], ps[f][:, :], ALU.add)


def rwkv_readout(nc, t, u, bonus, y):
    with Stage(nc, "rwkv_readout") as st:
        sq = st.sbuf("sq", [P, NR, LAT])
        rb = st.sbuf("rb", [P, NR, LAT])
        mean_ok = st.sem("mean")
        rb_ok = st.sem("rb")
        centered = st.sem("centered")
        squared = st.sem("squared")
        var_ok = st.sem("var")
        sum_ok = st.sem("bonus_sum")
        eps_ok = st.sem("eps")
        root = st.sem("root")
        own = st.sem("own")
        mps = st.banks("m", 2)
        vps = st.banks("v", NR)
        bps = st.banks("b", NR)
        block = st.block()
        heads = t["mask"][:, MASKS["heads"], :]
        v = seg(u[:, 6:9, :], 1)

        @block.gpsimd
        def _(pool):
            nc.gpsimd.tensor_tensor(rb[:, :, :], bonus[:, :, :], seg(u[:, 0:3, :], 1), ALU.mult).then_inc(rb_ok, 1)

        @block.tensor
        def _(pe):
            for f in range(NR):
                if f == 2:
                    pe.wait_ge(centered, 1)
                nc.tensor.matmul(mps[f % 2][:, :], heads, y[:, f, :], start=True, stop=True).then_inc(mean_ok, 1)
            pe.wait_ge(rb_ok, 1)
            for f in range(NR):
                nc.tensor.matmul(bps[f][:, :], heads, rb[:, f, :], start=True, stop=True).then_inc(sum_ok, 1)
            pe.wait_ge(squared, 1)
            for f in range(NR):
                nc.tensor.matmul(vps[f][:, :], heads, sq[:, f, :], start=True, stop=True).then_inc(var_ok, 1)

        @block.scalar
        def _(act):
            act.wait_ge(centered, NR)
            nc.scalar.activation(sq[:, :, :], y[:, :, :], ACT.Square).then_inc(squared, 1)
            act.wait_ge(eps_ok, NR)
            nc.scalar.activation(sq[:, :, :], sq[:, :, :], ACT.Sqrt).then_inc(root, 1)

        @block.vector
        def _(dve):
            chain = Chain(dve, own)
            for f in range(NR):
                dve.wait_ge(mean_ok, f + 1)
                nc.vector.scalar_tensor_tensor(y[:, f, :], mps[f % 2][:, :], -1.0 / HD, y[:, f, :],
                                               ALU.mult, ALU.add).then_inc(centered, 1)
            dve.wait_ge(centered, NR)
            for f in range(NR):
                dve.wait_ge(var_ok, NR)
                nc.vector.tensor_scalar(sq[:, f, :], vps[f][:, :], 1.0 / HD, 64e-5, ALU.mult, ALU.add).then_inc(eps_ok, 1)
            for f in range(NR):
                dve.wait_ge(sum_ok, f + 1)
                ins = nc.vector.tensor_tensor(rb[:, f, :], bps[f][:, :], v[:, f, :], ALU.mult)
            chain(ins)
            dve.wait_ge(root, 1)
            chain(nc.vector.reciprocal(sq[:, :, :], sq[:, :, :]))
            chain(nc.vector.tensor_tensor(y[:, :, :], y[:, :, :], sq[:, :, :], ALU.mult))
            for f in range(NR):
                ins = nc.vector.tensor_scalar(y[:, f, :], y[:, f, :], col(t, "rwkv_gn_g", f), col(t, "rwkv_gn_b", f),
                                              ALU.mult, ALU.add)
            chain(ins)
            nc.vector.tensor_tensor(y[:, :, :], y[:, :, :], rb[:, :, :], ALU.add)


def rwkv(nc, t, u, y, mem):
    def buf(name, shape, where=mem):
        return where.enter_context(nc.sbuf_tensor(f"rw_{name}", shape, F32))

    ident = t["mask"][:, MASKS["ident"], :]
    t["th"] = buf("th", [P, T])
    t["w_up"], t["a_up"] = buf("w_up", [P, D_RWKV]), buf("a_up", [P, D_RWKV])
    t["one_ka"] = buf("one_ka", [P, NR])
    load(nc, "load_up", [(t["w_up"][:, :], t["dram"]["w_up"]), (t["a_up"][:, :], t["dram"]["a_up"])])
    w = {"kk": buf("kk", [P, NR, T]), "bonus": buf("bonus", [P, NR, LAT]), "end": buf("end", [P, NR, NC]),
         "vt": buf("vt", [P, TT, D_RWKV])}
    rwkv_common(nc, t, u, w["kk"], t["th"])
    to_tokens(nc, "rwkv_vt", [([u[:, 6 + f, i * P:(i + 1) * P] for f in range(NR)], w["vt"][:, i, :])
                              for i in range(TT)], ident)
    for d in range(2):
        with ExitStack() as own:
            w["rt"] = buf(f"rt{d}", [P, NR, LAT], own)
            right = ExitStack()

            def right_buf(name, shape, stack):
                return stack.enter_context(nc.sbuf_tensor(f"rw_{name}{d}", shape, F32, side="right"))
            for name in ("kt", "bt", "at"):
                w[name] = right_buf(name, [P, NR, T], right)
            ends = ExitStack()
            for name in ("kh", "bh"):
                w[name] = right_buf(name, [P, NR, T], ends)
            rwkv_prepare(nc, t, d, u, w)
            for name in ("kht", "bht", "att"):
                w[name] = buf(f"{name}{d}", [P, TT, D_RWKV], own)
            to_tokens(nc, f"rwkv{d}_tok",
                      [([w[src][:, f, i * P:(i + 1) * P] for f in range(NR)], w[dst][:, i, :])
                       for src, dst in (("kh", "kht"), ("bh", "bht"), ("at", "att")) for i in range(TT)], ident)
            ends.close()
            w["lt"] = buf(f"lt{d}", [P, len(RWKV_TILES), P], own)
            w["arb"] = buf(f"arb{d}", [P, 24, P], own)
            w["lkv"] = buf(f"lkv{d}", [P, TT, D_RWKV], own)
            rwkv_grams(nc, t, d, w, y)
            right.close()
            w["xt"] = w["lt"]
            inverses(nc, t, f"rwkv{d}_inv", w["lt"], w["xt"], [slice(a, a + 4) for a in range(0, 36, 4)], d)
            w["m1t"] = buf(f"m1t{d}", [P, NR, T], own)
            w["m2"] = buf(f"m2{d}", [P, TT, D_RWKV], own)
            rwkv_solve(nc, d, w)
            w["sa"] = buf(f"sa{d}", [P, TT, D_RWKV], own)
            w["states"] = buf(f"states{d}", [P, NC, NR, HD], own)
            rwkv_states(nc, d, w)
            rwkv_outputs(nc, d, w, y)
    rwkv_readout(nc, t, u, w["bonus"], y)



POOL_PAD = 8
GRID = 64
POOL_ROWS = LAT // GRID
WINDOWS = (2, 4, 8, 16)


def pool_counts():
    c = np.arange(GRID)
    out = np.zeros((P, 2, GRID), np.float32)
    for g, win in enumerate(WINDOWS):
        left = win // 2
        n = np.minimum(c + win - 1 - left, GRID - 1) + 1 - np.maximum(c - left, 0)
        out[64 * (g % 2):64 * (g % 2) + 64, g // 2] = 1.0 / n
    return out


def pool_branch(nc, t, p, pooled):
    wide = GRID + 2 * POOL_PAD
    with Stage(nc, "pool") as st:
        s = [st.sbuf(f"s{a}", [P, 2, POOL_ROWS, wide]) for a in range(4)]
        mean = st.sbuf("mean", [P, 2, POOL_ROWS, GRID])
        pw = st.sbuf("w", [P, 2, 64])
        inv = st.sbuf("inv", [P, 2, GRID])
        loaded = st.sem("loaded")
        own = st.sem("own")
        mean_ok = st.sem("mean")
        mixed = st.sem("mixed")
        ps = st.banks("ps", 2)
        block = st.block()

        @block.sync
        def _(sp):
            sp.dma_start(pw[:, :, :], t["dram"]["pool_w"]).then_inc(loaded, 16)
            sp.dma_start(inv[:, :, :], t["dram"]["pool_counts"]).then_inc(loaded, 16)
            sp.wait_ge(loaded, 32)

        @block.vector
        def _(dve):
            chain = Chain(dve, own)
            chain(nc.vector.tensor_tensor(s[0][:, :, :, 1:wide], p[:, :, :, 0:wide - 1], p[:, :, :, 1:wide], ALU.add))
            lo, hi = 1, wide
            for a, off in ((1, 1), (2, 2), (3, 4)):
                lo, hi = lo + off, hi - off
                chain(nc.vector.tensor_tensor(s[a][:, :, :, lo:hi], s[a - 1][:, :, :, lo - off:hi - off],
                                              s[a - 1][:, :, :, lo + off:hi + off], ALU.add))
            dve.wait_ge(loaded, 32)
            mid = slice(POOL_PAD, POOL_PAD + GRID)
            for g in range(4):
                hp = slice(64 * (g % 2), 64 * (g % 2) + 64)
                ins = nc.vector.tensor_tensor(mean[hp, g // 2], s[g][hp, g // 2, :, mid],
                                              spread(inv[hp, g // 2, :], 1, POOL_ROWS), ALU.mult)
            chain(ins)
            nc.vector.tensor_tensor(mean[:, :, :, :], mean[:, :, :, :], p[:, :, :, mid], ALU.subtract
                                    ).then_inc(mean_ok, 1)
            dve.wait_ge(mixed, 1)
            for f in range(2):
                nc.vector.tensor_scalar(pooled[:, f, :], ps[f][:, :], col(t, "pool_scale", f), None, ALU.mult)

        @block.tensor
        def _(pe):
            pe.wait_ge(loaded, 32)
            pe.wait_ge(mean_ok, 1)
            for g in range(4):
                hp = slice(64 * (g % 2), 64 * (g % 2) + 64)
                done = nc.tensor.matmul(ps[g // 2][hp, :], pw[hp, g // 2, :],
                                        mean[hp, g // 2].rearrange("p r c -> p (r c)"), start=True, stop=True)
            done.then_inc(mixed, 1)


def gated(nc, name, parts, gates, hh, hl, n_tok):
    kt = len(parts)
    with Stage(nc, name) as st:
        full = st.sbuf("full", [P, kt, n_tok])
        full_ok = st.sem("full")
        high = st.sem("high")
        block = st.block()

        @block.vector
        def _(dve):
            for k in range(kt):
                if gates[k] is None:
                    ins = nc.vector.tensor_copy(full[:, k, :], parts[k])
                else:
                    ins = nc.vector.tensor_tensor(full[:, k, :], parts[k], gates[k], ALU.mult)
                ins.then_inc(full_ok, 1)

        @block.scalar
        def _(act):
            for k in range(kt):
                act.wait_ge(full_ok, k + 1)
                nc.scalar.activation(hh[:, k, :n_tok], full[:, k, :], ACT.Copy).then_inc(high, 1)

        @block.gpsimd
        def _(pool):
            for k in range(kt):
                pool.wait_ge(high, k + 1)
                nc.gpsimd.tensor_tensor(hl[:, k, :n_tok], full[:, k, :], hh[:, k, :n_tok].bitcast(F32), ALU.subtract)


def scaled(nc, name, out, src, factor):
    with Stage(nc, name) as st:
        block = st.block()

        @block.scalar
        def _(act):
            nc.scalar.activation(out, src, ACT.Copy, scale=factor)


def into_residual(nc, x, mods, tile0, spans):
    def evac_dve(dve, i, ps, slot):
        for (t0, n, j), b in zip(spans, ps):
            res = x[:, bass.ds(i, 1), t0:t0 + n]
            ins = nc.vector.scalar_tensor_tensor(res, b[:, :n], mods[:, bass.ds(tile0 + i, 1), j:j + 1].rearrange("p a j -> p (a j)"),
                                                 res, ALU.mult, ALU.add)
        return ins
    return evac_dve


ALPHA = float(2.0 ** 0.25)



def unit_norm(nc, name, x, nf, spans, mat, mult, eps, factor):
    jobs = [(f, t0, n) for f in range(nf) for t0, n in spans]
    lo, hi = spans[0][0], spans[-1][0] + spans[-1][1]
    with Stage(nc, name) as st:
        sq = st.sbuf("sq", [P, nf, hi - lo])
        squared = st.sem("squared")
        summed = st.sem("summed")
        eps_ok = st.sem("eps")
        root = st.sem("root")
        inv = st.sem("inverse")
        ps = st.banks("ps", 4)
        block = st.block()

        @block.scalar
        def _(act):
            nc.scalar.activation(sq[:, :, :], x[:, :, lo:hi], ACT.Square).then_inc(squared, 1)
            act.wait_ge(eps_ok, len(jobs))
            nc.scalar.activation(sq[:, :, :], sq[:, :, :], ACT.Sqrt).then_inc(root, 1)

        @block.tensor
        def _(pe):
            pe.wait_ge(squared, 1)
            for n, (f, t0, tn) in enumerate(jobs):
                if n >= 4:
                    pe.wait_ge(eps_ok, n - 3)
                nc.tensor.matmul(ps[n % 4][:, :tn], mat, sq[:, f, t0 - lo:t0 - lo + tn],
                                 start=True, stop=True).then_inc(summed, 1)

        @block.vector
        def _(dve):
            for n, (f, t0, tn) in enumerate(jobs):
                dve.wait_ge(summed, n + 1)
                nc.vector.tensor_scalar(sq[:, f, t0 - lo:t0 - lo + tn], ps[n % 4][:, :tn], mult, eps,
                                        ALU.mult, ALU.add).then_inc(eps_ok, 1)
            dve.wait_ge(root, 1)
            nc.vector.reciprocal(sq[:, :, :], sq[:, :, :]).then_inc(inv, 1)
            dve.wait_ge(inv, 1)
            for f in range(nf):
                nc.vector.scalar_tensor_tensor(x[:, f, lo:hi], x[:, f, lo:hi], factor(f), sq[:, f, :],
                                               ALU.mult, ALU.mult)


GW = 4
HV = 128


def gmlp(nc, t, u, vtok, y):
    jobs = [(f, s) for f in range(GW) for s in range(2)]
    with Stage(nc, "gmlp") as st:
        ws = st.sbuf("ws", [P, GW, P])
        bs = st.sbuf("bs", [P, GW, P])
        tmp = st.sbuf("tmp", [P, GW, T])
        loaded = st.sem("loaded")
        mixed = st.sem("mixed")
        biased = st.sem("biased")
        ps = st.banks("ps", 8)
        block = st.block()

        @block.sync
        def _(sp):
            sp.dma_start(ws[:, :, :], t["dram"]["a_ws"]).then_inc(loaded, 16)
            sp.dma_start(bs[:, :, :], t["dram"]["a_bs"].partition_broadcast(P)).then_inc(loaded, 16)
            sp.wait_ge(loaded, 32)

        @block.tensor
        def _(pe):
            pe.wait_ge(loaded, 32)
            for n, (f, s) in enumerate(jobs):
                t0, tn = SEGS[s]
                for i in range(t0 // P, (t0 + tn) // P):
                    done = nc.tensor.matmul(ps[n][:, i * P - t0:(i + 1) * P - t0], vtok[:, i, f * P:(f + 1) * P],
                                            ws[:, f, :], start=True, stop=True)
                done.then_inc(mixed, 1)

        @block.vector
        def _(dve):
            dve.wait_ge(loaded, 32)
            for n, (f, s) in enumerate(jobs):
                t0, tn = SEGS[s]
                dve.wait_ge(mixed, n + 1)
                nc.vector.tensor_tensor(tmp[:, f, t0:t0 + tn].rearrange("p (c i) -> p c i", i=P),
                                        ps[n][:, :tn].rearrange("p (c i) -> p c i", i=P),
                                        spread(bs[:, f, :], 1, tn // P), ALU.add).then_inc(biased, 1)
            dve.wait_ge(biased, len(jobs))
            nc.vector.tensor_tensor(y[:, :, :], u[:, :, :], tmp[:, :, :], ALU.mult)


ROW = (0, 32)
BETA = 64


def gdn_rows(nc, t, p_ab, rows, rest, toks, w):
    with Stage(nc, "gdn_rows") as st:
        par = st.sbuf("par", [P, 2])
        ea = st.sbuf("ea", [P, 1])
        xr = st.sbuf("xr", [P, T])
        ax = st.sbuf("ax", [P, T])
        loaded = st.sem("loaded")
        x_ok = st.sem("x")
        log_ok = st.sem("log")
        own_a = st.sem("own_act")
        own_v = st.sem("own_dve")
        block = st.block()

        @block.sync
        def _(sp):
            sp.dma_start(par[:, :], t["dram"]["gdn_rows"]).then_inc(loaded, 16)
            sp.wait_ge(loaded, 16)

        @block.scalar
        def _(act):
            act.wait_ge(x_ok, 1)
            chain = Chain(act, own_a)
            chain(nc.scalar.activation(ax[:, :], xr[:, :], ACT.Abs))
            chain(nc.scalar.activation(ax[:, :], ax[:, :], ACT.Exp, scale=-1.0))
            nc.scalar.activation(ea[:, :], par[:, 0:1], ACT.Exp)
            nc.scalar.activation(ax[:, :], ax[:, :], ACT.Ln, bias=1.0).then_inc(log_ok, 1)
            nc.scalar.activation(rows[64:128, :], p_ab[64:128, :], ACT.Sigmoid)

        @block.vector
        def _(dve):
            chain = Chain(dve, own_v)
            nc.vector.memset(rest[64:128, :], 0.0)
            dve.wait_ge(loaded, 16)
            nc.vector.tensor_scalar(xr[:, :], p_ab[:, :], par[:, 1:2], None, ALU.add).then_inc(x_ok, 1)
            dve.wait_ge(log_ok, 1)
            chain(nc.vector.scalar_tensor_tensor(xr[:, :], xr[:, :], 0.0, ax[:, :], ALU.max, ALU.add))
            chain(nc.vector.tensor_scalar(xr[:, :], xr[:, :], ea[:, :], -1.0, ALU.mult, ALU.mult))
            nc.vector.tensor_tensor_scan(rows[0:32, :], t["turn"][0:32, :], xr[0:32, :], 0.0, ALU.mult, ALU.add)
            chain(nc.vector.tensor_tensor_scan(rows[32:64, ::-1], t["turn"][32:64, :], xr[32:64, ::-1], 0.0,
                                               ALU.mult, ALU.add))
            for d in range(2):
                r = slice(32 * d, 32 * d + 32)
                gv = rows[r, :].rearrange("p (c t) -> p c t", t=C)
                nc.vector.tensor_tensor(rest[r, :].rearrange("p (c t) -> p c t", t=C),
                                        spread(gv[:, :, (0 if d else C - 1)], 2, C), gv, ALU.subtract)

    ident = t["mask"][:, MASKS["ident"], :]
    to_tokens(nc, "gdn_rows_tok", [([src[:, i * P:(i + 1) * P]], dst[:, i, :])
                                   for src, dst in zip((rows, rest), toks) for i in range(TT)], ident)
    with Stage(nc, "gdn_scalars") as st:
        exp_ok = st.sem("exp")
        block = st.block()

        @block.scalar
        def _(act):
            nc.scalar.activation(w["kd"][:, :, :], toks[1][:, :, 0:64], ACT.Exp)
            nc.scalar.activation(w["nbg"][:, :, :], toks[0][:, :, 0:64], ACT.Exp).then_inc(exp_ok, 1)

        @block.vector
        def _(dve):
            dve.wait_ge(exp_ok, 1)
            nc.vector.scalar_tensor_tensor(w["nbg"][:, :, :], w["nbg"][:, :, :], -1.0, toks[0][:, :, 64:128],
                                           ALU.mult, ALU.mult)


def gdn_spread(nc, t, d, rows, q, k, w):
    ident = t["mask"][:, MASKS["ident"], :]
    jobs = [(e, h, s) for h in range(GW) for e in range(2) for s in range(2)]
    with Stage(nc, f"gdn{d}_spread") as st:
        row_ok = st.sem("row")
        g_ok = st.sem("g")
        b_ok = st.sem("b")
        e_ok = st.sem("exp")
        ps = st.banks("ps", 8)
        block = st.block()

        @block.tensor
        def _(pe):
            for n, (e, h, s) in enumerate(jobs):
                t0, tn = SEGS[s]
                if n >= 8:
                    pe.wait_ge(b_ok if e else g_ok, 2 * ((n - 8) // 4) + s + 1)
                r = ROW[d] + h + e * BETA
                nc.tensor.matmul(ps[n % 8][:, :tn], ident[:, r:r + 1].to_broadcast([P, P]), rows[:, t0:t0 + tn],
                                 start=True, stop=True).then_inc(row_ok, 1)

        @block.scalar
        def _(act):
            for n, (e, h, s) in enumerate(jobs):
                t0, tn = SEGS[s]
                if e == 0:
                    act.wait_ge(row_ok, n + 1)
                    nc.scalar.activation(w["grow"][:, h, t0:t0 + tn], ps[n % 8][:, :tn], ACT.Copy).then_inc(g_ok, 1)
            act.wait_ge(g_ok, 2 * GW)
            nc.scalar.activation(w["qg"][:, :, :], w["grow"][:, :, :], ACT.Exp).then_inc(e_ok, 1)
            ends = w["grow"][:, :, :].rearrange("p h (c t) -> p h c t", t=C)[:, :, :, (0 if d else C - 1)]
            nc.scalar.activation(w["ge"][:, :, :], ends, ACT.Exp)

        @block.vector
        def _(dve):
            for n, (e, h, s) in enumerate(jobs):
                t0, tn = SEGS[s]
                if e == 1:
                    dve.wait_ge(row_ok, n + 1)
                    nc.vector.scalar_tensor_tensor(w["nkb"][:, h, t0:t0 + tn], ps[n % 8][:, :tn], -1.0,
                                                   k[:, h, t0:t0 + tn], ALU.mult, ALU.mult).then_inc(b_ok, 1)
            dve.wait_ge(e_ok, 1)
            nc.vector.tensor_tensor(w["qg"][:, :, :], q[:, :, :], w["qg"][:, :, :], ALU.mult)


def gdn_grams(nc, t, d, q, k, w):
    with Stage(nc, f"gdn{d}_grams") as st:
        dec = st.sbuf("dec", [P, 2, GW, P])
        ds = st.sbuf("ds", [P, 2, GW, P])
        di = st.sbuf("di", [P, 2, GW, P])
        diff_ok = st.sem("diff")
        dec_ok = st.sem("decay")
        mask_ok = st.sem("masked")
        gram_ok = st.sem("gram")
        out_ok = st.sem("out")
        a_ps = st.banks("a", 2)
        b_ps = st.banks("b", 2)
        block = st.block()

        @block.tensor
        def _(pe):
            for i in range(TT):
                tok = slice(i * P, (i + 1) * P)
                if i >= 2:
                    pe.wait_ge(out_ok, i - 1)
                for h in range(GW):
                    hs = slice(h * P, (h + 1) * P)
                    nc.tensor.matmul(a_ps[i % 2][:, hs], k[:, h, tok], w["nkb"][:, h, tok], start=True, stop=True)
                    done = nc.tensor.matmul(b_ps[i % 2][:, hs], k[:, h, tok], q[:, h, tok], start=True, stop=True)
                done.then_inc(gram_ok, 1)

        @block.vector
        def _(dve):
            def difference(i):
                if i >= 2:
                    dve.wait_ge(mask_ok, 2 * i - 2)
                for h in range(GW):
                    nc.vector.tensor_scalar(dec[:, i % 2, h, :], w["grow"][:, h, i * P:(i + 1) * P],
                                            w["tok"][:, i, ROW[d] + h:ROW[d] + h + 1], 0.0,
                                            ALU.subtract, ALU.min).then_inc(diff_ok, 1)
            difference(0)
            for i in range(TT):
                if i + 1 < TT:
                    difference(i + 1)
                dve.wait_ge(gram_ok, i + 1)
                dve.wait_ge(mask_ok, 2 * i + 2)
                nc.vector.tensor_tensor(w["lt"][:, GW * i:GW * i + GW, :], ds[:, i % 2],
                                        a_ps[i % 2][:, :].rearrange("p (h t) -> p h t", t=P), ALU.mult)
                nc.vector.tensor_tensor(w["attn"][:, GW * i:GW * i + GW, :], di[:, i % 2],
                                        b_ps[i % 2][:, :].rearrange("p (h t) -> p h t", t=P), ALU.mult
                                        ).then_inc(out_ok, 1)

        @block.scalar
        def _(act):
            for i in range(TT):
                act.wait_ge(diff_ok, GW * i + GW)
                nc.scalar.activation(dec[:, i % 2], dec[:, i % 2], ACT.Exp).then_inc(dec_ok, 1)

        @block.gpsimd
        def _(pool):
            for i in range(TT):
                pool.wait_ge(dec_ok, i + 1)
                if i >= 2:
                    pool.wait_ge(out_ok, i - 1)
                for out, m in ((ds, f"strict{d}"), (di, f"incl{d}")):
                    nc.gpsimd.tensor_tensor(out[:, i % 2], dec[:, i % 2],
                                            spread(t["mask"][:, MASKS[m], :], 1, GW), ALU.mult).then_inc(mask_ok, 1)


def gdn_solve(nc, d, w):
    r0 = ROW[d]
    with Stage(nc, f"gdn{d}_solve") as st:
        rhs = st.sbuf("rhs", [P, TT, GW, HV])
        rhs_ok = st.sem("rhs")
        solved = st.sem("solved")
        read = st.sem("read")
        ps = st.banks("ps", 4)
        block = st.block()

        @block.vector
        def _(dve):
            for n, (src, scal) in enumerate(((w["ktok"], w["nbg"][:, :, r0:r0 + GW]),
                                             (w["vtok"], w["tok"][:, :, BETA + r0:BETA + r0 + GW]))):
                if n:
                    dve.wait_ge(solved, TT)
                nc.vector.tensor_tensor(rhs[:, :, :, :], src[:, :, :].rearrange("p i (h c) -> p i h c", h=GW),
                                        spread(scal, 3, HV), ALU.mult).then_inc(rhs_ok, 1)

        @block.tensor
        def _(pe):
            for n in range(2 * TT):
                i = n % TT
                pe.wait_ge(rhs_ok, n // TT + 1)
                if n >= 4:
                    pe.wait_ge(read, n - 3)
                for h in range(GW):
                    out, xt, r = ps[n % 4][:, h * P:(h + 1) * P], w["xt"][:, GW * i + h, :], rhs[:, i, h, :]
                    left, right = (r, xt) if n < TT else (xt, r)
                    done = nc.tensor.matmul(out, left, right, start=True, stop=True)
                done.then_inc(solved, 1)

        @block.scalar
        def _(act):
            for n in range(2 * TT):
                i = n % TT
                act.wait_ge(solved, n + 1)
                out = w["wt"][:, :, i * P:(i + 1) * P] if n < TT else \
                    w["u"][:, i, :].rearrange("p (h v) -> p h v", h=GW)
                nc.scalar.activation(out, ps[n % 4][:, :].rearrange("p (h v) -> p h v", h=GW), ACT.Copy
                                     ).then_inc(read, 1)


def gdn_states(nc, d, w):
    r0 = ROW[d]
    with Stage(nc, f"gdn{d}_states") as st:
        kd = st.sbuf("kd", [P, TT, GW, HV])
        kd_ok = st.sem("kd")
        v_ps_ok = st.sem("v_product")
        v_ok = st.sem("v")
        decayed = st.sem("decayed")
        update = st.sem("update")
        state_ok = st.sem("state")
        tmp = st.sbuf("tmp", [P, 2, GW, HV])
        vps = st.banks("v", 2)
        ups = st.banks("up", 2)
        block = st.block()
        order = chunk_order(d)
        states = w["states"]

        @block.tensor
        def _(pe):
            pe.wait_ge(kd_ok, 1)
            for n, c in enumerate(order):
                tok, i = slice(C * (c % 2), C * (c % 2) + C), c // 2
                pe.wait_ge(state_ok, n + 1)
                for h in range(GW):
                    done = nc.tensor.matmul(vps[n % 2][tok, h * HV:(h + 1) * HV], w["wt"][:, h, c * C:(c + 1) * C],
                                            states[:, c, h, :], start=True, stop=True)
                done.then_inc(v_ps_ok, 1)
                if n == NC - 1:
                    break
                pe.wait_ge(v_ok, n + 1)
                for h in range(GW):
                    done = nc.tensor.matmul(ups[n % 2][:, h * HV:(h + 1) * HV], kd[tok, i, h, :],
                                            w["u"][tok, i, h * HV:(h + 1) * HV], start=True, stop=True)
                done.then_inc(update, 1)

        @block.gpsimd
        def _(pool):
            for n, c in enumerate(order[:-1]):
                pool.wait_ge(state_ok, n + 1)
                nc.gpsimd.tensor_tensor(tmp[:, n % 2], states[:, c], spread(w["ge"][:, :, c], 2, HV), ALU.mult
                                        ).then_inc(decayed, 1)

        @block.vector
        def _(dve):
            nc.vector.memset(states[:, order[0]], 0.0).then_inc(state_ok, 1)
            nc.vector.tensor_tensor(kd[:, :, :, :], w["ktok"][:, :, :].rearrange("p i (h c) -> p i h c", h=GW),
                                    spread(w["kd"][:, :, r0:r0 + GW], 3, HV), ALU.mult).then_inc(kd_ok, 1)
            for n, c in enumerate(order):
                tok, i = slice(C * (c % 2), C * (c % 2) + C), c // 2
                dve.wait_ge(v_ps_ok, n + 1)
                nc.vector.tensor_tensor(w["u"][tok, i, :], w["u"][tok, i, :], vps[n % 2][tok, :], ALU.add
                                        ).then_inc(v_ok, 1)
                if n == NC - 1:
                    break
                dve.wait_ge(decayed, n + 1)
                dve.wait_ge(update, n + 1)
                nc.vector.tensor_tensor(states[:, order[n + 1]], tmp[:, n % 2],
                                        ups[n % 2][:, :].rearrange("p (h v) -> p h v", v=HV), ALU.add
                                        ).then_inc(state_ok, 1)


def gdn_outputs(nc, d, w, o):
    jobs = [(h, s) for h in range(GW) for s in range(2)]
    with Stage(nc, f"gdn{d}_out") as st:
        summed = st.sem("summed")
        ps = st.banks("ps", 8)
        block = st.block()

        @block.tensor
        def _(pe):
            for n, (h, s) in enumerate(jobs):
                t0, tn = SEGS[s]
                for i in range(t0 // P, (t0 + tn) // P):
                    nc.tensor.matmul(ps[n][:, i * P - t0:(i + 1) * P - t0], w["u"][:, i, h * HV:(h + 1) * HV],
                                     w["attn"][:, GW * i + h, :], start=True, stop=False)
                    for c in (2 * i, 2 * i + 1):
                        done = nc.tensor.matmul(ps[n][:, c * C - t0:(c + 1) * C - t0], w["states"][:, c, h, :],
                                                w["qg"][:, h, c * C:(c + 1) * C], start=False, stop=c % 2 == 1)
                done.then_inc(summed, 1)

        @block.vector
        def _(dve):
            for n, (h, s) in enumerate(jobs):
                t0, tn = SEGS[s]
                dve.wait_ge(summed, n + 1)
                if d == 0:
                    nc.vector.tensor_copy(o[:, h, t0:t0 + tn], ps[n][:, :tn])
                else:
                    nc.vector.tensor_tensor(o[:, h, t0:t0 + tn], o[:, h, t0:t0 + tn], ps[n][:, :tn], ALU.add)


def gdn(nc, t, qkv, p_ab, o, mem):
    def buf(name, shape, where=mem, side=None):
        return where.enter_context(nc.sbuf_tensor(f"gd_{name}", shape, F32, side=side))

    ident = t["mask"][:, MASKS["ident"], :]
    q, k = qkv[:, 0:4, :], qkv[:, 4:8, :]
    w = {"ktok": buf("ktok", [P, TT, GW * HV]), "vtok": buf("vtok", [P, TT, GW * HV]),
         "tok": buf("tok", [P, TT, P]), "kd": buf("kd", [P, TT, 64]), "nbg": buf("nbg", [P, TT, 64]),
         "ge": buf("ge", [P, GW, NC])}
    rows = buf("rows", [P, T])
    with ExitStack() as part:
        rest = buf("rest", [P, T], part)
        rtok = buf("rtok", [P, TT, P], part)
        gdn_rows(nc, t, p_ab, rows, rest, (w["tok"], rtok), w)
    to_tokens(nc, "gdn_tok", [([qkv[:, f0 + f, i * P:(i + 1) * P] for f in range(GW)], w[dst][:, i, :])
                              for f0, dst in ((4, "ktok"), (8, "vtok")) for i in range(TT)], ident)
    for d in range(2):
        with ExitStack() as own:
            w["qg"] = buf(f"qg{d}", [P, GW, T], own)
            w["attn"] = buf(f"attn{d}", [P, TT * GW, P], own)
            solve = ExitStack()
            w["lt"] = buf(f"lt{d}", [P, TT * GW, P], solve, "right")
            with ExitStack() as part:
                w["grow"] = buf(f"grow{d}", [P, GW, T], part)
                w["nkb"] = buf(f"nkb{d}", [P, GW, T], part)
                gdn_spread(nc, t, d, rows, q, k, w)
                gdn_grams(nc, t, d, q, k, w)
            w["xt"] = w["lt"]
            inverses(nc, t, f"gdn{d}_inv", w["lt"], w["xt"], [slice(a, a + 4) for a in range(0, TT * GW, 4)], d)
            w["wt"] = buf(f"wt{d}", [P, GW, T], own)
            w["u"] = buf(f"u{d}", [P, TT, GW * HV], own)
            gdn_solve(nc, d, w)
            solve.close()
            w["states"] = buf(f"states{d}", [P, NC, GW, HV], own)
            gdn_states(nc, d, w)
            gdn_outputs(nc, d, w, o)



D_FF = 2816
FH = D_FF // P // 2


def ffn(nc, t, name, layer, x, hh, hl, spans, conds, mods, gate0):
    base, tokens, ns = spans[0][0], sum(n for _, n in spans), len(spans)
    local = [(t0 - base, n) for t0, n in spans]
    for part in range(2):
        with ExitStack() as mem:
            ah = mem.enter_context(nc.sbuf_tensor(f"{name}_ah{part}", [P, FH * tokens], F32R))
            al = mem.enter_context(nc.sbuf_tensor(f"{name}_al{part}", [P, FH * tokens], F32R))
            with ExitStack() as up:
                tmp = up.enter_context(nc.sbuf_tensor(f"{name}_tmp{part}", [P, 2, tokens], F32))
                sil = up.enter_context(nc.sbuf_tensor(f"{name}_sil{part}", [P, tokens], F32))

                def make(st):
                    before_ok = st.sem("tap_before")
                    conv_ok = st.sem("conv")
                    silu_ok = st.sem("silu")
                    prod_ok = st.sem("product")
                    high_ok = st.sem("high")

                    def tap(k, i):
                        o = COL["ffn_conv_w_2"][0] + (layer * 3 + k) * 44 + part * 22
                        return t["cols"][:, bass.ds(i + o, 1)]

                    def pair(buf, i):
                        return buf[:, bass.ds(i * (tokens // 2) - tokens // 2, tokens)]

                    def evac_act(act, i, ps, slot):
                        act.wait_ge(st.banks_free, i + 2)
                        if slot == 1:
                            nc.scalar.activation(sil[:, :], tmp[:, 0, :], ACT.Silu).then_inc(silu_ok, 2)
                        for (t0, n), b in zip(local, ps):
                            ins = nc.scalar.activation(tmp[:, slot, t0:t0 + n], b[:, :n], ACT.Copy, scale=tap(1, i))
                        return ins

                    def evac_dve(dve, i, ps, slot):
                        for (t0, n), b in zip(local, ps):
                            out = tmp[:, slot, t0 + 1:t0 + n]
                            nc.vector.scalar_tensor_tensor(out, b[:, :n - 1], tap(0, i), out, ALU.mult, ALU.add
                                                           ).then_inc(before_ok, 1)
                        dve.wait_ge(before_ok, i * ns + ns)
                        for (t0, n), b in zip(local, ps):
                            out = tmp[:, slot, t0:t0 + n - 1]
                            ins = nc.vector.scalar_tensor_tensor(out, b[:, 1:n], tap(2, i), out, ALU.mult, ALU.add)
                            if slot == 1:
                                ins.then_inc(conv_ok, 2)
                        if slot == 0:
                            return ins
                        dve.wait_ge(conv_ok, i * ns + ns)
                        dve.wait_ge(silu_ok, i + 1)
                        nc.vector.tensor_tensor(tmp[:, 1, :], tmp[:, 1, :], sil[:, :], ALU.mult).then_inc(prod_ok, 2)
                        dve.wait_ge(prod_ok, i + 1)
                        nc.vector.tensor_copy(pair(ah, i), tmp[:, 1, :]).then_inc(high_ok, 2)
                        dve.wait_ge(high_ok, i + 1)
                        return nc.vector.tensor_tensor(pair(al, i), tmp[:, 1, :], pair(ah, i).bitcast(F32), ALU.subtract)
                    return evac_act, evac_dve
                dense(nc, f"{name}_up{part}", t["dram"]["ffn_up"], 2 * FH, KD, hh, hl, spans, evac=make,
                      first=layer * 4 * FH + part * 2 * FH)
            dense(nc, f"{name}_down{part}", t["dram"]["ffn_down"], KD, FH,
                  ah[:, :].rearrange("p (k t) -> p k t", k=FH), al[:, :].rearrange("p (k t) -> p k t", k=FH),
                  local, evac_dve=into_residual(nc, x, mods, gate0, conds), first=(layer * 2 + part) * KD)



HEADS, ROPE = 8, 64
SCALE = float((128 + ROPE) ** -0.5)


def rope_tables():
    n_freq = ROPE // 4
    inv = (np.float32(10000.0) ** (-np.arange(n_freq, dtype=np.float32) / np.float32(n_freq))).astype(np.float32)
    tok = np.arange(LAT)
    row, column = (tok // GRID).astype(np.float32), (tok % GRID).astype(np.float32)
    ang = np.concatenate([row[:, None] * inv, column[:, None] * inv], -1).astype(np.float32)
    table = np.stack([np.tile(f(ang).astype(np.float32).T, (4, 1)) for f in (np.cos, np.sin)], 1)
    half = ROPE // 2
    turn = np.zeros((P, P), np.float32)
    for m in range(P):
        turn[(m + half, m) if m % ROPE < half else (m - half, m)] = -1.0 if m % ROPE < half else 1.0
    return np.ascontiguousarray(table), turn


def rotate(nc, t, tiles):
    with Stage(nc, "rope") as st:
        table = st.sbuf("table", [P, 2, LAT])
        swap = st.sbuf("swap", [P, P])
        part = st.sbuf("part", [P, len(tiles), LAT])
        loaded = st.sem("loaded")
        swapped = st.sem("swapped")
        sin_ok = st.sem("sin")
        cos_ok = st.sem("cos")
        ps = st.banks("ps", 8)
        block = st.block()

        @block.sync
        def _(sp):
            sp.dma_start(table[:, :, :], t["dram"]["rope_table"]).then_inc(loaded, 16)
            sp.dma_start(swap[:, :], t["dram"]["rope_swap"]).then_inc(loaded, 16)
            sp.wait_ge(loaded, 32)

        @block.tensor
        def _(pe):
            pe.wait_ge(loaded, 32)
            for n, x in enumerate(tiles):
                nc.tensor.matmul(ps[n][:, :], swap[:, :], x, start=True, stop=True).then_inc(swapped, 1)

        @block.vector
        def _(dve):
            dve.wait_ge(loaded, 32)
            for n, x in enumerate(tiles):
                dve.wait_ge(swapped, n + 1)
                nc.vector.tensor_tensor(part[:, n, :], ps[n][:, :], table[:, 1, :], ALU.mult).then_inc(sin_ok, 1)
            for n, x in enumerate(tiles):
                dve.wait_ge(sin_ok, n + 1)
                dve.wait_ge(cos_ok, n + 1)
                nc.vector.tensor_tensor(x, x, part[:, n, :], ALU.add)

        @block.gpsimd
        def _(pool):
            pool.wait_ge(loaded, 32)
            for n, x in enumerate(tiles):
                pool.wait_ge(swapped, n + 1)
                nc.gpsimd.tensor_tensor(x, x, table[:, 0, :], ALU.mult).then_inc(cos_ok, 1)


def attention(nc, t, qn, qr, kn, kr, vtok, oh, ol):
    QT = LAT // P
    jobs = [(h, q) for h in range(HEADS) for q in range(QT)]
    ident = t["mask"][:, MASKS["ident"], :]
    with Stage(nc, "att") as st:
        p = st.sbuf("p", [P, 2, T])
        pt = [st.sbuf(f"pt{j}", [P, TT, LAT]) for j in range(2)]
        top = st.sbuf("top", [P, 2])
        neg = st.sbuf("neg", [P, 2])
        total = st.sbuf("total", [P, 2])
        inv = st.sbuf("inv", [P, 2])
        scores_ok = st.sem("scores")
        top_ok = st.sem("top")
        neg_ok = st.sem("neg")
        exp_ok = st.sem("exp")
        inv_ok = st.sem("inv")
        probs_ok = st.sem("probs")
        turned = [st.sem("turned0"), st.sem("turned1")]
        copied = [st.sem("copied_act"), st.sem("copied_dve")]
        mixed = st.sem("mixed")
        high = st.sem("high")
        low = st.sem("low")
        s_ps = [st.mem.enter_context(nc.psum_tensor(f"att_s{j}", [P, 1024], F32)) for j in range(2)]
        t_ps = st.banks("turned", 2)
        o_ps = st.banks("o", 2)
        block = st.block()

        @block.tensor
        def _(pe):
            def scores(n):
                h, q = jobs[n]
                if n >= 2:
                    pe.wait_ge(exp_ok, n - 1)
                tok, hp = slice(q * P, (q + 1) * P), slice(ROPE * (h % 2), ROPE * (h % 2) + ROPE)
                for k0, kn_ in ((0, 512), (512, T - 512)):
                    out = s_ps[n % 2][:, k0:k0 + kn_]
                    nc.tensor.matmul(out, qn[:, h, tok], kn[:, h, k0:k0 + kn_], start=True, stop=False)
                    done = nc.tensor.matmul(out, qr[hp, h // 2, tok], kr[hp, k0:k0 + kn_], start=False, stop=True)
                done.then_inc(scores_ok, 1)

            def product(h):
                for c in copied:
                    pe.wait_ge(c, QT * (h + 1))
                if h >= 2:
                    pe.wait_ge(low, h - 1)
                for i in range(TT):
                    done = nc.tensor.matmul(o_ps[h % 2][:, :], vtok[:, i, h * P:(h + 1) * P], pt[h % 2][:, i, :],
                                            start=i == 0, stop=i == TT - 1)
                done.then_inc(mixed, 1)

            scores(0)
            for n, (h, q) in enumerate(jobs):
                if n + 1 < len(jobs):
                    scores(n + 1)
                if q == 0 and h:
                    product(h - 1)
                pe.wait_ge(probs_ok, n + 1)
                for b in range(2):
                    if n:
                        pe.wait_ge(copied[b], n)
                    for i in range(3):
                        k0 = (3 * b + i) * P
                        done = nc.tensor.transpose(t_ps[b][:, i * P:(i + 1) * P], p[:, n % 2, k0:k0 + P], ident)
                    done.then_inc(turned[b], 1)
            product(HEADS - 1)

        @block.scalar
        def _(act):
            def exponential(n):
                act.wait_ge(neg_ok, n + 1)
                if n >= 2:
                    act.wait_ge(turned[1], n - 1)
                nc.scalar.activation(p[:, n % 2, :], s_ps[n % 2][:, :T], ACT.Exp, scale=SCALE,
                                     bias=neg[:, n % 2:n % 2 + 1], accum_out=total[:, n % 2:n % 2 + 1]
                                     ).then_inc(exp_ok, 1)

            def high_part(h):
                act.wait_ge(mixed, h + 1)
                nc.scalar.activation(oh[:, h, :], o_ps[h % 2][:, :], ACT.Copy).then_inc(high, 1)

            exponential(0)
            for n, (h, q) in enumerate(jobs):
                if n + 1 < len(jobs):
                    exponential(n + 1)
                act.wait_ge(turned[0], n + 1)
                if h >= 2:
                    act.wait_ge(mixed, h - 1)
                nc.scalar.activation(pt[h % 2][:, 0:3, q * P:(q + 1) * P],
                                     t_ps[0][:, :3 * P].rearrange("p (i t) -> p i t", i=3), ACT.Copy).then_inc(copied[0], 1)
                if q == 0 and h:
                    high_part(h - 1)
            high_part(HEADS - 1)

        @block.vector
        def _(dve):
            def maximum(n):
                dve.wait_ge(scores_ok, n + 1)
                if n >= 2:
                    dve.wait_ge(exp_ok, n - 1)
                j = slice(n % 2, n % 2 + 1)
                nc.vector.tensor_reduce(top[:, j], s_ps[n % 2][:, :T], AX.X, ALU.max).then_inc(top_ok, 1)
                dve.wait_ge(top_ok, n + 1)
                nc.vector.tensor_scalar(neg[:, j], top[:, j], -SCALE, None, ALU.mult).then_inc(neg_ok, 1)

            def low_part(h):
                dve.wait_ge(high, h + 1)
                nc.vector.tensor_tensor(ol[:, h, :], o_ps[h % 2][:, :], oh[:, h, :].bitcast(F32), ALU.subtract
                                        ).then_inc(low, 1)

            maximum(0)
            for n, (h, q) in enumerate(jobs):
                j = slice(n % 2, n % 2 + 1)
                dve.wait_ge(exp_ok, n + 1)
                nc.vector.reciprocal(inv[:, j], total[:, j]).then_inc(inv_ok, 1)
                dve.wait_ge(inv_ok, n + 1)
                nc.vector.tensor_scalar(p[:, n % 2, :], p[:, n % 2, :], inv[:, j], None, ALU.mult).then_inc(probs_ok, 1)
                if n + 1 < len(jobs):
                    maximum(n + 1)
                dve.wait_ge(turned[1], n + 1)
                if h >= 2:
                    dve.wait_ge(mixed, h - 1)
                nc.vector.tensor_copy(pt[h % 2][:, 3:6, q * P:(q + 1) * P],
                                      t_ps[1][:, :3 * P].rearrange("p (i t) -> p i t", i=3)).then_inc(copied[1], 1)
                if q == 0 and h:
                    low_part(h - 1)
            low_part(HEADS - 1)



def clear(nc, name, ap):
    with Stage(nc, name) as st:
        block = st.block()

        @block.gpsimd
        def _(pool):
            nc.gpsimd.memset(ap, 0.0)


def constant(nc, name, value, where):
    c = where.enter_context(nc.sbuf_tensor(name, [P, P], F32))
    with Stage(nc, f"{name}_fill") as st:
        block = st.block()

        @block.vector
        def _(dve):
            nc.vector.memset(c[:, :], value)
    return c


def activated(nc, dst, func, spans, shift=0):
    def evac_act(act, i, ps, slot):
        for (t0, n), b in zip(spans, ps):
            ins = nc.scalar.activation(dst[:, bass.ds(i + shift, 1), t0:t0 + n], b[:, :n], func)
        return ins
    return evac_act


def rms_mod(nc, t, name, x, spans, mods, o, hh, hl):
    conds = [1 if t0 < CTX else 0 for t0, _ in spans]
    normed(nc, name, x, KD, spans, t["over_d"], 1e-6, False,
           [lambda k, j=j: mods[:, o + KD + k, j:j + 1] for j in conds],
           [lambda k, j=j: mods[:, o + k, j:j + 1] for j in conds], hh, hl)


A_U, A_V, A_QKV, A_GATE, A_AB = 0, 4, 8, 20, 24


def second(nc, d, t, out, x_dram, keep, probe):
    both = ((0, CTX, 1), (CTX, LAT, 0))
    gains1, gains2 = cols_of(t, "norm1_g_2"), cols_of(t, "norm2_g_2")
    with ExitStack() as mem:
        mods = keep("mods2", [P, 96, 2], where=mem)
        gemv_mods(nc, "ada", d["ada_w"], 96, KD, t["cond"][:, 1], cols_of(t, "ada_b_2"), mods)
        modulation(nc, t, "mods2", 0, (8, 32, 56, 80),
                   (gains1[:, :KD], gains2[:, :KD], gains1[:, KD:], gains2[:, KD:]))
        branches, tall = ExitStack(), ExitStack()
        y_a = keep("y_a", [P, GW, T], where=branches, side="right")
        o = keep("o_gdn", [P, GW, T], where=branches, side="right")
        hidden = ExitStack()
        hh = keep("h2_h", [P, KD, T], F32R, where=hidden)
        hl = keep("h2_l", [P, KD, T], F32R, where=hidden)
        with ExitStack() as part:
            x2 = keep("x_a", [P, KD, T], where=part)
            load(nc, "load_xa", [(x2[:, :, :CTX], d["ctx_2"]), (x2[:, :, CTX:], x_dram[:, :, CTX:])])
            rms_mod(nc, t, "rms_a", x2, SEGS, mods, 0, hh, hl)
        with ExitStack() as part:
            a_u = keep("a_u", [P, GW, T], where=part)
            a_v = keep("a_v", [P, GW, T], where=part)
            vtok = keep("a_vtok", [P, TT, GW * P], where=part)
            dense(nc, "a_u_mm", d["ab_w"], 4, KD, hh, hl, SEGS, first=A_U, evac_act=activated(nc, a_u, ACT.Gelu, SEGS))
            dense(nc, "a_v_mm", d["ab_w"], 4, KD, hh, hl, SEGS, first=A_V, evac_act=activated(nc, a_v, ACT.Gelu, SEGS))
            over = constant(nc, "over_512", 1.0 / 512, part)
            normed(nc, "a_ln", a_v, GW, SEGS, over, 1e-6, True, [lambda k: col(t, "a_ln_g_2", k)] * 2,
                   [lambda k: col(t, "a_ln_b_2", k)] * 2, None, None, out=a_v)
            to_tokens(nc, "a_tok", [([a_v[:, f, i * P:(i + 1) * P] for f in range(GW)], vtok[:, i, :])
                                    for i in range(TT)], t["mask"][:, MASKS["ident"], :])
            gmlp(nc, t, a_u, vtok, y_a)
        gate_dram = nc.dram_tensor("b_gate_kept", (P, GW, T), F32, kind="Internal").ap()
        with ExitStack() as part:
            gate = keep("b_gate", [P, GW, T], where=part)
            dense(nc, "b_gate_mm", d["ab_w"], 4, KD, hh, hl, SEGS, first=A_GATE,
                  evac_act=activated(nc, gate, ACT.Silu, SEGS))
            load(nc, "b_gate_store", [(gate_dram, gate[:, :, :])])
        qkv = keep("qkv", [P, 12, T], where=tall, side="right")
        p_ab = keep("p_ab", [P, 1, T], where=tall, side="right")
        dense(nc, "qkv_mm", d["ab_w"], 12, KD, hh, hl, SEGS, first=A_QKV,
              evac=three_taps(nc, t, "b_conv_w_2", 12, lambda i, t0, n: qkv[:, bass.ds(i, 1), t0:t0 + n], SEGS))
        dense(nc, "ab_mm", d["ab_w"], 1, KD, hh, hl, SEGS, first=A_AB, evac_act=activated(nc, p_ab, ACT.Copy, SEGS))
        hidden.close()
        if probe:
            probe("y_a", y_a[:, :, :])
        ones = constant(nc, "ones", 1.0, mem)
        with Stage(nc, "qkv_silu") as st:
            block = st.block()

            @block.scalar
            def _(act):
                nc.scalar.activation(qkv[:, :, :], qkv[:, :, :], ACT.Silu)
        unit_norm(nc, "qk_unit", qkv[:, 0:8, :], 8, SEGS, ones[:, :], 1.0, 1e-6,
                  lambda f: float(HV ** -0.5) if f < GW else 1.0)
        if probe:
            probe("qkv", qkv[:, :, :])
        with ExitStack() as part:
            gdn(nc, t, qkv, p_ab[:, 0, :], o, part)
        tall.close()
        unit_norm(nc, "o_rms", o, GW, SEGS, ones[:, :], 1.0 / HV, 1e-6, lambda f: col(t, "b_norm_g_2", 0))
        if probe:
            probe("o_gdn", o[:, :, :])
        x2 = keep("x_b", [P, KD, T], where=mem)
        load(nc, "load_xb", [(x2[:, :, :CTX], d["ctx_2"]), (x2[:, :, CTX:], x_dram[:, :, CTX:])])
        hh = keep("h_h", [P, KD, T], F32R, where=mem)
        hl = keep("h_l", [P, KD, T], F32R, where=mem)
        with ExitStack() as part:
            gate = keep("b_gate_back", [P, GW, T], where=part)
            load(nc, "b_gate_load", [(gate[:, :, :], gate_dram)])
            gated(nc, "mix2", [y_a[:, f, :] for f in range(GW)] + [o[:, f, :] for f in range(GW)],
                  [None] * GW + [gate[:, f, :] for f in range(GW)], hh, hl, T)
        dense(nc, "ab_out_mm", d["ab_w_out"], KD, KD, hh, hl, SEGS, evac_dve=into_residual(nc, x2, mods, 16, both))
        if probe:
            probe("x_ab", x2[:, :, :])
        branches.close()
        rms_mod(nc, t, "rms_f0", x2, SEGS, mods, 24, hh, hl)
        ffn(nc, t, "f0", 0, x2, hh, hl, SEGS, both, mods, 40)
        if probe:
            probe("x_f0", x2[:, :, :])

        rms_mod(nc, t, "rms_c", x2, SEGS, mods, 48, hh, hl)
        with ExitStack() as part:
            v = keep("c_vtok", [P, TT, HEADS * P], where=part)
            kn = keep("c_kn", [P, HEADS, T], where=part)
            kr = keep("c_kr", [P, 1, T], where=part)
            qn = keep("c_qn", [P, HEADS, LAT], where=part)
            qr = keep("c_qr", [P, HEADS // 2, LAT], where=part)
            with ExitStack() as low:
                cq = keep("c_cq", [P, 3, LAT], where=low)
                cq_h = keep("c_cq_h", [P, 3, LAT], F32R, where=low)
                cq_l = keep("c_cq_l", [P, 3, LAT], F32R, where=low)
                over = constant(nc, "over_384", 1.0 / 384, low)
                shifted = [(0, LAT)]

                def cq_out(act, i, ps, slot):
                    return nc.scalar.activation(cq[:, bass.ds(i, 1), :], ps[0][:, :], ACT.Copy)
                dense(nc, "cq_mm", d["mla_w"], 3, KD, hh, hl, LAT_ONLY, evac_act=cq_out)
                normed(nc, "cq_rms", cq, 3, shifted, over, 1e-6, False, [lambda k: col(t, "mla_q_norm_g_2", k)],
                       None, cq_h, cq_l)
                dense(nc, "qn_mm", d["mla_uq"], HEADS, 3, cq_h, cq_l, shifted, evac_act=activated(nc, qn, ACT.Copy, shifted))
                dense(nc, "qr_mm", d["mla_uq"], HEADS // 2, 3, cq_h, cq_l, shifted, first=HEADS,
                      evac_act=activated(nc, qr, ACT.Copy, shifted))
            with ExitStack() as low:
                ckv = keep("c_ckv", [P, 2, T], where=low)
                ckv_h = keep("c_ckv_h", [P, 2, T], F32R, where=low)
                ckv_l = keep("c_ckv_l", [P, 2, T], F32R, where=low)
                over = constant(nc, "over_256", 1.0 / 256, low)
                dense(nc, "ckv_mm", d["mla_w"], 2, KD, hh, hl, SEGS, first=3, evac_act=activated(nc, ckv, ACT.Copy, SEGS))
                dense(nc, "kr_mm", d["mla_w"], 1, KD, hh, hl, SEGS, first=5, evac_act=activated(nc, kr, ACT.Copy, SEGS))
                normed(nc, "ckv_rms", ckv, 2, SEGS, over, 1e-6, False, [lambda k: col(t, "mla_kv_norm_g_2", k)] * 2,
                       None, ckv_h, ckv_l)
                dense(nc, "kn_mm", d["mla_ukv"], HEADS, 2, ckv_h, ckv_l, SEGS, evac_act=activated(nc, kn, ACT.Copy, SEGS))
                with ExitStack() as turn:
                    vf = keep("c_vf", [P, 4, T], where=turn)
                    for half in range(2):
                        dense(nc, f"v_mm{half}", d["mla_ukv"], 4, 2, ckv_h, ckv_l, SEGS, first=HEADS + 4 * half,
                              evac_act=activated(nc, vf, ACT.Copy, SEGS))
                        to_tokens(nc, f"v_tok{half}", [([vf[:, f, i * P:(i + 1) * P] for f in range(4)],
                                                        v[:, i, half * 512:half * 512 + 512]) for i in range(TT)],
                                  t["mask"][:, MASKS["ident"], :])
            rotate(nc, t, [qr[:, f, :] for f in range(HEADS // 2)] + [kr[:, 0, CTX:]])
            attention(nc, t, qn, qr, kn, kr[:, 0, :], v, hh[:, :, :LAT], hl[:, :, :LAT])
        dense(nc, "c_out_mm", d["mla_w_out"], KD, KD, hh, hl, ((0, LAT),),
              evac_dve=into_residual(nc, x2, mods, 64, both[1:]))
        rms_mod(nc, t, "rms_f1", x2, LAT_ONLY, mods, 72, hh, hl)
        ffn(nc, t, "f1", 1, x2, hh, hl, LAT_ONLY, both[1:], mods, 88)
        normed(nc, "final", x2, KD, LAT_ONLY, t["over_d"], 1e-6, False, [lambda k: col(t, "final_g_2", k)],
               None, None, None, out=x2)
        load(nc, "store", [(out, x2[:, :, CTX:])])


def build(nc, d, out, probe=None):
    with ExitStack() as mem:
        t = setup(nc, d, mem)
        t["dram"] = d

        def keep(name, shape, dt=F32, where=mem, side=None):
            t[name] = where.enter_context(nc.sbuf_tensor(name, shape, dt, side=side))
            return t[name]

        x_dram = nc.dram_tensor("x_kept", (P, KD, T), F32, kind="Internal").ap()
        mods = keep("mods", [P, 24, 2])
        gemv_mods(nc, "mod", d["mod_w"], 24, KD, t["cond"][:, 0], cols_of(t, "mod_b"), mods)
        modulation(nc, t, "mods", 0, (8,))
        with ExitStack() as first:
            o_hgrn = keep("o_hgrn", [P, NR, LAT], where=first)
            hidden = ExitStack()
            hh = keep("hh", [P, KD, T], F32R, where=hidden)
            hl = keep("hl", [P, KD, T], F32R, where=hidden)
            with ExitStack() as part:
                x = keep("x_in", [P, KD, T], where=part)
                load(nc, "load_x", [(x[:, :, :CTX], d["ctx"]), (x[:, :, CTX:], d["x"])])
                normed(nc, "ln0", x, KD, SEGS, t["over_d"], 1e-5, True,
                       [lambda k, j=j: mods[:, 8 + k, j:j + 1] for j in (1, 0)],
                       [lambda k, j=j: mods[:, k, j:j + 1] for j in (1, 0)], hh, hl)
            with ExitStack() as part:
                p_hgrn = keep("p_hgrn", [P, 12, T], where=part)

                def copy_out(act, i, ps, slot):
                    for (t0, n), b in zip(SEGS, ps):
                        ins = nc.scalar.activation(p_hgrn[:, bass.ds(i, 1), t0:t0 + n], b[:, :n], ACT.Copy)
                    return ins
                dense(nc, "p_hgrn_mm", d["w_in"], 12, KD, hh, hl, SEGS, evac_act=copy_out, first=O_HGRN)
                hgrn(nc, t, p_hgrn, o_hgrn, part)
            pooled = keep("pooled", [P, 2, LAT], where=first, side="right")
            with ExitStack() as part:
                p_pool = keep("p_pool", [P, 2, POOL_ROWS, GRID + 2 * POOL_PAD], where=part)
                clear(nc, "pool_clear", p_pool[:, :, :, :])

                def pool_out(act, i, ps, slot):
                    return nc.scalar.activation(
                        p_pool[:, bass.ds(i, 1), :, POOL_PAD:POOL_PAD + GRID].rearrange("p a r c -> p (a r) c"),
                        ps[0][:, :].rearrange("p (r c) -> p r c", c=GRID), ACT.Copy)
                dense(nc, "pool_mm", d["w_in"], 2, KD, hh, hl, LAT_ONLY, evac_act=pool_out, first=O_POOL)
                pool_branch(nc, t, p_pool, pooled)

            gate_dram = nc.dram_tensor("gate_kept", (P, KD, LAT), F32, kind="Internal").ap()
            with ExitStack() as part:
                gate = keep("gate", [P, KD, LAT], where=part)

                def gate_out(act, i, ps, slot):
                    return nc.scalar.activation(gate[:, bass.ds(i, 1), :], ps[0][:, :], ACT.Silu)
                dense(nc, "gate_mm", d["w_in"], KD, KD, hh, hl, LAT_ONLY, evac_act=gate_out, first=O_GATE)
                load(nc, "gate_store", [(gate_dram, gate[:, :, :])])
            u = keep("u", [P, N_RWKV_IN, T], where=first, side="right")
            dense(nc, "u_mm", d["w_in"], N_RWKV_IN, KD, hh, hl, SEGS, first=O_RWKV,
                  evac=three_taps(nc, t, "rwkv_shift", N_RWKV_IN,
                                  lambda i, t0, n: u[:, bass.ds(i, 1), t0:t0 + n], SEGS))
            hidden.close()
            y = keep("y_rwkv", [P, NR, LAT], where=first)
            with ExitStack() as part:
                rwkv(nc, t, u, y, part)
            hh = keep("mix_h", [P, KD, LAT], F32R, where=first)
            hl = keep("mix_l", [P, KD, LAT], F32R, where=first)
            if probe:
                probe("pooled", pooled[:, :, :])
            parts = [pooled[:, f, :] for f in range(2)] + [y[:, f, :] for f in range(NR)] + \
                [o_hgrn[:, f, :] for f in range(NR)]
            gate = keep("gate_back", [P, KD, LAT], where=first)
            load(nc, "gate_load", [(gate[:, :, :], gate_dram)])
            gated(nc, "mix", parts, [gate[:, k, :] for k in range(KD)], hh, hl, LAT)
            x2 = keep("x2", [P, KD, T], where=first)
            load(nc, "load_x2", [(x2[:, :, CTX:], d["x"])])
            scaled(nc, "alpha_x", x2[:, :, CTX:], x2[:, :, CTX:], ALPHA)
            dense(nc, "w_out_mm", d["w_out"], KD, KD, hh, hl, ((0, LAT),),
                  evac_dve=into_residual(nc, x2, mods, 16, [(CTX, LAT, 0)]))
            normed(nc, "ln1", x2, KD, LAT_ONLY, t["over_d"], 1e-5, True,
                   [lambda k: col(t, "ln_g", k)], [lambda k: col(t, "ln_b", k)], None, None, out=x2)
            if probe:
                probe("x_mid", x2[:, :, CTX:])
            load(nc, "x_store", [(x_dram[:, :, CTX:], x2[:, :, CTX:])])
        second(nc, d, t, out, x_dram, keep, probe)


def kernel(**inputs):
    import concourse.bacc as bacc
    from concourse.bass_utils import run_bass_kernel_spmd

    arrays = lay_out(inputs)
    nc = bacc.Bacc("TRN2", target_bir_lowering=False, num_devices=1)
    dram = {name: nc.dram_tensor(f"in_{name}", a.shape, mybir.dt.from_np(a.dtype), kind="ExternalInput").ap()
            for name, a in arrays.items()}
    out = nc.dram_tensor("out_y", (P, KD, LAT), F32, kind="ExternalOutput").ap()
    build(nc, dram, out)
    r = run_bass_kernel_spmd(nc, [{f"in_{k}": v for k, v in arrays.items()}], core_ids=[0])
    y = r.results[0]["out_y"]
    return np.ascontiguousarray(y.transpose(2, 1, 0).reshape(1, LAT, D))
```

```python
from contextlib import ExitStack

import numpy as np

import concourse.bass as bass
from concourse import mybir

F32 = mybir.dt.float32
F32R = mybir.dt.float32r
ALU = mybir.AluOpType
ACT = mybir.ActivationFunctionType
AX = mybir.AxisListType

P = 128
D = 1024
KD = D // P
CTX, LAT = 256, 512
T = CTX + LAT
SEGS = ((0, CTX), (CTX, LAT))
LAT_ONLY = ((CTX, LAT),)
TT = T // P
CT = CTX // P


class Stage:

    def __init__(self, nc, name):
        self.nc, self.name = nc, name
        self.mem, self.sems, self.credits = ExitStack(), [], None

    def __enter__(self):
        return self

    def sem(self, name):
        s = self.nc.alloc_semaphore(f"{self.name}_{name}")
        self.sems.append(s)
        return s

    def sbuf(self, name, shape, dt=F32):
        return self.mem.enter_context(self.nc.sbuf_tensor(f"{self.name}_{name}", shape, dt))

    def banks(self, name, n):
        return [self.mem.enter_context(self.nc.psum_tensor(f"{self.name}_{name}{i}", [P, 512], F32))
                for i in range(n)]

    def block(self):
        return self.mem.enter_context(self.nc.Block())

    def __exit__(self, *exc):
        self.mem.close()
        if exc[0] is None:
            self.nc.clear_and_free_semaphores(self.sems)
            self.nc.all_engine_barrier()
        return False


def tile_loop(eng, n, body, ahead=1):
    turns = max(n - ahead, 0) // 2
    if turns > 1:
        with eng.Fori(0, turns) as t:
            body(2 * t, 0, False)
            body(2 * t + 1, 1, False)
    else:
        for i in range(2 * turns):
            body(i, i % 2, False)
    for i in range(2 * turns, n):
        body(i, i % 2, i + ahead >= n)


def open_clock(nc, lhs, rhs, bank, n):
    for _ in range(n):
        nc.tensor.matmul(bank[:, :rhs.shape[-1]], lhs, rhs, start=True, stop=True)


def dense(nc, name, w_tiles, n_tiles, kt, xh, xl, spans, evac_act=None, evac_dve=None, first=0, evac=None,
          side=None, warm=None, also=()):
    st = Stage(nc, name)
    ns = len(spans)
    if evac is not None:
        evac_act, evac_dve = evac(st)
    w_loaded = [st.sem(f"w_loaded{j}") for j in range(2)]
    w_high = st.sem("w_high")
    w_low = st.sem("w_low")
    tile_done = st.sem("tile_done")
    act_done = st.sem("act_done")
    banks_free = st.banks_free = st.sem("banks_free")
    with st:
        stage = st.sbuf("stage", [P, 2, kt * P])
        wh = st.sbuf("wh", [P, 2, kt * P], F32R)
        wl = st.sbuf("wl", [P, 2, kt * P], F32R)
        ps = st.banks("ps", 2 * ns)
        if side:
            side.place(st)
        if warm:
            warmed = st.sbuf("warmed", [P, 1])
        moved = st.sem("moved")
        block = st.block()

        @block.sync
        def _(sp):
            def load(i, slot, last):
                sp.wait_ge(w_low, i + 1)
                sp.dma_start(stage[:, slot, :], w_tiles[bass.ds(first + i, 1)].rearrange("a p f -> p (a f)")
                             ).then_inc(w_loaded[slot], 16)
                if side:
                    side.load(sp, i, slot)
            if side:
                side.load_vec(sp)
            tile_loop(sp, n_tiles, load)
            for dst, src in also:
                sp.dma_start(dst, src).then_inc(moved, 16)
            if also:
                sp.wait_ge(moved, 16 * len(also))

        @block.gpsimd
        def _(pool):
            pool.sem_inc(w_low, 2)

            def low(i, slot, last):
                pool.wait_ge(w_high, i + 1)
                nc.gpsimd.tensor_tensor(wl[:, slot, :], stage[:, slot, :], wh[:, slot, :].bitcast(F32),
                                        ALU.subtract).then_inc(w_low, 1)
            tile_loop(pool, n_tiles, low)

        @block.scalar
        def _(act):
            def high(i, slot):
                act.wait_ge(w_loaded[slot], 8 * i + (16 if slot == 0 else 8))
                act.wait_ge(tile_done, i + 1)
                nc.scalar.activation(wh[:, slot, :], stage[:, slot, :], ACT.Copy).then_inc(w_high, 1)

            high(0, 0)
            if n_tiles > 1:
                high(1, 1)
            if side:
                side.silu(nc, act)
            if warm:
                nc.scalar.activation(warmed[:, :], xh[:, 0, spans[0][0]:spans[0][0] + 1].bitcast(F32), warm)

            def step(i, slot, last):
                if not last:
                    high(i + 2, slot)
                if evac_act is not None:
                    act.wait_ge(tile_done, i + 3)
                    ins = evac_act(act, i, ps[slot * ns:slot * ns + ns], slot)
                    ins.then_inc(act_done if evac_dve is not None else banks_free, 1)
            if evac_act is not None and evac_dve is None:
                act.sem_inc(banks_free, 2)
            if evac is not None and st.credits is not None:
                st.credits(act)
            tile_loop(act, n_tiles, step, ahead=2)

        @block.vector
        def _(dve):
            if evac_dve is None and side is None:
                return
            if evac_dve is not None:
                dve.sem_inc(banks_free, 2)
            if side:
                dve.sem_inc(side.used, 2)
                dve.sem_inc(side.summed, 2)
                dve.wait_ge(side.vec_ok, 1)

            def step(i, slot, last):
                if side:
                    side.sums(nc, dve, i, slot)
                if evac_dve is None:
                    return
                if evac_act is None:
                    dve.wait_ge(tile_done, i + 3)
                else:
                    dve.wait_ge(act_done, i + 1)
                ins = evac_dve(dve, i, ps[slot * ns:slot * ns + ns], slot)
                if ins is not None:
                    ins.then_inc(banks_free, 1)
            tile_loop(dve, n_tiles, step)

        @block.tensor
        def _(pe):
            pe.sem_inc(tile_done, 2)
            t0, n = spans[-1]
            open_clock(nc, xh[:, 0, t0:t0 + P], xh[:, 0, t0:t0 + n], ps[-1], 12)

            def products(i, slot, last):
                pe.wait_ge(w_low, i + 3)
                pe.wait_ge(banks_free, i + 1)
                for s, (t0, n) in enumerate(spans):
                    out = ps[slot * ns + s][:, :n]
                    for k in range(kt):
                        w_hi = wh[:, slot, k * P:(k + 1) * P]
                        w_lo = wl[:, slot, k * P:(k + 1) * P]
                        nc.tensor.matmul(out, w_hi, xh[:, k, t0:t0 + n], start=k == 0, stop=False)
                        nc.tensor.matmul(out, w_hi, xl[:, k, t0:t0 + n], start=False, stop=False)
                        done = nc.tensor.matmul(out, w_lo, xh[:, k, t0:t0 + n], start=False, stop=k == kt - 1)
                done.then_inc(tile_done, 1)
            tile_loop(pe, n_tiles, products)




def three_taps(nc, t, name, per_tap, dst, spans, shift=0):
    def make(st):
        before_ok = st.sem("tap_before")

        def tap(k, i):
            return t["cols"][:, bass.ds(COL[name][0] + k * per_tap + shift + i, 1)]

        def evac_act(act, i, ps, slot):
            for (t0, n), b in zip(spans, ps):
                ins = nc.scalar.activation(dst(i, t0, n), b[:, :n], ACT.Copy, scale=tap(1, i))
            return ins

        def evac_dve(dve, i, ps, slot):
            for (t0, n), b in zip(spans, ps):
                out = dst(i, t0 + 1, n - 1)
                nc.vector.scalar_tensor_tensor(out, b[:, :n - 1], tap(0, i), out, ALU.mult, ALU.add
                                               ).then_inc(before_ok, 1)
            dve.wait_ge(before_ok, len(spans) * i + len(spans))
            for (t0, n), b in zip(spans, ps):
                out = dst(i, t0, n - 1)
                ins = nc.vector.scalar_tensor_tensor(out, b[:, 1:n], tap(2, i), out, ALU.mult, ALU.add)
            return ins
        return evac_act, evac_dve
    return make


class Chain:

    def __init__(self, eng, sem):
        self.eng, self.sem, self.n = eng, sem, 0

    def __call__(self, ins):
        self.n += 1
        ins.then_inc(self.sem, 1)
        self.eng.wait_ge(self.sem, self.n)


def spread(ap, at, n):
    shape = list(ap.shape)
    shape.insert(at, n)
    return ap.unsqueeze(at).to_broadcast(shape)


EPS = (1e-5, 1e-6, 1e-12, 64e-5)


def eps_col(t, eps):
    i = EPS.index(eps)
    return t["eps"][:, i:i + 1]


def normed(nc, t, name, x, kt, spans, ones, eps, center, scale, shift, xh, xl, out=None, also=(), store=None):
    st = Stage(nc, name)
    parts = [(s, t0 + a, min(256, n - a)) for s, (t0, n) in enumerate(spans) for a in range(0, n, 256)]
    np_, x = len(parts), x[:, :kt, :]
    centered = st.sem("centered")
    squared = st.sem("squared")
    mean = st.sem("mean")
    var = st.sem("var")
    root = st.sem("root")
    rstd_ok = st.sem("rstd")
    xn_ok = st.sem("xn")
    high = st.sem("high")
    full = st.sem("full")
    low = st.sem("low")
    moved = st.sem("moved")
    with st:
        xc = st.sbuf("xc", [P, kt, T])
        sq = st.sbuf("sq", [P, 2, kt, 256])
        rs = st.sbuf("rs", [P, np_, 256])
        rstd = st.sbuf("rstd", [P, np_, 256])
        mps = st.banks("mean", np_ if center else 0)
        vps = st.banks("var", np_)
        block = st.block()

        @block.sync
        def _(sp):
            for dst, src in also:
                sp.dma_start(dst, src).then_inc(moved, 16)
            if store:
                for j, (s, t0, n) in enumerate(parts):
                    sp.wait_ge(full, kt * (j + 1))
                    sp.dma_start(store(t0, n), out[:, :, t0:t0 + n]).then_inc(moved, 16)
            if also or store:
                sp.wait_ge(moved, 16 * (len(also) + (np_ if store else 0)))

        @block.tensor
        def _(pe):
            if center:
                for j, (s, t0, n) in enumerate(parts):
                    for k in range(kt):
                        done = nc.tensor.matmul(mps[j][:, :n], ones[:, :], x[:, k, t0:t0 + n],
                                                start=k == 0, stop=k == kt - 1)
                    done.then_inc(mean, 1)
            for j, (s, t0, n) in enumerate(parts):
                pe.wait_ge(squared, j + 1)
                for k in range(kt):
                    done = nc.tensor.matmul(vps[j][:, :n], ones[:, :], sq[:, j % 2, k, :n],
                                            start=k == 0, stop=k == kt - 1)
                done.then_inc(var, 1)

        @block.scalar
        def _(act):
            def square(j):
                s, t0, n = parts[j]
                if center:
                    act.wait_ge(centered, j + 1)
                if j >= 2:
                    act.wait_ge(var, j - 1)
                src = xc if center else x
                nc.scalar.activation(sq[:, j % 2, :, :n], src[:, :, t0:t0 + n], ACT.Square).then_inc(squared, 1)

            def high_part(j):
                s, t0, n = parts[j]
                act.wait_ge(xn_ok, j + 1)
                for k in range(kt):
                    nc.scalar.activation(xh[:, k, t0:t0 + n], xc[:, k, t0:t0 + n], ACT.Identity,
                                         scale=scale[s](k), bias=shift[s](k) if shift else 0.0
                                         ).then_inc(high, 1)

            for j in range(min(2, np_)):
                square(j)
            for j, (s, t0, n) in enumerate(parts):
                act.wait_ge(var, j + 1)
                nc.scalar.activation(rs[:, j, :n], vps[j][:, :n], ACT.Sqrt, bias=eps_col(t, eps)).then_inc(root, 1)
                if j + 2 < np_:
                    square(j + 2)
                if out is None and j:
                    high_part(j - 1)
            if out is None:
                high_part(np_ - 1)

        @block.vector
        def _(dve):
            def center_part(j):
                s, t0, n = parts[j]
                dve.wait_ge(mean, j + 1)
                nc.vector.tensor_tensor(xc[:, :, t0:t0 + n], x[:, :, t0:t0 + n],
                                        spread(mps[j][:, :n], 1, kt), ALU.subtract).then_inc(centered, 1)
            if center:
                for j in range(np_):
                    center_part(j)
                dve.wait_ge(centered, np_)

            def normalise(j):
                s, t0, n = parts[j]
                dve.wait_ge(root, j + 1)
                nc.vector.reciprocal(rstd[:, j, :n], rs[:, j, :n]).then_inc(rstd_ok, 1)
                dve.wait_ge(rstd_ok, j + 1)
                src = xc if center else x
                nc.vector.tensor_tensor(xc[:, :, t0:t0 + n], src[:, :, t0:t0 + n],
                                        spread(rstd[:, j, :n], 1, kt), ALU.mult).then_inc(xn_ok, 1)

            normalise(0)
            for j, (s, t0, n) in enumerate(parts):
                if j + 1 < np_:
                    normalise(j + 1)
                dve.wait_ge(xn_ok, j + 1)
                for k in range(kt):
                    dst = xc if out is None else out
                    if out is None:
                        dve.wait_ge(high, j * kt + k + 1)
                    if shift:
                        ins = nc.vector.tensor_scalar(dst[:, k, t0:t0 + n], xc[:, k, t0:t0 + n],
                                                      scale[s](k), shift[s](k), ALU.mult, ALU.add)
                    else:
                        ins = nc.vector.tensor_scalar(dst[:, k, t0:t0 + n], xc[:, k, t0:t0 + n],
                                                      scale[s](k), None, ALU.mult)
                    ins.then_inc(full, 1)

        @block.gpsimd
        def _(pool):
            if out is None:
                for j, (s, t0, n) in enumerate(parts):
                    pool.wait_ge(full, j * kt + kt)
                    nc.gpsimd.tensor_tensor(xl[:, :, t0:t0 + n], xc[:, :, t0:t0 + n],
                                            xh[:, :, t0:t0 + n].bitcast(F32), ALU.subtract).then_inc(low, 1)


class Gemv:

    def __init__(self, w, vec, mods, first, per):
        self.w, self.vec, self.mods, self.first, self.per = w, vec, mods, first, per

    def place(self, st):
        self.rows = st.sbuf("side_w", [P, 2, self.per, D])
        self.conds = st.sbuf("side_vec", [P, 2, D])
        self.junk = st.sbuf("side_junk", [P, 2, D])
        self.summed = st.sem("side_summed")
        self.loaded = [st.sem(f"side_loaded{j}") for j in range(2)]
        self.vec_loaded = st.sem("side_vec_loaded")
        self.vec_ok = st.sem("side_vec")
        self.used = st.sem("side_used")

    def load_vec(self, sp):
        sp.dma_start(self.conds[:, :, :], self.vec.partition_broadcast(P)).then_inc(self.vec_loaded, 16)

    def load(self, sp, i, slot):
        sp.wait_ge(self.used, i + 1)
        sp.dma_start(self.rows[:, slot], self.w[bass.ds(i * self.per + self.first, self.per)].rearrange("a p f -> p a f")
                     ).then_inc(self.loaded[slot], 16)

    def silu(self, nc, act):
        act.wait_ge(self.vec_loaded, 16)
        nc.scalar.activation(self.conds[:, :, :], self.conds[:, :, :], ACT.Silu).then_inc(self.vec_ok, 1)

    def sums(self, nc, dve, i, slot):
        dve.wait_ge(self.loaded[slot], 8 * i + (16 if slot == 0 else 8))
        for g in range(self.per):
            for j in range(2):
                dve.wait_ge(self.summed, i * (2 * self.per) + 2 * g + j + 1)
                out = self.mods[:, bass.ds(i * self.per + self.first + g, 1), j:j + 1].rearrange("p a j -> p (a j)")
                nc.vector.scalar_tensor_tensor(self.junk[:, j, :], self.rows[:, slot, g, :], 1.0, self.conds[:, j, :],
                                               ALU.mult, ALU.mult, accum_out=out).then_inc(self.summed, 1)
        dve.wait_ge(self.summed, i * (2 * self.per) + 2 * self.per + 2)
        dve.sem_inc(self.used, 1)


def gemv_mods(nc, name, w, n_tiles, vec, mods, also=(), group=2):
    by_pool = [i for i in range(n_tiles) if i % 3 == 2]
    by_dve = [i for i in range(n_tiles) if i % 3 != 2]
    with Stage(nc, name) as st:
        rows = st.sbuf("w", [P, n_tiles // group, group, D])
        conds = st.sbuf("vec", [P, 2, D])
        junk = [st.sbuf(f"junk{j}", [P, 2, D]) for j in range(2)]
        summed = [st.sem(f"summed{j}") for j in range(2)]
        multiplied = st.sem("multiplied")
        vec_loaded = st.sem("vec_loaded")
        loaded = [st.sem(f"loaded{a}") for a in range(n_tiles // group)]
        moved = st.sem("moved")
        vec_ok = st.sem("vec")
        block = st.block()
        assert n_tiles % group == 0

        @block.sync
        def _(sp):
            sp.dma_start(conds[:, :, :], vec.partition_broadcast(P)).then_inc(vec_loaded, 16)
            for a in range(n_tiles // group):
                sp.dma_start(rows[:, a], w[group * a:group * a + group].rearrange("a p f -> p a f")).then_inc(loaded[a], 16)
            for dst, src in also:
                sp.dma_start(dst, src).then_inc(moved, 16)
            if also:
                sp.wait_ge(moved, 16 * len(also))

        @block.scalar
        def _(act):
            act.wait_ge(vec_loaded, 16)
            nc.scalar.activation(conds[:, :, :], conds[:, :, :], ACT.Silu).then_inc(vec_ok, 1)
            for n, i in enumerate(by_pool):
                for j in range(2):
                    act.wait_ge(multiplied, 2 * n + j + 1)
                    nc.scalar.activation(junk[1][:, j, :], junk[1][:, j, :], ACT.Copy, accum_out=mods[:, i, j:j + 1]
                                         ).then_inc(summed[1], 1)

        @block.vector
        def _(dve):
            dve.wait_ge(vec_ok, 1)
            for n, i in enumerate(by_dve):
                dve.wait_ge(loaded[i // group], 16)
                for j in range(2):
                    if n:
                        dve.wait_ge(summed[0], 2 * n + j - 1)
                    nc.vector.scalar_tensor_tensor(junk[0][:, j, :], rows[:, i // group, i % group, :], 1.0, conds[:, j, :],
                                                   ALU.mult, ALU.mult, accum_out=mods[:, i, j:j + 1]
                                                   ).then_inc(summed[0], 1)

        @block.gpsimd
        def _(pool):
            pool.wait_ge(vec_ok, 1)
            for n, i in enumerate(by_pool):
                pool.wait_ge(loaded[i // group], 16)
                for j in range(2):
                    if n:
                        pool.wait_ge(summed[1], 2 * n + j - 1)
                    nc.gpsimd.tensor_tensor(junk[1][:, j, :], rows[:, i // group, i % group, :], conds[:, j, :], ALU.mult
                                            ).then_inc(multiplied, 1)



def tiles_of(w, n):
    k = w.shape[0]
    return np.ascontiguousarray(
        w[:, :n].reshape(k // P, P, n // P, P).transpose(2, 1, 0, 3).reshape(n // P, P, k))


def columns(v):
    v = np.asarray(v, np.float32).reshape(-1, P)
    return v.T


D_POOL, D_RWKV, D_HGRN = 256, 384, 384
NR = D_RWKV // P
N_RWKV_IN = 11
HD = 64
C = 64
NC = T // C
CC = CTX // C
O_POOL, O_RWKV, O_HGRN, O_GATE = 0, 2, 13, 25


def masks():
    j, t = np.arange(P)[:, None], np.arange(P)[None, :]
    same = j // C == t // C
    m = {"ident": (j == t), "heads": j // HD == t // HD,
         "strict0": same & (j < t), "strict1": same & (j > t),
         "incl0": same & (j <= t), "incl1": same & (j >= t)}
    for lv in range(6):
        s = 1 << lv
        half = (j // (2 * s) == t // (2 * s)) & (j // s != t // s)
        m[f"level{lv}_0"] = half & (j < t)
        m[f"level{lv}_1"] = half & (j > t)
    return m


MASKS = {name: i for i, name in enumerate(masks())}

PACKED = (
    ("mod_b", 24), ("ada_b_2", 96),
    ("rwkv_shift", 33), ("rwkv_w0", 6), ("rwkv_a0", 6), ("rwkv_k_k", 3), ("rwkv_k_a", 3), ("rwkv_r_k", 6),
    ("rwkv_gn_g", 3), ("rwkv_gn_b", 3), ("hgrn_lb_logits", 6), ("hgrn_norm_g", 3), ("pool_scale", 2),
    ("ln_g", KD), ("ln_b", KD), ("norm1_g_2", 16), ("norm2_g_2", 16), ("a_ln_g_2", 4), ("a_ln_b_2", 4),
    ("b_conv_w_2", 36), ("b_norm_g_2", 1), ("mla_q_norm_g_2", 3), ("mla_kv_norm_g_2", 2),
    ("ffn_conv_w_2", 264), ("final_g_2", KD),
)
COL = {}
for _name, _n in PACKED:
    COL[_name] = (sum(n for _, n in PACKED[:len(COL)]), _n)
N_COLS = sum(n for _, n in PACKED)

def lay_out(inputs):
    g = {k: np.asarray(v) for k, v in inputs.items()}
    g["ffn_conv_w_2"] = pairs_of(g["ffn_conv_w_2"])
    arrays = {
        "x": np.ascontiguousarray(g["x"][0].T.reshape(KD, P, LAT).transpose(1, 0, 2)),
        "ctx": np.ascontiguousarray(g["ctx"][0].T.reshape(KD, P, CTX).transpose(1, 0, 2)),
        "ctx_2": np.ascontiguousarray(g["ctx_2"][0].T.reshape(KD, P, CTX).transpose(1, 0, 2)),
        "columns": np.ascontiguousarray(np.concatenate([columns(g[name]) for name, _ in PACKED], 1)),
        "masks": np.ascontiguousarray(np.stack([m.astype(np.float32) for m in masks().values()], 1)),
        "mod_w": rows_of(g["mod_w"][0]),
        "vec_1": np.stack([g["c"][0], g["c_ctx"]]), "vec_2": np.stack([g["c_2"][0], g["c_ctx_2"]]),
        "w_up": g["rwkv_w_up"].reshape(P, D_RWKV), "a_up": g["rwkv_a_up"].reshape(P, D_RWKV),
        "pool_w": np.ascontiguousarray(g["pool_w"].reshape(2, P, 64).transpose(1, 0, 2)),
        "pool_counts": pool_counts(),
        "w_out": tiles_of(g["w_out"][0], D),
        "w_in": tiles_of(g["w_in"][0], 4224),
    }
    arrays.update(lay_out_second(g))
    assert arrays["columns"].shape == (P, N_COLS)
    return arrays


def rows_of(w):
    return np.ascontiguousarray(w.T).reshape(-1, P, w.shape[0])


def pairs_of(w):
    v = w.reshape(w.shape[:-1] + (2, -1, P))
    return np.ascontiguousarray(np.moveaxis(v, -3, -2)).reshape(w.shape)


def lay_out_second(g):
    w = g["ab_w_in_2"][0]
    raw = w[:, 3072:3088].reshape(D, 2, 2, 4)
    ab = np.zeros((D, 4, 32), np.float32)
    ab[:, :, :4] = raw.reshape(D, 4, 4)
    rows = np.zeros((P, 2), np.float32)
    for d in range(2):
        rows[32 * d:32 * d + 4, 0] = g["b_a_log_2"][0, d]
        rows[32 * d:32 * d + 4, 1] = g["b_dt_bias_2"][0, d]
    w_mla, w_uq, w_ukv = g["mla_w_in_2"][0], g["mla_w_uq_2"][0].reshape(384, 8, 192), \
        g["mla_w_ukv_2"][0].reshape(256, 8, 256)
    table, swap = rope_tables()
    down = g["ffn_w_down_2"]
    return {
        "ada_w": np.concatenate([rows_of(g["ada_w_2"][i]) for i in range(2)]),
        "ab_w": tiles_of(np.concatenate([w[:, :3072], ab.reshape(D, P)], 1), 25 * P),
        "gdn_rows": rows,
        "a_ws": np.ascontiguousarray(g["a_ws_2"][0].transpose(2, 0, 1)),
        "a_bs": g["a_bs_2"][0],
        "ab_w_out": tiles_of(g["ab_w_out_2"][0], D),
        "mla_w": tiles_of(np.concatenate([w_mla, w_mla[:, 640:]], 1), 6 * P),
        "mla_uq": tiles_of(np.concatenate([w_uq[..., :128].reshape(384, -1), w_uq[..., 128:].reshape(384, -1)], 1), 12 * P),
        "mla_ukv": tiles_of(np.concatenate([w_ukv[..., :128].reshape(256, -1), w_ukv[..., 128:].reshape(256, -1)], 1), 16 * P),
        "mla_w_out": tiles_of(g["mla_w_out_2"][0], D),
        "rope_table": table, "rope_swap": swap,
        "ffn_up": np.concatenate([tiles_of(pairs_of(g["ffn_w_up_2"][i]), 44 * P) for i in range(2)]),
        "ffn_down": np.concatenate([tiles_of(down[i, h * 1408:(h + 1) * 1408], D) for i in range(2) for h in range(2)]),
    }


def setup(nc, d, mem):
    t = {}

    def keep(name, shape, dt=F32):
        t[name] = mem.enter_context(nc.sbuf_tensor(name, shape, dt))
        return t[name]

    cols = keep("cols", [P, N_COLS])
    mask = keep("mask", [P, len(MASKS), P])
    eps = keep("eps", [P, len(EPS)])
    over_d = keep("over_d", [P, P])
    turn = keep("turn", [P, T])
    with Stage(nc, "setup") as st:
        loaded = st.sem("loaded")
        ready = st.sem("ready")
        block = st.block()

        @block.sync
        def _(sp):
            sp.dma_start(cols[:, :], d["columns"]).then_inc(loaded, 16)
            sp.dma_start(mask[:, :, :], d["masks"]).then_inc(loaded, 16)
            sp.wait_ge(loaded, 32)

        @block.vector
        def _(dve):
            nc.vector.memset(over_d[:, :], 1.0 / D).then_inc(ready, 1)
            nc.vector.memset(turn[:, :], 1.0).then_inc(ready, 1)
            for i, value in enumerate(EPS):
                nc.vector.memset(eps[:, i:i + 1], value)
            dve.wait_ge(ready, 2)
            nc.vector.memset(turn[:, :].rearrange("p (c t) -> p c t", t=C)[:, :, 0:1], 0.0)
    return t


def col(t, name, i):
    o, n = COL[name]
    assert i < n
    return t["cols"][:, o + i:o + i + 1]


def open_clock_with(nc, t, bank, n, columns=512):
    open_clock(nc, t["mask"][:, MASKS["ident"], :], t["turn"][:, :columns], bank, n)


def cols_of(t, name):
    o, n = COL[name]
    return t["cols"][:, o:o + n]


def modulation(nc, t, name, tile0, bias, scale_tiles, gains=()):
    mods = t[name]
    n_tiles = bias.shape[1]
    with Stage(nc, f"{name}_scale{tile0}") as st:
        chain_sem = st.sem("own")
        block = st.block()

        @block.vector
        def _(dve):
            own = Chain(dve, chain_sem)
            every = mods[:, tile0:tile0 + n_tiles, :]
            own(nc.vector.tensor_tensor(every, every, spread(bias, 2, 2), ALU.add))
            for n, s0 in enumerate(scale_tiles):
                part = mods[:, s0:s0 + KD, :]
                own(nc.vector.tensor_scalar(part, part, 1.0, None, ALU.add))
                if gains:
                    own(nc.vector.tensor_tensor(part, part, spread(gains[n], 2, 2), ALU.mult))


def load(nc, name, pairs):
    with Stage(nc, name) as st:
        loaded = st.sem("loaded")
        block = st.block()

        @block.sync
        def _(sp):
            for out, src in pairs:
                sp.dma_start(out, src).then_inc(loaded, 16)
            sp.wait_ge(loaded, 16 * len(pairs))





def chunk_order(d):
    return [*range(CC), *range(CC, NC)] if d == 0 else [*range(CC - 1, -1, -1), *range(NC - 1, CC - 1, -1)]


def to_tokens(nc, name, jobs, ident):
    with Stage(nc, name) as st:
        turned = st.sem("turned")
        read = [st.sem("read_act"), st.sem("read_dve")]
        ps = st.banks("ps", 4)
        block = st.block()

        @block.tensor
        def _(pe):
            for j, (sources, _) in enumerate(jobs):
                if j >= 4:
                    pe.wait_ge(read[j % 2], (j - 4) // 2 + 1)
                for f, src in enumerate(sources):
                    done = nc.tensor.transpose(ps[j % 4][:, f * P:(f + 1) * P], src, ident)
                done.then_inc(turned, 1)

        def read_out(eng, j, copy):
            sources, out = jobs[j]
            eng.wait_ge(turned, j + 1)
            copy(out, ps[j % 4][:, :len(sources) * P]).then_inc(read[j % 2], 1)

        @block.scalar
        def _(act):
            for j in range(0, len(jobs), 2):
                read_out(act, j, lambda o, i: nc.scalar.activation(o, i, ACT.Copy))

        @block.vector
        def _(dve):
            for j in range(1, len(jobs), 2):
                read_out(dve, j, lambda o, i: nc.vector.tensor_copy(o, i))



def seg(ap, s):
    t0, n = SEGS[s]
    return ap[:, :, t0:t0 + n]


def later_half(ap, d, s):
    v = ap.rearrange("p f (b h s) -> p (f b) h s", h=2, s=s)
    return v[:, :, 1 - d, :], v[:, :, d, :]


def hgrn_prepare(nc, t, d, p, w):
    with Stage(nc, f"hgrn{d}_prep") as st:
        z = p[:, 6 + 3 * d:9 + 3 * d, :]
        absz = st.sbuf("absz", [P, NR, T])
        soft = st.sbuf("soft", [P, NR, T])
        logf = st.sbuf("logf", [P, NR, T])
        g = [st.sbuf("g0", [P, NR, CTX]), w["g"]]
        e_qg = st.sbuf("e_qg", [P, NR, LAT])
        soft_ok = st.sem("softplus")
        logf_ok = st.sem("logf")
        lk_ok = st.sem("log_k")
        k_ok = st.sem("k")
        q_ok = st.sem("q")
        g_ok = st.sem("g")
        rest_ok = st.sem("rest")
        exp_ok = st.sem("exp")
        own = st.sem("own")
        block = st.block()

        @block.scalar
        def _(act):
            chain = Chain(act, own)
            chain(nc.scalar.activation(absz[:, :, :], z, ACT.Abs))
            chain(nc.scalar.activation(absz[:, :, :], absz[:, :, :], ACT.Exp, scale=-1.0))
            nc.scalar.activation(soft[:, :, :], absz[:, :, :], ACT.Ln, bias=1.0).then_inc(soft_ok, 1)
            if d == 0:
                nc.scalar.activation(w["q"][:, :, :], seg(p[:, 0:NR, :], 1), ACT.Copy).then_inc(q_ok, 1)
            for s in range(2):
                act.wait_ge(lk_ok, s + 1)
                nc.scalar.activation(w["k"][s][:, :, :], seg(absz, s), ACT.Exp).then_inc(k_ok, 1)
            for s in range(2):
                act.wait_ge(rest_ok, s + 1)
                nc.scalar.activation(seg(soft, s), seg(soft, s), ACT.Exp).then_inc(exp_ok, 1)
                ends = g[s][:, :, :].rearrange("p f (c t) -> p f c t", t=C)[:, :, :, (0 if d else C - 1)]
                c0, cn = SEGS[s][0] // C, SEGS[s][1] // C
                nc.scalar.activation(w["end"][:, :, c0:c0 + cn], ends, ACT.Exp)
            nc.scalar.activation(e_qg[:, :, :], g[1][:, :, :], ACT.Exp).then_inc(exp_ok, 1)

        @block.vector
        def _(dve):
            dve.wait_ge(soft_ok, 1)
            nc.vector.scalar_tensor_tensor(logf[:, :, :], z, 0.0, soft[:, :, :], ALU.min, ALU.subtract
                                           ).then_inc(logf_ok, 1)
            dve.wait_ge(logf_ok, 1)
            for s in range(2):
                nc.vector.tensor_tensor(seg(absz, s), seg(logf, s), seg(z, s), ALU.subtract).then_inc(lk_ok, 1)
            for s, (t0, n) in enumerate(SEGS):
                for f in range(NR):
                    src, dst = logf[:, f, t0:t0 + n], g[s][:, f, :]
                    if d:
                        src, dst = src[:, ::-1], dst[:, ::-1]
                    nc.vector.tensor_tensor_scan(dst, t["turn"][:, :n], src, 0.0, ALU.mult, ALU.add
                                                 ).then_inc(g_ok, 1)
            for s, (t0, n) in enumerate(SEGS):
                dve.wait_ge(g_ok, NR * (s + 1))
                for f in range(NR):
                    gv = g[s][:, f, :].rearrange("p (c t) -> p c t", t=C)
                    end = gv[:, :, (0 if d else C - 1)]
                    ins = nc.vector.tensor_tensor(soft[:, f, t0:t0 + n].rearrange("p (c t) -> p c t", t=C),
                                                  spread(end, 2, C), gv, ALU.subtract)
                ins.then_inc(rest_ok, 1)
            dve.wait_ge(k_ok, 2)
            for s in range(2):
                dve.wait_ge(exp_ok, s + 1)
                nc.vector.tensor_tensor(w["kh"][s][:, :, :], w["k"][s][:, :, :], seg(soft, s), ALU.mult)
            if d == 0:
                dve.wait_ge(q_ok, 1)
            dve.wait_ge(exp_ok, 3)
            nc.vector.tensor_tensor(w["qg"][:, :, :], w["q"][:, :, :], e_qg[:, :, :], ALU.mult)


def half(h):
    return slice(HD * (h % 2), HD * (h % 2) + HD)


def score_groups():
    return [[(i, 2 * f + parity) for f, i in pairs]
            for pairs in ([(f, i) for i in range(LAT // P)] for f in range(NR)) for parity in range(2)]


SCORE_AT = {tile: 4 * b + a for b, group in enumerate(score_groups()) for a, tile in enumerate(group)}


def hgrn_scores(nc, t, d, w):
    groups = score_groups()
    ng = len(groups)
    levels = list(range(6)) + ["diagonal"]
    scores, g = w["scores"], w["g"]
    with Stage(nc, f"hgrn{d}_scores") as st:
        diff = st.sbuf("diff", [P, 2, NR, LAT])
        e_lv = st.sbuf("e_lv", [P, 2, NR, LAT])
        ops = st.sbuf("ops", [P, 2, NR, LAT])
        diff_ok = st.sem("diff")
        elv_ok = st.sem("level_exp")
        hq_ok = st.sem("level_q")
        hk_ok = st.sem("level_k")
        cleared = st.sem("cleared")
        product = st.sem("product")
        picked = st.sem("picked")
        ps = st.banks("ps", 6)
        spare = st.banks("spare", 1)[0]
        block = st.block()

        @block.scalar
        def _(act):
            for lv in range(6):
                act.wait_ge(diff_ok, lv + 1)
                if lv >= 2:
                    act.wait_ge(hq_ok, lv - 1)
                    act.wait_ge(hk_ok, lv - 1)
                later, earlier = later_half(e_lv[:, lv % 2], d, 1 << lv)
                dl, de = later_half(diff[:, lv % 2], d, 1 << lv)
                nc.scalar.activation(later, dl, ACT.Exp).then_inc(elv_ok, 1)
                nc.scalar.activation(earlier, de, ACT.Exp, scale=-1.0).then_inc(elv_ok, 1)

        @block.gpsimd
        def _(pool):
            nc.gpsimd.memset(scores[:, :, :], 0.0).then_inc(cleared, 1)
            for lv in range(6):
                pool.wait_ge(elv_ok, 2 * lv + 2)
                if lv >= 2:
                    pool.wait_ge(product, ng * (lv - 1))
                _, earlier = later_half(ops[:, lv % 2], d, 1 << lv)
                _, k = later_half(w["k"][1][:, :, :], d, 1 << lv)
                _, e = later_half(e_lv[:, lv % 2], d, 1 << lv)
                nc.gpsimd.tensor_tensor(earlier, k, e, ALU.mult).then_inc(hk_ok, 1)

        @block.vector
        def _(dve):
            def difference(lv):
                s = 1 << lv
                v = g[:, :, :].rearrange("p f (b h s) -> p (f b) h s", h=2, s=s)
                border = v[:, :, d, (0 if d else s - 1)]
                if lv >= 2:
                    dve.wait_ge(elv_ok, 2 * lv - 2)
                nc.vector.tensor_tensor(
                    diff[:, lv % 2].rearrange("p f (b e) -> p (f b) e", e=2 * s),
                    g[:, :, :].rearrange("p f (b e) -> p (f b) e", e=2 * s),
                    spread(border, 2, 2 * s), ALU.subtract).then_inc(diff_ok, 1)

            def queries(lv):
                dve.wait_ge(elv_ok, 2 * lv + 1)
                if lv >= 2:
                    dve.wait_ge(product, ng * (lv - 1))
                later, _ = later_half(ops[:, lv % 2], d, 1 << lv)
                q, _ = later_half(w["q"][:, :, :], d, 1 << lv)
                e, _ = later_half(e_lv[:, lv % 2], d, 1 << lv)
                nc.vector.tensor_tensor(later, q, e, ALU.mult).then_inc(hq_ok, 1)

            difference(0)
            difference(1)
            queries(0)
            dve.wait_ge(cleared, 1)
            for n, lv in enumerate(levels):
                if n + 1 < 6:
                    queries(n + 1)
                if n + 2 < 6:
                    difference(n + 2)
                m = MASKS["ident" if lv == "diagonal" else f"level{lv}_{d}"]
                for b in range(ng):
                    dve.wait_ge(product, ng * n + b + 1)
                    nc.vector.copy_predicated(
                        scores[:, 4 * b:4 * b + 4, :], spread(t["mask"][:, m, :], 1, 4).bitcast(mybir.dt.int32),
                        ps[b][:, :].rearrange("p (a t) -> p a t", t=P)).then_inc(picked, 1)

        @block.tensor
        def _(pe):
            open_clock_with(nc, t, ps[0], 8)
            for n, lv in enumerate(levels):
                if n:
                    open_clock_with(nc, t, spare, 2)
                if lv != "diagonal":
                    pe.wait_ge(hq_ok, lv + 1)
                    pe.wait_ge(hk_ok, lv + 1)
                left = w["k"][1] if lv == "diagonal" else ops[:, lv % 2]
                right = w["q"] if lv == "diagonal" else ops[:, lv % 2]
                for b in range(0, ng, 2):
                    if n:
                        pe.wait_ge(picked, ng * (n - 1) + b + 2)
                    for a in range(4):
                        for e in range(2):
                            i, h = groups[b + e][a]
                            tok = slice(i * P, (i + 1) * P)
                            done = nc.tensor.matmul(ps[b + e][:, a * P:(a + 1) * P], left[half(h), h // 2, tok],
                                                    right[half(h), h // 2, tok], start=True, stop=True)
                            if a == 3:
                                done.then_inc(product, 1)


def hgrn_states(nc, d, w, vt):
    with Stage(nc, f"hgrn{d}_states") as st:
        update = st.sem("update")
        added = st.sem("added")
        decayed = st.sem("decayed")
        tmp = st.sbuf("tmp", [P, NR, HD])
        ps = st.banks("ps", 4)
        block = st.block()
        order = chunk_order(d)
        states = w["states"]

        @block.tensor
        def _(pe):
            for n, c in enumerate(order[:-1]):
                if n >= 4:
                    pe.wait_ge(added, n - 3)
                tok = slice(C * (c % 2), C * (c % 2) + C)
                for h in range(6):
                    f = slice(HD * h, HD * h + HD)
                    done = nc.tensor.matmul(ps[n % 4][half(h), HD * (h // 2):HD * (h // 2) + HD],
                                            w["kht"][tok, c // 2, f], vt[tok, c // 2, f], start=True, stop=True)
                done.then_inc(update, 1)

        @block.vector
        def _(dve):
            nc.vector.memset(states[:, order[0]], 0.0).then_inc(decayed, 1)
            for n, c in enumerate(order[:-1]):
                dve.wait_ge(decayed, n + 1)
                if n:
                    dve.wait_ge(added, n)
                nc.vector.tensor_tensor(tmp[:, :, :], states[:, c], spread(w["end"][:, :, c], 2, HD), ALU.mult
                                        ).then_inc(decayed, 1)
                dve.wait_ge(decayed, n + 2)
                dve.wait_ge(update, n + 1)
                nc.vector.tensor_tensor(states[:, order[n + 1]], tmp[:, :, :],
                                        ps[n % 4][:, :NR * HD].rearrange("p (f v) -> p f v", v=HD), ALU.add
                                        ).then_inc(added, 1)


def hgrn_outputs(nc, d, w, vt, o):
    with Stage(nc, f"hgrn{d}_out") as st:
        summed = st.sem("summed")
        ps = st.banks("ps", NR)
        block = st.block()

        @block.tensor
        def _(pe):
            for f in range(NR):
                for i in range(LAT // P):
                    for h in (2 * f, 2 * f + 1):
                        hd = slice(HD * h, HD * h + HD)
                        nc.tensor.matmul(ps[f][half(h), i * P:(i + 1) * P], vt[:, CT + i, hd],
                                         w["scores"][:, SCORE_AT[i, h], :], start=True, stop=False)
                        for c in (2 * i, 2 * i + 1):
                            done = nc.tensor.matmul(ps[f][half(h), c * C:(c + 1) * C],
                                                    w["states"][half(h), CC + c, f, :],
                                                    w["qg"][half(h), f, c * C:(c + 1) * C],
                                                    start=False, stop=c % 2 == 1)
                done.then_inc(summed, 1)

        @block.vector
        def _(dve):
            for f in range(NR):
                dve.wait_ge(summed, f + 1)
                if d == 0:
                    nc.vector.tensor_copy(o[:, f, :], ps[f][:, :])
                else:
                    nc.vector.tensor_tensor(o[:, f, :], o[:, f, :], ps[f][:, :], ALU.add)


def head_rms(nc, t, o, gain):
    with Stage(nc, "hgrn_rms") as st:
        squared = st.sem("squared")
        mean = st.sem("mean")
        log_ok = st.sem("log")
        root = st.sem("root")
        gained = st.sem("gained")
        sq = st.sbuf("sq", [P, NR, LAT])
        ps = st.banks("ps", NR)
        block = st.block()

        @block.scalar
        def _(act):
            nc.scalar.activation(sq[:, :, :], o[:, :, :], ACT.Square).then_inc(squared, 1)
            act.wait_ge(mean, NR)
            for f in range(NR):
                nc.scalar.activation(sq[:, f, :], ps[f][:, :], ACT.Ln, scale=1.0 / HD, bias=eps_col(t, 1e-6)
                                     ).then_inc(log_ok, 1)
            act.wait_ge(log_ok, NR)
            nc.scalar.activation(sq[:, :, :], sq[:, :, :], ACT.Exp, scale=-0.5).then_inc(root, 1)

        @block.tensor
        def _(pe):
            pe.wait_ge(squared, 1)
            for f in range(NR):
                nc.tensor.matmul(ps[f][:, :], t["mask"][:, MASKS["heads"], :], sq[:, f, :],
                                 start=True, stop=True).then_inc(mean, 1)

        @block.vector
        def _(dve):
            dve.wait_ge(squared, 1)
            for f in range(NR):
                nc.vector.tensor_scalar(o[:, f, :], o[:, f, :], gain(f), None, ALU.mult).then_inc(gained, 1)
            dve.wait_ge(root, 1)
            dve.wait_ge(gained, NR)
            nc.vector.tensor_tensor(o[:, :, :], o[:, :, :], sq[:, :, :], ALU.mult)


def hgrn(nc, t, p, o, mem):
    def buf(name, shape):
        return mem.enter_context(nc.sbuf_tensor(f"hg_{name}", shape, F32))

    ident = t["mask"][:, MASKS["ident"], :]
    vt = buf("vt", [P, TT, D_HGRN])
    to_tokens(nc, "hgrn_vt", [([p[:, 3 + f, i * P:(i + 1) * P] for f in range(NR)], vt[:, i, :])
                              for i in range(TT)], ident)
    w = {
        "q": buf("q", [P, NR, LAT]),
        "k": [buf(f"k{s}", [P, NR, n]) for s, (_, n) in enumerate(SEGS)],
        "kh": [buf(f"kh{s}", [P, NR, n]) for s, (_, n) in enumerate(SEGS)],
        "qg": buf("qg", [P, NR, LAT]), "g": buf("g", [P, NR, LAT]), "end": buf("end", [P, NR, NC]),
    }
    for d in range(2):
        hgrn_prepare(nc, t, d, p, w)
        with ExitStack() as late:
            w["scores"] = late.enter_context(nc.sbuf_tensor(f"hg_scores_{d}", [P, 24, P], F32))
            hgrn_scores(nc, t, d, w)
            w["kht"] = late.enter_context(nc.sbuf_tensor(f"hg_kht_{d}", [P, TT, D_HGRN], F32))
            w["states"] = late.enter_context(nc.sbuf_tensor(f"hg_states_{d}", [P, NC, NR, HD], F32))
            tok = [(0, i) for i in range(CT)] + [(1, i) for i in range(LAT // P)]
            to_tokens(nc, f"hgrn{d}_kht",
                      [([w["kh"][s][:, f, i * P:(i + 1) * P] for f in range(NR)], w["kht"][:, n, :])
                       for n, (s, i) in enumerate(tok)], ident)
            hgrn_states(nc, d, w, vt)
            hgrn_outputs(nc, d, w, vt, o)
    head_rms(nc, t, o, lambda f: col(t, "hgrn_norm_g", f))



def inverses(nc, t, name, lt, xt, groups, d):
    g_slots = 3
    waves = [groups[a:a + g_slots] for a in range(0, len(groups), g_slots)]
    flat = [(w, lv, g) for w, wave in enumerate(waves) for lv in range(6) for g in range(len(wave))]
    at_mask = {key: n for n, key in enumerate(flat)}
    at_merge = {key: n for n, key in enumerate(k for k in flat if k[1] >= 1)}
    at_turn = {key: n for n, key in enumerate(k for k in flat if k[1] < 5)}
    at_init = {key[::2]: n for n, key in enumerate(k for k in flat if k[1] == 0)}
    ident = t["mask"][:, MASKS["ident"], :]
    with Stage(nc, name) as st:
        ct = st.sbuf("ct", [P, g_slots, 4, P])
        x = st.sbuf("x", [P, g_slots, 4, P])
        xs = st.sbuf("xs", [P, g_slots, 4, P])
        cx = st.sbuf("cx", [P, g_slots, 4, P])
        masked = st.sem("masked")
        first = st.sem("first")
        product1 = st.sem("product1")
        copied = st.sem("copied")
        product2 = st.sem("product2")
        added = st.sem("added")
        turned = st.sem("turned")
        kept = st.sem("kept")
        bank_a = st.banks("a", g_slots)
        bank_b = st.banks("b", g_slots)
        block = st.block()

        def four(bank):
            return bank[:, :].rearrange("p (a t) -> p a t", t=P)

        @block.gpsimd
        def _(pool):
            for w, lv, g in flat:
                if lv == 0 and w:
                    pool.wait_ge(product1, at_merge[w - 1, 5, g] + 1)
                if lv == 1:
                    pool.wait_ge(first, at_init[w, g] + 1)
                if lv >= 2:
                    pool.wait_ge(product1, at_merge[w, lv - 1, g] + 1)
                m = t["mask"][:, MASKS[f"level{lv}_{d}"], :]
                nc.gpsimd.tensor_tensor(ct[:, g], lt[:, waves[w][g], :], spread(m, 1, 4), ALU.mult
                                        ).then_inc(masked, 1)

        @block.vector
        def _(dve):
            for w, wave in enumerate(waves):
                for g in range(len(wave)):
                    dve.wait_ge(masked, at_mask[w, 0, g] + 1)
                    if w:
                        dve.wait_ge(added, at_merge[w - 1, 5, g] + 1)
                    nc.vector.tensor_tensor(xs[:, g], ct[:, g], spread(ident, 1, 4), ALU.add).then_inc(first, 1)
                for lv in range(1, 6):
                    for g in range(len(wave)):
                        dve.wait_ge(product2, at_merge[w, lv, g] + 1)
                        if lv < 5:
                            ins = nc.vector.tensor_tensor(x[:, g], x[:, g], four(bank_b[g]), ALU.add)
                        else:
                            ins = nc.vector.tensor_tensor(xt[:, wave[g], :], xs[:, g], four(bank_b[g]), ALU.add)
                        ins.then_inc(added, 1)

        @block.scalar
        def _(act):
            for w, wave in enumerate(waves):
                for g in range(len(wave)):
                    act.wait_ge(turned, at_turn[w, 0, g] + 1)
                    nc.scalar.activation(x[:, g], four(bank_a[g]), ACT.Copy).then_inc(kept, 1)
                for lv in range(1, 6):
                    for g in range(len(wave)):
                        act.wait_ge(product1, at_merge[w, lv, g] + 1)
                        nc.scalar.activation(cx[:, g], four(bank_a[g]), ACT.Copy).then_inc(copied, 1)
                    for g in range(len(wave)):
                        if lv < 5:
                            act.wait_ge(turned, at_turn[w, lv, g] + 1)
                            nc.scalar.activation(xs[:, g], four(bank_a[g]), ACT.Copy).then_inc(kept, 1)

        @block.tensor
        def _(pe):
            def turn(src, g):
                for a in range(4):
                    done = nc.tensor.transpose(bank_a[g][:, a * P:(a + 1) * P], src[:, g, a, :], ident)
                done.then_inc(turned, 1)

            for w, wave in enumerate(waves):
                for g in range(len(wave)):
                    pe.wait_ge(first, at_init[w, g] + 1)
                    turn(xs, g)
                for lv in range(1, 6):
                    for g in range(len(wave)):
                        pe.wait_ge(masked, at_mask[w, lv, g] + 1)
                        pe.wait_ge(kept, at_turn[w, lv - 1, g] + 1)
                        for a in range(4):
                            done = nc.tensor.matmul(bank_a[g][:, a * P:(a + 1) * P], ct[:, g, a, :],
                                                    x[:, g, a, :], start=True, stop=True)
                        done.then_inc(product1, 1)
                    for g in range(len(wave)):
                        pe.wait_ge(copied, at_merge[w, lv, g] + 1)
                        for a in range(4):
                            left, right = (xs, cx) if lv < 5 else (cx, xs)
                            done = nc.tensor.matmul(bank_b[g][:, a * P:(a + 1) * P], left[:, g, a, :],
                                                    right[:, g, a, :], start=True, stop=True)
                        done.then_inc(product2, 1)
                    for g in range(len(wave)):
                        if lv < 5:
                            pe.wait_ge(added, at_merge[w, lv, g] + 1)
                            turn(x, g)



DECAY = float(np.exp(-0.5))


def rwkv_common(nc, t, u, kk, th):
    with Stage(nc, "rwkv_common") as st:
        sq = st.sbuf("sq", [P, NR, T])
        scaled = st.sem("scaled")
        squared = st.sem("squared")
        summed = st.sem("summed")
        log_ok = st.sem("log")
        root = st.sem("root")
        ps = st.banks("ps", 2 * NR)
        block = st.block()

        @block.vector
        def _(dve):
            for f in range(NR):
                nc.vector.tensor_scalar(kk[:, f, :], u[:, 3 + f, :], col(t, "rwkv_k_k", f), None, ALU.mult
                                        ).then_inc(scaled, 1)
            dve.wait_ge(root, 1)
            dve.wait_ge(scaled, NR)
            nc.vector.tensor_tensor(kk[:, :, :], kk[:, :, :], sq[:, :, :], ALU.mult)

        @block.scalar
        def _(act):
            nc.scalar.activation(th[:, :], u[:, 9, :], ACT.Tanh)
            act.wait_ge(scaled, NR)
            nc.scalar.activation(sq[:, :, :], kk[:, :, :], ACT.Square).then_inc(squared, 1)
            act.wait_ge(summed, 2 * NR)
            for f in range(NR):
                for s, (t0, n) in enumerate(SEGS):
                    nc.scalar.activation(sq[:, f, t0:t0 + n], ps[2 * f + s][:, :n], ACT.Ln, bias=eps_col(t, 1e-12)
                                         ).then_inc(log_ok, 1)
            act.wait_ge(log_ok, 2 * NR)
            nc.scalar.activation(sq[:, :, :], sq[:, :, :], ACT.Exp, scale=-0.5).then_inc(root, 1)

        @block.tensor
        def _(pe):
            pe.wait_ge(squared, 1)
            for f in range(NR):
                for s, (t0, n) in enumerate(SEGS):
                    nc.tensor.matmul(ps[2 * f + s][:, :n], t["mask"][:, MASKS["heads"], :], sq[:, f, t0:t0 + n],
                                     start=True, stop=True).then_inc(summed, 1)


def rwkv_prepare(nc, t, d, u, w):
    with Stage(nc, f"rwkv{d}_prep") as st:
        sg = st.sbuf("sg", [P, NR, T])
        gs = st.sbuf("gs", [P, NR, T])
        a = st.sbuf("a", [P, NR, T])
        km = st.sbuf("km", [P, NR, T])
        inv, rest, incl = w["bt"], w["bh"], w["rt"]
        lora = st.sem("lora")
        gate_ok = st.sem("gate")
        scanned = st.sem("scanned")
        excl_ok = st.sem("exclusive")
        rest_ok = st.sem("rest")
        exp_ok = st.sem("exp")
        bn_ok = st.sem("bn")
        km_ok = st.sem("km")
        kh_ok = st.sem("kh")
        own = st.sem("own")
        ps = st.banks("ps", 8)
        block = st.block()
        jobs = [(wh, f, s) for wh in range(2) for f in range(NR) for s in range(2)]
        rank = slice(64 * d, 64 * d + 64)

        @block.tensor
        def _(pe):
            for n, (wh, f, s) in enumerate(jobs):
                t0, tn = SEGS[s]
                if n >= 8:
                    pe.wait_ge(gate_ok, n - 7)
                up = t["a_up" if wh else "w_up"][rank, f * P:(f + 1) * P]
                src = u[rank, 10, t0:t0 + tn] if wh else t["th"][rank, t0:t0 + tn]
                nc.tensor.matmul(ps[n % 8][:, :tn], up, src, start=True, stop=True).then_inc(lora, 1)

        @block.scalar
        def _(act):
            for n, (wh, f, s) in enumerate(jobs):
                t0, tn = SEGS[s]
                act.wait_ge(lora, n + 1)
                nc.scalar.activation((a if wh else sg)[:, f, t0:t0 + tn], ps[n % 8][:, :tn], ACT.Sigmoid,
                                     bias=col(t, "rwkv_a0" if wh else "rwkv_w0", 3 * d + f)).then_inc(gate_ok, 1)
            act.wait_ge(scanned, NR)
            nc.scalar.activation(inv[:, :, :], gs[:, :, :], ACT.Exp, scale=DECAY).then_inc(exp_ok, 1)
            act.wait_ge(excl_ok, 1)
            nc.scalar.activation(sg[:, :, :], sg[:, :, :], ACT.Exp, scale=-DECAY).then_inc(exp_ok, 1)
            act.wait_ge(rest_ok, 1)
            nc.scalar.activation(rest[:, :, :], rest[:, :, :], ACT.Exp, scale=-DECAY).then_inc(exp_ok, 1)
            nc.scalar.activation(incl[:, :, :], seg(gs, 1), ACT.Exp, scale=-DECAY).then_inc(exp_ok, 1)
            ends = gs[:, :, :].rearrange("p f (c t) -> p f c t", t=C)[:, :, :, (0 if d else C - 1)]
            nc.scalar.activation(w["end"][:, :, :], ends, ACT.Exp, scale=-DECAY)

        @block.vector
        def _(dve):
            chain = Chain(dve, own)
            chain(nc.vector.tensor_scalar(t["one_ka"][:, :], cols_of(t, "rwkv_k_a"), -1.0, 1.0, ALU.mult, ALU.add))
            dve.wait_ge(gate_ok, 2 * NR)
            for f in range(NR):
                src, dst = sg[:, f, :], gs[:, f, :]
                if d:
                    src, dst = src[:, ::-1], dst[:, ::-1]
                nc.vector.tensor_tensor_scan(dst, t["turn"][:, :], src, 0.0, ALU.mult, ALU.add).then_inc(scanned, 1)
            dve.wait_ge(scanned, NR)
            nc.vector.tensor_tensor(sg[:, :, :], gs[:, :, :], sg[:, :, :], ALU.subtract).then_inc(excl_ok, 1)
            for f in range(NR):
                gv = gs[:, f, :].rearrange("p (c t) -> p c t", t=C)
                ins = nc.vector.tensor_tensor(rest[:, f, :].rearrange("p (c t) -> p c t", t=C),
                                              spread(gv[:, :, (0 if d else C - 1)], 2, C), gv, ALU.subtract)
            ins.then_inc(rest_ok, 1)
            dve.wait_ge(gate_ok, 4 * NR)
            for f in range(NR):
                ins = nc.vector.tensor_scalar(km[:, f, :], a[:, f, :], col(t, "rwkv_k_a", f),
                                              t["one_ka"][:, f:f + 1], ALU.mult, ALU.add)
            chain(ins)
            nc.vector.tensor_tensor(km[:, :, :], km[:, :, :], u[:, 3:6, :], ALU.mult).then_inc(km_ok, 1)
            nc.vector.scalar_tensor_tensor(a[:, :, :], a[:, :, :], -1.0, w["kk"][:, :, :], ALU.mult, ALU.mult
                                           ).then_inc(bn_ok, 1)
            dve.wait_ge(km_ok, 1)
            dve.wait_ge(bn_ok, 1)
            for f in range(NR):
                rk = col(t, "rwkv_r_k", 3 * d + f)
                if d == 0:
                    nc.vector.tensor_scalar(w["bonus"][:, f, :], km[:, f, CTX:], rk, None, ALU.mult)
                else:
                    nc.vector.scalar_tensor_tensor(w["bonus"][:, f, :], km[:, f, CTX:], rk, w["bonus"][:, f, :],
                                                   ALU.mult, ALU.add)
            dve.wait_ge(exp_ok, 1)
            chain(nc.vector.tensor_tensor(w["kt"][:, :, :], km[:, :, :], inv[:, :, :], ALU.mult))
            nc.vector.tensor_tensor(w["bt"][:, :, :], a[:, :, :], inv[:, :, :], ALU.mult)
            dve.wait_ge(exp_ok, 2)
            nc.vector.tensor_tensor(w["at"][:, :, :], w["kk"][:, :, :], sg[:, :, :], ALU.mult)
            dve.wait_ge(exp_ok, 4)
            nc.vector.tensor_tensor(w["rt"][:, :, :], seg(u[:, 0:3, :], 1), incl[:, :, :], ALU.mult)

        @block.gpsimd
        def _(pool):
            pool.wait_ge(km_ok, 1)
            pool.wait_ge(bn_ok, 1)
            pool.wait_ge(exp_ok, 3)
            nc.gpsimd.tensor_tensor(w["kh"][:, :, :], km[:, :, :], rest[:, :, :], ALU.mult).then_inc(kh_ok, 1)
            pool.wait_ge(kh_ok, 1)
            nc.gpsimd.tensor_tensor(w["bh"][:, :, :], a[:, :, :], rest[:, :, :], ALU.mult)


RWKV_TILES = [(i, h) for i in range(TT) for h in range(6)]


def rwkv_grams(nc, t, d, w, y):
    with Stage(nc, f"rwkv{d}_grams") as st:
        gram = st.sem("gram")
        masked = st.sem("masked")
        used = st.sem("used")
        lkv_read = st.sem("lkv_read")
        lk = st.sbuf("lk", [P, 4, 2, P])
        ps = st.banks("g", 3)
        lps = st.banks("l", 2)
        yps = st.banks("y", NR)
        block = st.block()
        strict = t["mask"][:, MASKS[f"strict{d}"], :]
        incl = t["mask"][:, MASKS[f"incl{d}"], :]
        n_tiles = len(RWKV_TILES)

        @block.tensor
        def _(pe):
            def grams(n):
                i, h = RWKV_TILES[n]
                tok = slice(i * P, (i + 1) * P)
                f = h // 2
                if n >= 3:
                    pe.wait_ge(masked, n - 2)
                for e, left in enumerate((w["bt"], w["kt"])):
                    done = nc.tensor.matmul(ps[n % 3][:, e * P:(e + 1) * P], left[half(h), f, tok],
                                            w["at"][half(h), f, tok], start=True, stop=True)
                    if i >= CT:
                        lat = slice((i - CT) * P, (i - CT + 1) * P)
                        done = nc.tensor.matmul(ps[n % 3][:, (2 + e) * P:(3 + e) * P], left[half(h), f, tok],
                                                w["rt"][half(h), f, lat], start=True, stop=True)
                done.then_inc(gram, 1)

            def uses(n):
                i, h = RWKV_TILES[n]
                hd = slice(HD * h, HD * h + HD)
                pe.wait_ge(masked, n + 1)
                if h == 0 and i >= 2:
                    pe.wait_ge(lkv_read, i - 1)
                done = nc.tensor.matmul(lps[i % 2][:, hd], lk[:, n % 4, 0, :], w["vt"][:, i, hd],
                                        start=True, stop=True)
                if i >= CT:
                    done = nc.tensor.matmul(yps[h // 2][half(h), (i - CT) * P:(i - CT + 1) * P], w["vt"][:, i, hd],
                                            lk[:, n % 4, 1, :], start=True, stop=True)
                done.then_inc(used, 1)

            open_clock_with(nc, t, ps[2], 8)
            for n in range(n_tiles):
                grams(n)
                if n:
                    uses(n - 1)
            uses(n_tiles - 1)

        @block.vector
        def _(dve):
            for n, (i, h) in enumerate(RWKV_TILES):
                dve.wait_ge(gram, n + 1)
                if n >= 4:
                    dve.wait_ge(used, n - 3)
                bank = ps[n % 3]
                nc.vector.tensor_tensor(w["lt"][:, n, :], bank[:, 0:P], strict, ALU.mult)
                ins = nc.vector.tensor_tensor(lk[:, n % 4, 0, :], bank[:, P:2 * P], strict, ALU.mult)
                if i >= CT:
                    m = n - CT * 6
                    nc.vector.tensor_tensor(w["arb"][:, m, :], bank[:, 2 * P:3 * P], incl, ALU.mult)
                    ins = nc.vector.tensor_tensor(lk[:, n % 4, 1, :], bank[:, 3 * P:4 * P], incl, ALU.mult)
                ins.then_inc(masked, 1)
            dve.wait_ge(used, n_tiles)
            for f in range(NR):
                if d == 0:
                    nc.vector.tensor_copy(y[:, f, :], yps[f][:, :])
                else:
                    nc.vector.tensor_tensor(y[:, f, :], y[:, f, :], yps[f][:, :], ALU.add)

        @block.scalar
        def _(act):
            for i in range(TT):
                act.wait_ge(used, 6 * i + 6)
                nc.scalar.activation(w["lkv"][:, i, :], lps[i % 2][:, :D_RWKV], ACT.Copy).then_inc(lkv_read, 1)


def rwkv_solve(nc, d, w):
    with Stage(nc, f"rwkv{d}_solve") as st:
        m1_ok = st.sem("m1")
        m2_ok = st.sem("m2")
        m1_read = st.sem("m1_read")
        m2_read = st.sem("m2_read")
        a_ps = st.banks("a", 2)
        b_ps = st.banks("b", 2)
        block = st.block()

        @block.tensor
        def _(pe):
            for i in range(TT):
                if i >= 2:
                    pe.wait_ge(m1_read, i - 1)
                    pe.wait_ge(m2_read, i - 1)
                for h in range(6):
                    hd = slice(HD * h, HD * h + HD)
                    xt = w["xt"][:, 6 * i + h, :]
                    last1 = nc.tensor.matmul(a_ps[i % 2][half(h), (h // 2) * P:(h // 2 + 1) * P], w["att"][:, i, hd],
                                             xt, start=True, stop=True)
                    if h == 5:
                        last1.then_inc(m1_ok, 1)
                    last2 = nc.tensor.matmul(b_ps[i % 2][:, hd], xt, w["lkv"][:, i, hd], start=True, stop=True)
                last2.then_inc(m2_ok, 1)

        @block.scalar
        def _(act):
            for i in range(TT):
                act.wait_ge(m1_ok, i + 1)
                nc.scalar.activation(w["m1t"][:, :, i * P:(i + 1) * P],
                                     a_ps[i % 2][:, :NR * P].rearrange("p (f t) -> p f t", t=P), ACT.Copy
                                     ).then_inc(m1_read, 1)

        @block.vector
        def _(dve):
            for i in range(TT):
                dve.wait_ge(m2_ok, i + 1)
                nc.vector.tensor_copy(w["m2"][:, i, :], b_ps[i % 2][:, :D_RWKV]).then_inc(m2_read, 1)


def rwkv_states(nc, t, d, w):
    with Stage(nc, f"rwkv{d}_states") as st:
        sa_ps_ok = st.sem("sa_product")
        sa_ok = st.sem("sa")
        decayed = st.sem("decayed")
        update = st.sem("update")
        state_ok = st.sem("state")
        tmp = st.sbuf("tmp", [P, 2, NR, HD])
        even = st.banks("even", 2)
        odd = st.banks("odd", 2)
        ups = st.banks("up", 2)
        spare = st.banks("spare", 1)[0]
        block = st.block()
        order = chunk_order(d)
        states, sa = w["states"], w["sa"]

        @block.tensor
        def _(pe):
            open_clock_with(nc, t, spare, 8)
            for n, c in enumerate(order):
                tok, i = slice(C * (c % 2), C * (c % 2) + C), c // 2
                pe.wait_ge(state_ok, n + 1)
                for h in range(6):
                    bank = (even, odd)[h % 2][n % 2]
                    done = nc.tensor.matmul(bank[tok, HD * (h // 2):HD * (h // 2) + HD],
                                            w["m1t"][half(h), h // 2, c * C:(c + 1) * C],
                                            states[half(h), c, h // 2, :], start=True, stop=True)
                done.then_inc(sa_ps_ok, 1)
                open_clock_with(nc, t, spare, 2, 256)
                if n == NC - 1:
                    break
                pe.wait_ge(sa_ok, n + 1)
                for h in range(6):
                    hd = slice(HD * h, HD * h + HD)
                    out = ups[n % 2][half(h), HD * (h // 2):HD * (h // 2) + HD]
                    nc.tensor.matmul(out, w["kht"][tok, i, hd], w["vt"][tok, i, hd], start=True, stop=False)
                    done = nc.tensor.matmul(out, w["bht"][tok, i, hd], sa[tok, i, hd], start=False, stop=True)
                done.then_inc(update, 1)
                open_clock_with(nc, t, spare, 2, 256)

        @block.gpsimd
        def _(pool):
            for n, c in enumerate(order[:-1]):
                pool.wait_ge(state_ok, n + 1)
                nc.gpsimd.tensor_tensor(tmp[:, n % 2], states[:, c], spread(w["end"][:, :, c], 2, HD), ALU.mult
                                        ).then_inc(decayed, 1)

        @block.vector
        def _(dve):
            nc.vector.memset(states[:, order[0]], 0.0).then_inc(state_ok, 1)
            for n, c in enumerate(order):
                tok, i = slice(C * (c % 2), C * (c % 2) + C), c // 2
                dve.wait_ge(sa_ps_ok, n + 1)
                for e, bank in enumerate((even[n % 2], odd[n % 2])):
                    def pairs(ap):
                        return ap.rearrange("p (f e v) -> p f e v", e=2, v=HD)[:, :, e, :]
                    ins = nc.vector.tensor_tensor(pairs(sa[tok, i, :]), pairs(w["m2"][tok, i, :]),
                                                  bank[tok, :NR * HD].rearrange("p (f v) -> p f v", v=HD), ALU.add)
                ins.then_inc(sa_ok, 1)
                if n == NC - 1:
                    break
                dve.wait_ge(decayed, n + 1)
                dve.wait_ge(update, n + 1)
                nc.vector.tensor_tensor(states[:, order[n + 1]], tmp[:, n % 2],
                                        ups[n % 2][:, :NR * HD].rearrange("p (f v) -> p f v", v=HD), ALU.add
                                        ).then_inc(state_ok, 1)


def rwkv_outputs(nc, d, w, y):
    with Stage(nc, f"rwkv{d}_out") as st:
        summed = st.sem("summed")
        ps = st.banks("ps", NR)
        block = st.block()

        @block.tensor
        def _(pe):
            for f in range(NR):
                for i in range(LAT // P):
                    for h in (2 * f, 2 * f + 1):
                        hd = slice(HD * h, HD * h + HD)
                        nc.tensor.matmul(ps[f][half(h), i * P:(i + 1) * P], w["sa"][:, CT + i, hd],
                                         w["arb"][:, 6 * i + h, :], start=True, stop=False)
                        for c in (2 * i, 2 * i + 1):
                            done = nc.tensor.matmul(ps[f][half(h), c * C:(c + 1) * C],
                                                    w["states"][half(h), CC + c, f, :],
                                                    w["rt"][half(h), f, c * C:(c + 1) * C],
                                                    start=False, stop=c % 2 == 1)
                done.then_inc(summed, 1)

        @block.vector
        def _(dve):
            for f in range(NR):
                dve.wait_ge(summed, f + 1)
                nc.vector.tensor_tensor(y[:, f, :], y[:, f, :], ps[f][:, :], ALU.add)


def rwkv_readout(nc, t, u, bonus, y):
    with Stage(nc, "rwkv_readout") as st:
        sq = st.sbuf("sq", [P, NR, LAT])
        rb = st.sbuf("rb", [P, NR, LAT])
        mean_ok = st.sem("mean")
        rb_ok = st.sem("rb")
        centered = st.sem("centered")
        squared = st.sem("squared")
        var_ok = st.sem("var")
        sum_ok = st.sem("bonus_sum")
        log_ok = st.sem("log")
        root = st.sem("root")
        own = st.sem("own")
        mps = st.banks("m", 2)
        vps = st.banks("v", NR)
        bps = st.banks("b", NR)
        block = st.block()
        heads = t["mask"][:, MASKS["heads"], :]
        v = seg(u[:, 6:9, :], 1)

        @block.gpsimd
        def _(pool):
            nc.gpsimd.tensor_tensor(rb[:, :, :], bonus[:, :, :], seg(u[:, 0:3, :], 1), ALU.mult).then_inc(rb_ok, 1)

        @block.tensor
        def _(pe):
            for f in range(NR):
                if f == 2:
                    pe.wait_ge(centered, 1)
                nc.tensor.matmul(mps[f % 2][:, :], heads, y[:, f, :], start=True, stop=True).then_inc(mean_ok, 1)
            pe.wait_ge(rb_ok, 1)
            for f in range(NR):
                nc.tensor.matmul(bps[f][:, :], heads, rb[:, f, :], start=True, stop=True).then_inc(sum_ok, 1)
            pe.wait_ge(squared, 1)
            for f in range(NR):
                nc.tensor.matmul(vps[f][:, :], heads, sq[:, f, :], start=True, stop=True).then_inc(var_ok, 1)

        @block.scalar
        def _(act):
            act.wait_ge(centered, NR)
            nc.scalar.activation(sq[:, :, :], y[:, :, :], ACT.Square).then_inc(squared, 1)
            act.wait_ge(var_ok, NR)
            for f in range(NR):
                nc.scalar.activation(sq[:, f, :], vps[f][:, :], ACT.Ln, scale=1.0 / HD, bias=eps_col(t, 64e-5)
                                     ).then_inc(log_ok, 1)
            act.wait_ge(log_ok, NR)
            nc.scalar.activation(sq[:, :, :], sq[:, :, :], ACT.Exp, scale=-0.5).then_inc(root, 1)

        @block.vector
        def _(dve):
            chain = Chain(dve, own)
            for f in range(NR):
                dve.wait_ge(mean_ok, f + 1)
                nc.vector.scalar_tensor_tensor(y[:, f, :], mps[f % 2][:, :], -1.0 / HD, y[:, f, :],
                                               ALU.mult, ALU.add).then_inc(centered, 1)
            dve.wait_ge(centered, NR)
            for f in range(NR):
                dve.wait_ge(sum_ok, f + 1)
                ins = nc.vector.tensor_tensor(rb[:, f, :], bps[f][:, :], v[:, f, :], ALU.mult)
            chain(ins)
            dve.wait_ge(root, 1)
            chain(nc.vector.tensor_tensor(y[:, :, :], y[:, :, :], sq[:, :, :], ALU.mult))
            for f in range(NR):
                ins = nc.vector.tensor_scalar(y[:, f, :], y[:, f, :], col(t, "rwkv_gn_g", f), col(t, "rwkv_gn_b", f),
                                              ALU.mult, ALU.add)
            chain(ins)
            nc.vector.tensor_tensor(y[:, :, :], y[:, :, :], rb[:, :, :], ALU.add)


def rwkv(nc, t, u, y, mem):
    def buf(name, shape, where=mem):
        return where.enter_context(nc.sbuf_tensor(f"rw_{name}", shape, F32))

    ident = t["mask"][:, MASKS["ident"], :]
    t["th"] = buf("th", [P, T])
    t["one_ka"] = buf("one_ka", [P, NR])
    w = {"kk": buf("kk", [P, NR, T]), "bonus": buf("bonus", [P, NR, LAT]), "end": buf("end", [P, NR, NC]),
         "vt": buf("vt", [P, TT, D_RWKV])}
    rwkv_common(nc, t, u, w["kk"], t["th"])
    to_tokens(nc, "rwkv_vt", [([u[:, 6 + f, i * P:(i + 1) * P] for f in range(NR)], w["vt"][:, i, :])
                              for i in range(TT)], ident)
    for d in range(2):
        with ExitStack() as own:
            w["rt"] = buf(f"rt{d}", [P, NR, LAT], own)
            right = ExitStack()

            def right_buf(name, shape, stack):
                return stack.enter_context(nc.sbuf_tensor(f"rw_{name}{d}", shape, F32, side="right"))
            for name in ("kt", "bt", "at"):
                w[name] = right_buf(name, [P, NR, T], right)
            ends = ExitStack()
            for name in ("kh", "bh"):
                w[name] = right_buf(name, [P, NR, T], ends)
            rwkv_prepare(nc, t, d, u, w)
            for name in ("kht", "bht", "att"):
                w[name] = buf(f"{name}{d}", [P, TT, D_RWKV], own)
            to_tokens(nc, f"rwkv{d}_tok",
                      [([w[src][:, f, i * P:(i + 1) * P] for f in range(NR)], w[dst][:, i, :])
                       for src, dst in (("kh", "kht"), ("bh", "bht"), ("at", "att")) for i in range(TT)], ident)
            ends.close()
            w["lt"] = buf(f"lt{d}", [P, len(RWKV_TILES), P], own)
            w["arb"] = buf(f"arb{d}", [P, 24, P], own)
            w["lkv"] = buf(f"lkv{d}", [P, TT, D_RWKV], own)
            rwkv_grams(nc, t, d, w, y)
            right.close()
            w["xt"] = w["lt"]
            inverses(nc, t, f"rwkv{d}_inv", w["lt"], w["xt"], [slice(a, a + 4) for a in range(0, 36, 4)], d)
            w["m1t"] = buf(f"m1t{d}", [P, NR, T], own)
            w["m2"] = buf(f"m2{d}", [P, TT, D_RWKV], own)
            rwkv_solve(nc, d, w)
            w["sa"] = buf(f"sa{d}", [P, TT, D_RWKV], own)
            w["states"] = buf(f"states{d}", [P, NC, NR, HD], own)
            rwkv_states(nc, t, d, w)
            rwkv_outputs(nc, d, w, y)
    rwkv_readout(nc, t, u, w["bonus"], y)



POOL_PAD = 8
GRID = 64
POOL_ROWS = LAT // GRID
WINDOWS = (2, 4, 8, 16)


def pool_counts():
    c = np.arange(GRID)
    out = np.zeros((P, 2, GRID), np.float32)
    for g, win in enumerate(WINDOWS):
        left = win // 2
        n = np.minimum(c + win - 1 - left, GRID - 1) + 1 - np.maximum(c - left, 0)
        out[64 * (g % 2):64 * (g % 2) + 64, g // 2] = 1.0 / n
    return out


def pool_branch(nc, t, p, pooled):
    wide = GRID + 2 * POOL_PAD
    with Stage(nc, "pool") as st:
        s = [st.sbuf(f"s{a}", [P, 2, POOL_ROWS, wide]) for a in range(4)]
        mean = st.sbuf("mean", [P, 2, POOL_ROWS, GRID])
        pw = st.sbuf("w", [P, 2, 64])
        inv = st.sbuf("inv", [P, 2, GRID])
        loaded = st.sem("loaded")
        own = st.sem("own")
        mean_ok = st.sem("mean")
        mixed = st.sem("mixed")
        ps = st.banks("ps", 2)
        block = st.block()

        @block.sync
        def _(sp):
            sp.dma_start(pw[:, :, :], t["dram"]["pool_w"]).then_inc(loaded, 16)
            sp.dma_start(inv[:, :, :], t["dram"]["pool_counts"]).then_inc(loaded, 16)
            sp.wait_ge(loaded, 32)

        @block.vector
        def _(dve):
            chain = Chain(dve, own)
            chain(nc.vector.tensor_tensor(s[0][:, :, :, 1:wide], p[:, :, :, 0:wide - 1], p[:, :, :, 1:wide], ALU.add))
            lo, hi = 1, wide
            for a, off in ((1, 1), (2, 2), (3, 4)):
                lo, hi = lo + off, hi - off
                chain(nc.vector.tensor_tensor(s[a][:, :, :, lo:hi], s[a - 1][:, :, :, lo - off:hi - off],
                                              s[a - 1][:, :, :, lo + off:hi + off], ALU.add))
            dve.wait_ge(loaded, 32)
            mid = slice(POOL_PAD, POOL_PAD + GRID)
            for g in range(4):
                hp = slice(64 * (g % 2), 64 * (g % 2) + 64)
                ins = nc.vector.tensor_tensor(mean[hp, g // 2], s[g][hp, g // 2, :, mid],
                                              spread(inv[hp, g // 2, :], 1, POOL_ROWS), ALU.mult)
            chain(ins)
            nc.vector.tensor_tensor(mean[:, :, :, :], mean[:, :, :, :], p[:, :, :, mid], ALU.subtract
                                    ).then_inc(mean_ok, 1)
            dve.wait_ge(mixed, 1)
            for f in range(2):
                nc.vector.tensor_scalar(pooled[:, f, :], ps[f][:, :], col(t, "pool_scale", f), None, ALU.mult)

        @block.tensor
        def _(pe):
            pe.wait_ge(loaded, 32)
            pe.wait_ge(mean_ok, 1)
            for g in range(4):
                hp = slice(64 * (g % 2), 64 * (g % 2) + 64)
                done = nc.tensor.matmul(ps[g // 2][hp, :], pw[hp, g // 2, :],
                                        mean[hp, g // 2].rearrange("p r c -> p (r c)"), start=True, stop=True)
            done.then_inc(mixed, 1)


def gated(nc, name, parts, gates, hh, hl, n_tok, also=(), factor=None):
    kt = len(parts)
    with Stage(nc, name) as st:
        full = st.sbuf("full", [P, kt, n_tok])
        full_ok = st.sem("full")
        high = st.sem("high")
        moved = st.sem("moved")
        block = st.block()

        @block.sync
        def _(sp):
            for dst, src in also:
                sp.dma_start(dst, src).then_inc(moved, 16)
            if also:
                sp.wait_ge(moved, 16 * len(also))

        @block.vector
        def _(dve):
            for k in range(kt):
                if gates[k] is None:
                    ins = nc.vector.tensor_copy(full[:, k, :], parts[k])
                else:
                    ins = nc.vector.tensor_tensor(full[:, k, :], parts[k], gates[k], ALU.mult)
                ins.then_inc(full_ok, 1)

        @block.scalar
        def _(act):
            for k in range(kt):
                act.wait_ge(full_ok, k + 1)
                nc.scalar.activation(hh[:, k, :n_tok], full[:, k, :], ACT.Copy).then_inc(high, 1)
            if factor is not None:
                act.wait_ge(moved, 16 * len(also))
                nc.scalar.activation(also[-1][0], also[-1][0], ACT.Copy, scale=factor)

        @block.gpsimd
        def _(pool):
            for k in range(kt):
                pool.wait_ge(high, k + 1)
                nc.gpsimd.tensor_tensor(hl[:, k, :n_tok], full[:, k, :], hh[:, k, :n_tok].bitcast(F32), ALU.subtract)


def into_residual(nc, x, mods, tile0, spans):
    def evac_dve(dve, i, ps, slot):
        for (t0, n, j), b in zip(spans, ps):
            res = x[:, bass.ds(i, 1), t0:t0 + n]
            ins = nc.vector.scalar_tensor_tensor(res, b[:, :n], mods[:, bass.ds(tile0 + i, 1), j:j + 1].rearrange("p a j -> p (a j)"),
                                                 res, ALU.mult, ALU.add)
        return ins
    return evac_dve


ALPHA = float(2.0 ** 0.25)



def unit_norm(nc, t, name, x, nf, spans, mat, mult, eps, factor, before=None, also=()):
    jobs = [(f, t0, n) for f in range(nf) for t0, n in spans]
    lo, hi = spans[0][0], spans[-1][0] + spans[-1][1]
    with Stage(nc, name) as st:
        sq = st.sbuf("sq", [P, nf, hi - lo])
        ready = st.sem("ready")
        squared = st.sem("squared")
        summed = st.sem("summed")
        log_ok = st.sem("log")
        inv = st.sem("inverse")
        moved = st.sem("moved")
        ps = st.banks("ps", 8)
        block = st.block()

        @block.sync
        def _(sp):
            for dst, src in also:
                sp.dma_start(dst, src).then_inc(moved, 16)
            if also:
                sp.wait_ge(moved, 16 * len(also))

        @block.scalar
        def _(act):
            if before is not None:
                for f in range(nf):
                    nc.scalar.activation(x[:, f, lo:hi], x[:, f, lo:hi], before).then_inc(ready, 1)
            for f in range(nf):
                if before is not None:
                    act.wait_ge(ready, f + 1)
                nc.scalar.activation(sq[:, f, :], x[:, f, lo:hi], ACT.Square).then_inc(squared, 1)
            for n, (f, t0, tn) in enumerate(jobs):
                act.wait_ge(summed, n + 1)
                nc.scalar.activation(sq[:, f, t0 - lo:t0 - lo + tn], ps[n % 8][:, :tn], ACT.Ln, scale=mult,
                                     bias=eps_col(t, eps)).then_inc(log_ok, 1)
            for f in range(nf):
                act.wait_ge(log_ok, len(spans) * (f + 1))
                nc.scalar.activation(sq[:, f, :], sq[:, f, :], ACT.Exp, scale=-0.5).then_inc(inv, 1)

        @block.tensor
        def _(pe):
            for n, (f, t0, tn) in enumerate(jobs):
                pe.wait_ge(squared, f + 1)
                if n >= 8:
                    pe.wait_ge(log_ok, n - 7)
                nc.tensor.matmul(ps[n % 8][:, :tn], mat, sq[:, f, t0 - lo:t0 - lo + tn],
                                 start=True, stop=True).then_inc(summed, 1)

        @block.vector
        def _(dve):
            for f in range(nf):
                dve.wait_ge(inv, f + 1)
                nc.vector.scalar_tensor_tensor(x[:, f, lo:hi], x[:, f, lo:hi], factor(f), sq[:, f, :],
                                               ALU.mult, ALU.mult)


GW = 4
HV = 128


def gmlp(nc, t, u, vtok, y):
    jobs = [(f, s) for f in range(GW) for s in range(2)]
    with Stage(nc, "gmlp") as st:
        ws = st.sbuf("ws", [P, GW, P])
        bs = st.sbuf("bs", [P, GW, P])
        tmp = st.sbuf("tmp", [P, GW, T])
        loaded = st.sem("loaded")
        mixed = st.sem("mixed")
        biased = st.sem("biased")
        ps = st.banks("ps", 8)
        block = st.block()

        @block.sync
        def _(sp):
            sp.dma_start(ws[:, :, :], t["dram"]["a_ws"]).then_inc(loaded, 16)
            sp.dma_start(bs[:, :, :], t["dram"]["a_bs"].partition_broadcast(P)).then_inc(loaded, 16)
            sp.wait_ge(loaded, 32)

        @block.tensor
        def _(pe):
            pe.wait_ge(loaded, 32)
            for n, (f, s) in enumerate(jobs):
                t0, tn = SEGS[s]
                for i in range(t0 // P, (t0 + tn) // P):
                    done = nc.tensor.matmul(ps[n][:, i * P - t0:(i + 1) * P - t0], vtok[:, i, f * P:(f + 1) * P],
                                            ws[:, f, :], start=True, stop=True)
                done.then_inc(mixed, 1)

        @block.vector
        def _(dve):
            dve.wait_ge(loaded, 32)
            for n, (f, s) in enumerate(jobs):
                t0, tn = SEGS[s]
                dve.wait_ge(mixed, n + 1)
                nc.vector.tensor_tensor(tmp[:, f, t0:t0 + tn].rearrange("p (c i) -> p c i", i=P),
                                        ps[n][:, :tn].rearrange("p (c i) -> p c i", i=P),
                                        spread(bs[:, f, :], 1, tn // P), ALU.add).then_inc(biased, 1)
            dve.wait_ge(biased, len(jobs))
            nc.vector.tensor_tensor(y[:, :, :], u[:, :, :], tmp[:, :, :], ALU.mult)


ROW = (0, 32)
BETA = 64


def gdn_rows(nc, t, p_ab, rows, rest, toks, w):
    with Stage(nc, "gdn_rows") as st:
        par = st.sbuf("par", [P, 2])
        ea = st.sbuf("ea", [P, 1])
        xr = st.sbuf("xr", [P, T])
        ax = st.sbuf("ax", [P, T])
        loaded = st.sem("loaded")
        x_ok = st.sem("x")
        log_ok = st.sem("log")
        own_a = st.sem("own_act")
        own_v = st.sem("own_dve")
        block = st.block()

        @block.sync
        def _(sp):
            sp.dma_start(par[:, :], t["dram"]["gdn_rows"]).then_inc(loaded, 16)
            sp.wait_ge(loaded, 16)

        @block.scalar
        def _(act):
            act.wait_ge(x_ok, 1)
            chain = Chain(act, own_a)
            chain(nc.scalar.activation(ax[:, :], xr[:, :], ACT.Abs))
            chain(nc.scalar.activation(ax[:, :], ax[:, :], ACT.Exp, scale=-1.0))
            nc.scalar.activation(ea[:, :], par[:, 0:1], ACT.Exp)
            nc.scalar.activation(ax[:, :], ax[:, :], ACT.Ln, bias=1.0).then_inc(log_ok, 1)
            nc.scalar.activation(rows[64:128, :], p_ab[64:128, :], ACT.Sigmoid)

        @block.vector
        def _(dve):
            chain = Chain(dve, own_v)
            nc.vector.memset(rest[64:128, :], 0.0)
            dve.wait_ge(loaded, 16)
            nc.vector.tensor_scalar(xr[:, :], p_ab[:, :], par[:, 1:2], None, ALU.add).then_inc(x_ok, 1)
            dve.wait_ge(log_ok, 1)
            chain(nc.vector.scalar_tensor_tensor(xr[:, :], xr[:, :], 0.0, ax[:, :], ALU.max, ALU.add))
            chain(nc.vector.tensor_scalar(xr[:, :], xr[:, :], ea[:, :], -1.0, ALU.mult, ALU.mult))
            nc.vector.tensor_tensor_scan(rows[0:32, :], t["turn"][0:32, :], xr[0:32, :], 0.0, ALU.mult, ALU.add)
            chain(nc.vector.tensor_tensor_scan(rows[32:64, ::-1], t["turn"][32:64, :], xr[32:64, ::-1], 0.0,
                                               ALU.mult, ALU.add))
            for d in range(2):
                r = slice(32 * d, 32 * d + 32)
                gv = rows[r, :].rearrange("p (c t) -> p c t", t=C)
                nc.vector.tensor_tensor(rest[r, :].rearrange("p (c t) -> p c t", t=C),
                                        spread(gv[:, :, (0 if d else C - 1)], 2, C), gv, ALU.subtract)

    ident = t["mask"][:, MASKS["ident"], :]
    to_tokens(nc, "gdn_rows_tok", [([src[:, i * P:(i + 1) * P]], dst[:, i, :])
                                   for src, dst in zip((rows, rest), toks) for i in range(TT)], ident)
    with Stage(nc, "gdn_scalars") as st:
        exp_ok = st.sem("exp")
        block = st.block()

        @block.scalar
        def _(act):
            nc.scalar.activation(w["kd"][:, :, :], toks[1][:, :, 0:64], ACT.Exp)
            nc.scalar.activation(w["nbg"][:, :, :], toks[0][:, :, 0:64], ACT.Exp).then_inc(exp_ok, 1)

        @block.vector
        def _(dve):
            dve.wait_ge(exp_ok, 1)
            nc.vector.scalar_tensor_tensor(w["nbg"][:, :, :], w["nbg"][:, :, :], -1.0, toks[0][:, :, 64:128],
                                           ALU.mult, ALU.mult)


def gdn_spread(nc, t, d, rows, q, k, w):
    ident = t["mask"][:, MASKS["ident"], :]
    jobs = [(e, h, s) for h in range(GW) for e in range(2) for s in range(2)]
    with Stage(nc, f"gdn{d}_spread") as st:
        row_ok = st.sem("row")
        g_ok = st.sem("g")
        b_ok = st.sem("b")
        e_ok = st.sem("exp")
        ps = st.banks("ps", 8)
        block = st.block()

        @block.tensor
        def _(pe):
            for n, (e, h, s) in enumerate(jobs):
                t0, tn = SEGS[s]
                if n >= 8:
                    pe.wait_ge(b_ok if e else g_ok, 2 * ((n - 8) // 4) + s + 1)
                r = ROW[d] + h + e * BETA
                nc.tensor.matmul(ps[n % 8][:, :tn], ident[:, r:r + 1].to_broadcast([P, P]), rows[:, t0:t0 + tn],
                                 start=True, stop=True).then_inc(row_ok, 1)

        @block.scalar
        def _(act):
            for n, (e, h, s) in enumerate(jobs):
                t0, tn = SEGS[s]
                if e == 0:
                    act.wait_ge(row_ok, n + 1)
                    nc.scalar.activation(w["grow"][:, h, t0:t0 + tn], ps[n % 8][:, :tn], ACT.Copy).then_inc(g_ok, 1)
            act.wait_ge(g_ok, 2 * GW)
            nc.scalar.activation(w["qg"][:, :, :], w["grow"][:, :, :], ACT.Exp).then_inc(e_ok, 1)
            ends = w["grow"][:, :, :].rearrange("p h (c t) -> p h c t", t=C)[:, :, :, (0 if d else C - 1)]
            nc.scalar.activation(w["ge"][:, :, :], ends, ACT.Exp)

        @block.vector
        def _(dve):
            for n, (e, h, s) in enumerate(jobs):
                t0, tn = SEGS[s]
                if e == 1:
                    dve.wait_ge(row_ok, n + 1)
                    nc.vector.scalar_tensor_tensor(w["nkb"][:, h, t0:t0 + tn], ps[n % 8][:, :tn], -1.0,
                                                   k[:, h, t0:t0 + tn], ALU.mult, ALU.mult).then_inc(b_ok, 1)
            dve.wait_ge(e_ok, 1)
            nc.vector.tensor_tensor(w["qg"][:, :, :], q[:, :, :], w["qg"][:, :, :], ALU.mult)


def gdn_grams(nc, t, d, q, k, w):
    with Stage(nc, f"gdn{d}_grams") as st:
        dec = st.sbuf("dec", [P, 2, GW, P])
        ds = st.sbuf("ds", [P, 2, GW, P])
        di = st.sbuf("di", [P, 2, GW, P])
        diff_ok = st.sem("diff")
        dec_ok = st.sem("decay")
        mask_ok = st.sem("masked")
        gram_ok = st.sem("gram")
        out_ok = st.sem("out")
        a_ps = st.banks("a", 2)
        b_ps = st.banks("b", 2)
        block = st.block()

        @block.tensor
        def _(pe):
            for i in range(TT):
                tok = slice(i * P, (i + 1) * P)
                if i >= 2:
                    pe.wait_ge(out_ok, i - 1)
                for h in range(GW):
                    hs = slice(h * P, (h + 1) * P)
                    nc.tensor.matmul(a_ps[i % 2][:, hs], k[:, h, tok], w["nkb"][:, h, tok], start=True, stop=True)
                    done = nc.tensor.matmul(b_ps[i % 2][:, hs], k[:, h, tok], q[:, h, tok], start=True, stop=True)
                done.then_inc(gram_ok, 1)

        @block.vector
        def _(dve):
            def difference(i):
                if i >= 2:
                    dve.wait_ge(mask_ok, 2 * i - 2)
                for h in range(GW):
                    nc.vector.tensor_scalar(dec[:, i % 2, h, :], w["grow"][:, h, i * P:(i + 1) * P],
                                            w["tok"][:, i, ROW[d] + h:ROW[d] + h + 1], 0.0,
                                            ALU.subtract, ALU.min).then_inc(diff_ok, 1)
            difference(0)
            for i in range(TT):
                if i + 1 < TT:
                    difference(i + 1)
                dve.wait_ge(gram_ok, i + 1)
                dve.wait_ge(mask_ok, 2 * i + 2)
                nc.vector.tensor_tensor(w["lt"][:, GW * i:GW * i + GW, :], ds[:, i % 2],
                                        a_ps[i % 2][:, :].rearrange("p (h t) -> p h t", t=P), ALU.mult)
                nc.vector.tensor_tensor(w["attn"][:, GW * i:GW * i + GW, :], di[:, i % 2],
                                        b_ps[i % 2][:, :].rearrange("p (h t) -> p h t", t=P), ALU.mult
                                        ).then_inc(out_ok, 1)

        @block.scalar
        def _(act):
            for i in range(TT):
                act.wait_ge(diff_ok, GW * i + GW)
                nc.scalar.activation(dec[:, i % 2], dec[:, i % 2], ACT.Exp).then_inc(dec_ok, 1)

        @block.gpsimd
        def _(pool):
            for i in range(TT):
                pool.wait_ge(dec_ok, i + 1)
                if i >= 2:
                    pool.wait_ge(out_ok, i - 1)
                for out, m in ((ds, f"strict{d}"), (di, f"incl{d}")):
                    nc.gpsimd.tensor_tensor(out[:, i % 2], dec[:, i % 2],
                                            spread(t["mask"][:, MASKS[m], :], 1, GW), ALU.mult).then_inc(mask_ok, 1)


def gdn_solve(nc, d, w):
    r0 = ROW[d]
    with Stage(nc, f"gdn{d}_solve") as st:
        rhs = st.sbuf("rhs", [P, TT, GW, HV])
        rhs_ok = st.sem("rhs")
        solved = st.sem("solved")
        read = st.sem("read")
        ps = st.banks("ps", 4)
        block = st.block()

        @block.vector
        def _(dve):
            for n, (src, scal) in enumerate(((w["ktok"], w["nbg"][:, :, r0:r0 + GW]),
                                             (w["vtok"], w["tok"][:, :, BETA + r0:BETA + r0 + GW]))):
                if n:
                    dve.wait_ge(solved, TT)
                nc.vector.tensor_tensor(rhs[:, :, :, :], src[:, :, :].rearrange("p i (h c) -> p i h c", h=GW),
                                        spread(scal, 3, HV), ALU.mult).then_inc(rhs_ok, 1)

        @block.tensor
        def _(pe):
            for n in range(2 * TT):
                i = n % TT
                pe.wait_ge(rhs_ok, n // TT + 1)
                if n >= 4:
                    pe.wait_ge(read, n - 3)
                for h in range(GW):
                    out, xt, r = ps[n % 4][:, h * P:(h + 1) * P], w["xt"][:, GW * i + h, :], rhs[:, i, h, :]
                    left, right = (r, xt) if n < TT else (xt, r)
                    done = nc.tensor.matmul(out, left, right, start=True, stop=True)
                done.then_inc(solved, 1)

        @block.scalar
        def _(act):
            for n in range(2 * TT):
                i = n % TT
                act.wait_ge(solved, n + 1)
                out = w["wt"][:, :, i * P:(i + 1) * P] if n < TT else \
                    w["u"][:, i, :].rearrange("p (h v) -> p h v", h=GW)
                nc.scalar.activation(out, ps[n % 4][:, :].rearrange("p (h v) -> p h v", h=GW), ACT.Copy
                                     ).then_inc(read, 1)


def gdn_states(nc, t, d, w):
    r0 = ROW[d]
    with Stage(nc, f"gdn{d}_states") as st:
        kd = st.sbuf("kd", [P, TT, GW, HV])
        kd_ok = st.sem("kd")
        v_ps_ok = st.sem("v_product")
        v_ok = st.sem("v")
        decayed = st.sem("decayed")
        update = st.sem("update")
        state_ok = st.sem("state")
        tmp = st.sbuf("tmp", [P, 2, GW, HV])
        vps = st.banks("v", 2)
        ups = st.banks("up", 2)
        spare = st.banks("spare", 1)[0]
        block = st.block()
        order = chunk_order(d)
        states = w["states"]

        @block.tensor
        def _(pe):
            open_clock_with(nc, t, spare, 8)
            pe.wait_ge(kd_ok, 1)
            for n, c in enumerate(order):
                tok, i = slice(C * (c % 2), C * (c % 2) + C), c // 2
                pe.wait_ge(state_ok, n + 1)
                for h in range(GW):
                    done = nc.tensor.matmul(vps[n % 2][tok, h * HV:(h + 1) * HV], w["wt"][:, h, c * C:(c + 1) * C],
                                            states[:, c, h, :], start=True, stop=True)
                done.then_inc(v_ps_ok, 1)
                open_clock_with(nc, t, spare, 2, 256)
                if n == NC - 1:
                    break
                pe.wait_ge(v_ok, n + 1)
                for h in range(GW):
                    done = nc.tensor.matmul(ups[n % 2][:, h * HV:(h + 1) * HV], kd[tok, i, h, :],
                                            w["u"][tok, i, h * HV:(h + 1) * HV], start=True, stop=True)
                done.then_inc(update, 1)
                open_clock_with(nc, t, spare, 2, 256)

        @block.gpsimd
        def _(pool):
            for n, c in enumerate(order[:-1]):
                pool.wait_ge(state_ok, n + 1)
                nc.gpsimd.tensor_tensor(tmp[:, n % 2], states[:, c], spread(w["ge"][:, :, c], 2, HV), ALU.mult
                                        ).then_inc(decayed, 1)

        @block.vector
        def _(dve):
            nc.vector.memset(states[:, order[0]], 0.0).then_inc(state_ok, 1)
            nc.vector.tensor_tensor(kd[:, :, :, :], w["ktok"][:, :, :].rearrange("p i (h c) -> p i h c", h=GW),
                                    spread(w["kd"][:, :, r0:r0 + GW], 3, HV), ALU.mult).then_inc(kd_ok, 1)
            for n, c in enumerate(order):
                tok, i = slice(C * (c % 2), C * (c % 2) + C), c // 2
                dve.wait_ge(v_ps_ok, n + 1)
                nc.vector.tensor_tensor(w["u"][tok, i, :], w["u"][tok, i, :], vps[n % 2][tok, :], ALU.add
                                        ).then_inc(v_ok, 1)
                if n == NC - 1:
                    break
                dve.wait_ge(decayed, n + 1)
                dve.wait_ge(update, n + 1)
                nc.vector.tensor_tensor(states[:, order[n + 1]], tmp[:, n % 2],
                                        ups[n % 2][:, :].rearrange("p (h v) -> p h v", v=HV), ALU.add
                                        ).then_inc(state_ok, 1)


def gdn_outputs(nc, t, d, w, o):
    jobs = [(h, s) for h in range(GW) for s in range(2)]
    with Stage(nc, f"gdn{d}_out") as st:
        summed = st.sem("summed")
        ps = st.banks("ps", 8)
        block = st.block()

        @block.tensor
        def _(pe):
            open_clock_with(nc, t, ps[0], 6)
            for n, (h, s) in enumerate(jobs):
                t0, tn = SEGS[s]
                for i in range(t0 // P, (t0 + tn) // P):
                    nc.tensor.matmul(ps[n][:, i * P - t0:(i + 1) * P - t0], w["u"][:, i, h * HV:(h + 1) * HV],
                                     w["attn"][:, GW * i + h, :], start=True, stop=False)
                    for c in (2 * i, 2 * i + 1):
                        done = nc.tensor.matmul(ps[n][:, c * C - t0:(c + 1) * C - t0], w["states"][:, c, h, :],
                                                w["qg"][:, h, c * C:(c + 1) * C], start=False, stop=c % 2 == 1)
                done.then_inc(summed, 1)

        @block.vector
        def _(dve):
            for n, (h, s) in enumerate(jobs):
                t0, tn = SEGS[s]
                dve.wait_ge(summed, n + 1)
                if d == 0:
                    nc.vector.tensor_copy(o[:, h, t0:t0 + tn], ps[n][:, :tn])
                else:
                    nc.vector.tensor_tensor(o[:, h, t0:t0 + tn], o[:, h, t0:t0 + tn], ps[n][:, :tn], ALU.add)


def gdn(nc, t, qkv, p_ab, o, mem):
    def buf(name, shape, where=mem, side=None):
        return where.enter_context(nc.sbuf_tensor(f"gd_{name}", shape, F32, side=side))

    ident = t["mask"][:, MASKS["ident"], :]
    q, k = qkv[:, 0:4, :], qkv[:, 4:8, :]
    w = {"ktok": buf("ktok", [P, TT, GW * HV]), "vtok": buf("vtok", [P, TT, GW * HV]),
         "tok": buf("tok", [P, TT, P]), "kd": buf("kd", [P, TT, 64]), "nbg": buf("nbg", [P, TT, 64]),
         "ge": buf("ge", [P, GW, NC])}
    rows = buf("rows", [P, T])
    with ExitStack() as part:
        rest = buf("rest", [P, T], part)
        rtok = buf("rtok", [P, TT, P], part)
        gdn_rows(nc, t, p_ab, rows, rest, (w["tok"], rtok), w)
    to_tokens(nc, "gdn_tok", [([qkv[:, f0 + f, i * P:(i + 1) * P] for f in range(GW)], w[dst][:, i, :])
                              for f0, dst in ((4, "ktok"), (8, "vtok")) for i in range(TT)], ident)
    for d in range(2):
        with ExitStack() as own:
            w["qg"] = buf(f"qg{d}", [P, GW, T], own)
            w["attn"] = buf(f"attn{d}", [P, TT * GW, P], own)
            solve = ExitStack()
            w["lt"] = buf(f"lt{d}", [P, TT * GW, P], solve, "right")
            with ExitStack() as part:
                w["grow"] = buf(f"grow{d}", [P, GW, T], part)
                w["nkb"] = buf(f"nkb{d}", [P, GW, T], part)
                gdn_spread(nc, t, d, rows, q, k, w)
                gdn_grams(nc, t, d, q, k, w)
            w["xt"] = w["lt"]
            inverses(nc, t, f"gdn{d}_inv", w["lt"], w["xt"], [slice(a, a + 4) for a in range(0, TT * GW, 4)], d)
            w["wt"] = buf(f"wt{d}", [P, GW, T], own)
            w["u"] = buf(f"u{d}", [P, TT, GW * HV], own)
            gdn_solve(nc, d, w)
            solve.close()
            w["states"] = buf(f"states{d}", [P, NC, GW, HV], own)
            gdn_states(nc, t, d, w)
            gdn_outputs(nc, t, d, w, o)



D_FF = 2816
FH = D_FF // P // 2


def ffn(nc, t, name, layer, x, hh, hl, spans, conds, mods, gate0, sides=(None, None)):
    base, tokens, ns = spans[0][0], sum(n for _, n in spans), len(spans)
    local = [(t0 - base, n) for t0, n in spans]
    for part in range(2):
        with ExitStack() as mem:
            ah = mem.enter_context(nc.sbuf_tensor(f"{name}_ah{part}", [P, FH * tokens], F32R))
            al = mem.enter_context(nc.sbuf_tensor(f"{name}_al{part}", [P, FH * tokens], F32R))
            with ExitStack() as up:
                tmp = up.enter_context(nc.sbuf_tensor(f"{name}_tmp{part}", [P, 2, tokens], F32))
                sil = up.enter_context(nc.sbuf_tensor(f"{name}_sil{part}", [P, tokens], F32))

                def make(st):
                    before_ok = st.sem("tap_before")
                    silu_ok = st.sem("silu")
                    pair_ok = st.sem("pair")
                    prod_ok = st.sem("product")
                    high_ok = st.sem("high")

                    def tap(k, i):
                        o = COL["ffn_conv_w_2"][0] + (layer * 3 + k) * 44 + part * 22
                        return t["cols"][:, bass.ds(i + o, 1)]

                    def pair(buf, i):
                        return buf[:, bass.ds(i * (tokens // 2) - tokens // 2, tokens)]

                    def credits(act):
                        act.sem_inc(silu_ok, 2)
                        act.sem_inc(pair_ok, 2)

                    def evac_act(act, i, ps, slot):
                        if slot == 0:
                            act.wait_ge(silu_ok, i + 2)
                        else:
                            act.wait_ge(st.banks_free, i + 2)
                            act.wait_ge(pair_ok, i + 1)
                            nc.scalar.activation(sil[:, :], tmp[:, 0, :], ACT.Silu).then_inc(silu_ok, 2)
                        for (t0, n), b in zip(local, ps):
                            ins = nc.scalar.activation(tmp[:, slot, t0:t0 + n], b[:, :n], ACT.Copy, scale=tap(1, i))
                        return ins

                    def evac_dve(dve, i, ps, slot):
                        for (t0, n), b in zip(local, ps):
                            out = tmp[:, slot, t0 + 1:t0 + n]
                            nc.vector.scalar_tensor_tensor(out, b[:, :n - 1], tap(0, i), out, ALU.mult, ALU.add
                                                           ).then_inc(before_ok, 1)
                        dve.wait_ge(before_ok, i * ns + ns)
                        for (t0, n), b in zip(local, ps):
                            out = tmp[:, slot, t0:t0 + n - 1]
                            ins = nc.vector.scalar_tensor_tensor(out, b[:, 1:n], tap(2, i), out, ALU.mult, ALU.add)
                        ins.then_inc(st.banks_free, 1)
                        if slot == 0:
                            return None
                        dve.wait_ge(st.banks_free, i + 3)
                        dve.wait_ge(silu_ok, i + 3)
                        nc.vector.tensor_tensor(tmp[:, 1, :], tmp[:, 1, :], sil[:, :], ALU.mult).then_inc(prod_ok, 2)
                        dve.wait_ge(prod_ok, i + 1)
                        nc.vector.tensor_copy(pair(ah, i), tmp[:, 1, :]).then_inc(high_ok, 2)
                        dve.wait_ge(high_ok, i + 1)
                        nc.vector.tensor_tensor(pair(al, i), tmp[:, 1, :], pair(ah, i).bitcast(F32), ALU.subtract
                                                ).then_inc(pair_ok, 2)
                        return None
                    st.credits = credits
                    return evac_act, evac_dve
                dense(nc, f"{name}_up{part}", t["dram"]["ffn_up"], 2 * FH, KD, hh, hl, spans, evac=make, warm=ACT.Silu,
                      first=layer * 4 * FH + part * 2 * FH)
            dense(nc, f"{name}_down{part}", t["dram"]["ffn_down"], KD, FH,
                  ah[:, :].rearrange("p (k t) -> p k t", k=FH), al[:, :].rearrange("p (k t) -> p k t", k=FH),
                  local, evac_dve=into_residual(nc, x, mods, gate0, conds), first=(layer * 2 + part) * KD,
                  side=sides[part])



HEADS, ROPE = 8, 64
SCALE = float((128 + ROPE) ** -0.5)


def rope_tables():
    n_freq = ROPE // 4
    inv = (np.float32(10000.0) ** (-np.arange(n_freq, dtype=np.float32) / np.float32(n_freq))).astype(np.float32)
    tok = np.arange(LAT)
    row, column = (tok // GRID).astype(np.float32), (tok % GRID).astype(np.float32)
    ang = np.concatenate([row[:, None] * inv, column[:, None] * inv], -1).astype(np.float32)
    table = np.stack([np.tile(f(ang).astype(np.float32).T, (4, 1)) for f in (np.cos, np.sin)], 1)
    half = ROPE // 2
    turn = np.zeros((P, P), np.float32)
    for m in range(P):
        turn[(m + half, m) if m % ROPE < half else (m - half, m)] = -1.0 if m % ROPE < half else 1.0
    return np.ascontiguousarray(table), turn


def values(nc, w_tiles, first, ch, cl, v):
    jobs = [(i, s) for i in range(TT) for s in range(2)]
    with Stage(nc, "values") as st:
        w = st.sbuf("w", [P, HEADS, 2 * P])
        wh = st.sbuf("wh", [P, HEADS, 2 * P], F32R)
        wl = st.sbuf("wl", [P, HEADS, 2 * P], F32R)
        loaded = st.sem("loaded")
        w_high = st.sem("w_high")
        w_low = st.sem("w_low")
        done_ok = st.sem("done")
        read = [st.sem("read_act"), st.sem("read_dve")]
        ps = st.banks("ps", 4)
        block = st.block()

        @block.sync
        def _(sp):
            sp.dma_start(w[:, :, :], w_tiles[first:first + HEADS].rearrange("a p f -> p a f")).then_inc(loaded, 16)
            sp.wait_ge(loaded, 16)

        @block.gpsimd
        def _(pool):
            pool.wait_ge(w_high, 1)
            nc.gpsimd.tensor_tensor(wl[:, 4:, :], w[:, 4:, :], wh[:, 4:, :].bitcast(F32), ALU.subtract).then_inc(w_low, 1)

        @block.tensor
        def _(pe):
            open_clock(nc, ch[:, 0, CTX:CTX + P], ch[:, 0, CTX:T], ps[3], 12)
            pe.wait_ge(w_low, 2)
            for n, (i, s) in enumerate(jobs):
                if n >= 4:
                    pe.wait_ge(read[n % 2], (n - 4) // 2 + 1)
                tok = slice(i * P, (i + 1) * P)
                for k in range(2):
                    high, low = (b[:, 4 * s:4 * s + 4, k * P:(k + 1) * P] for b in (wh, wl))
                    out = ps[n % 4][:, :].rearrange("p (a f) -> p a f", f=P)
                    nc.tensor.matmul(out, ch[:, k, tok], high, start=k == 0, stop=False)
                    nc.tensor.matmul(out, cl[:, k, tok], high, start=False, stop=False)
                    done = nc.tensor.matmul(out, ch[:, k, tok], low, start=False, stop=k == 1)
                done.then_inc(done_ok, 1)

        def read_out(eng, n, copy):
            i, s = jobs[n]
            eng.wait_ge(done_ok, n + 1)
            copy(v[:, i, 512 * s:512 * s + 512], ps[n % 4][:, :]).then_inc(read[n % 2], 1)

        @block.scalar
        def _(act):
            act.wait_ge(loaded, 16)
            nc.scalar.activation(wh[:, :, :], w[:, :, :], ACT.Copy).then_inc(w_high, 1)
            for n in range(0, len(jobs), 2):
                read_out(act, n, lambda o, i: nc.scalar.activation(o, i, ACT.Copy))

        @block.vector
        def _(dve):
            dve.wait_ge(w_high, 1)
            nc.vector.tensor_tensor(wl[:, :4, :], w[:, :4, :], wh[:, :4, :].bitcast(F32), ALU.subtract).then_inc(w_low, 1)
            for n in range(1, len(jobs), 2):
                read_out(dve, n, lambda o, i: nc.vector.tensor_copy(o, i))


def rotate(nc, t, tiles):
    with Stage(nc, "rope") as st:
        table = st.sbuf("table", [P, 2, LAT])
        swap = st.sbuf("swap", [P, P])
        part = st.sbuf("part", [P, len(tiles), LAT])
        loaded = st.sem("loaded")
        swapped = st.sem("swapped")
        sin_ok = st.sem("sin")
        cos_ok = st.sem("cos")
        ps = st.banks("ps", 8)
        block = st.block()

        @block.sync
        def _(sp):
            sp.dma_start(table[:, :, :], t["dram"]["rope_table"]).then_inc(loaded, 16)
            sp.dma_start(swap[:, :], t["dram"]["rope_swap"]).then_inc(loaded, 16)
            sp.wait_ge(loaded, 32)

        @block.tensor
        def _(pe):
            pe.wait_ge(loaded, 32)
            for n, x in enumerate(tiles):
                nc.tensor.matmul(ps[n][:, :], swap[:, :], x, start=True, stop=True).then_inc(swapped, 1)

        @block.vector
        def _(dve):
            dve.wait_ge(loaded, 32)
            for n, x in enumerate(tiles):
                dve.wait_ge(swapped, n + 1)
                nc.vector.tensor_tensor(part[:, n, :], ps[n][:, :], table[:, 1, :], ALU.mult).then_inc(sin_ok, 1)
            for n, x in enumerate(tiles):
                dve.wait_ge(sin_ok, n + 1)
                dve.wait_ge(cos_ok, n + 1)
                nc.vector.tensor_tensor(x, x, part[:, n, :], ALU.add)

        @block.gpsimd
        def _(pool):
            pool.wait_ge(loaded, 32)
            for n, x in enumerate(tiles):
                pool.wait_ge(swapped, n + 1)
                nc.gpsimd.tensor_tensor(x, x, table[:, 0, :], ALU.mult).then_inc(cos_ok, 1)


def attention(nc, t, qn, qr, kn, kr, vtok, oh, ol):
    QT = LAT // P
    jobs = [(h, q) for h in range(HEADS) for q in range(QT)]
    ident = t["mask"][:, MASKS["ident"], :]
    with Stage(nc, "att") as st:
        p = st.sbuf("p", [P, 2, T])
        pt = [st.sbuf(f"pt{j}", [P, TT, LAT]) for j in range(2)]
        top = st.sbuf("top", [P, 2])
        neg = st.sbuf("neg", [P, 2])
        total = st.sbuf("total", [P, 2])
        inv = st.sbuf("inv", [P, 2])
        scores_ok = st.sem("scores")
        top_ok = st.sem("top")
        neg_ok = st.sem("neg")
        exp_ok = st.sem("exp")
        inv_ok = st.sem("inv")
        probs_ok = st.sem("probs")
        turned = [st.sem("turned0"), st.sem("turned1")]
        copied = [st.sem("copied_act"), st.sem("copied_dve")]
        mixed = st.sem("mixed")
        high = st.sem("high")
        low = st.sem("low")
        s_ps = [st.mem.enter_context(nc.psum_tensor(f"att_s{j}", [P, 1024], F32)) for j in range(2)]
        t_ps = st.banks("turned", 2)
        o_ps = st.banks("o", 2)
        block = st.block()

        @block.tensor
        def _(pe):
            def scores(n):
                h, q = jobs[n]
                if n >= 2:
                    pe.wait_ge(exp_ok, n - 1)
                tok, hp = slice(q * P, (q + 1) * P), slice(ROPE * (h % 2), ROPE * (h % 2) + ROPE)
                for k0, kn_ in ((0, 512), (512, T - 512)):
                    out = s_ps[n % 2][:, k0:k0 + kn_]
                    nc.tensor.matmul(out, qn[:, h, tok], kn[:, h, k0:k0 + kn_], start=True, stop=False)
                    done = nc.tensor.matmul(out, qr[hp, h // 2, tok], kr[hp, k0:k0 + kn_], start=False, stop=True)
                done.then_inc(scores_ok, 1)

            def product(h):
                for c in copied:
                    pe.wait_ge(c, QT * (h + 1))
                if h >= 2:
                    pe.wait_ge(low, h - 1)
                for i in range(TT):
                    done = nc.tensor.matmul(o_ps[h % 2][:, :], vtok[:, i, h * P:(h + 1) * P], pt[h % 2][:, i, :],
                                            start=i == 0, stop=i == TT - 1)
                done.then_inc(mixed, 1)

            scores(0)
            for n, (h, q) in enumerate(jobs):
                if n + 1 < len(jobs):
                    scores(n + 1)
                if q == 0 and h:
                    product(h - 1)
                pe.wait_ge(probs_ok, n + 1)
                for b in range(2):
                    if n:
                        pe.wait_ge(copied[b], n)
                    for i in range(3):
                        k0 = (3 * b + i) * P
                        done = nc.tensor.transpose(t_ps[b][:, i * P:(i + 1) * P], p[:, n % 2, k0:k0 + P], ident)
                    done.then_inc(turned[b], 1)
            product(HEADS - 1)

        @block.scalar
        def _(act):
            def exponential(n):
                act.wait_ge(neg_ok, n + 1)
                if n >= 2:
                    act.wait_ge(turned[1], n - 1)
                nc.scalar.activation(p[:, n % 2, :], s_ps[n % 2][:, :T], ACT.Exp, scale=SCALE,
                                     bias=neg[:, n % 2:n % 2 + 1], accum_out=total[:, n % 2:n % 2 + 1]
                                     ).then_inc(exp_ok, 1)

            def high_part(h):
                act.wait_ge(mixed, h + 1)
                nc.scalar.activation(oh[:, h, :], o_ps[h % 2][:, :], ACT.Copy).then_inc(high, 1)

            exponential(0)
            for n, (h, q) in enumerate(jobs):
                if n + 1 < len(jobs):
                    exponential(n + 1)
                act.wait_ge(turned[0], n + 1)
                if h >= 2:
                    act.wait_ge(mixed, h - 1)
                nc.scalar.activation(pt[h % 2][:, 0:3, q * P:(q + 1) * P],
                                     t_ps[0][:, :3 * P].rearrange("p (i t) -> p i t", i=3), ACT.Copy).then_inc(copied[0], 1)
                if q == 0 and h:
                    high_part(h - 1)
            high_part(HEADS - 1)

        @block.vector
        def _(dve):
            def maximum(n):
                dve.wait_ge(scores_ok, n + 1)
                if n >= 2:
                    dve.wait_ge(exp_ok, n - 1)
                j = slice(n % 2, n % 2 + 1)
                nc.vector.tensor_reduce(top[:, j], s_ps[n % 2][:, :T], AX.X, ALU.max).then_inc(top_ok, 1)
                dve.wait_ge(top_ok, n + 1)
                nc.vector.tensor_scalar(neg[:, j], top[:, j], -SCALE, None, ALU.mult).then_inc(neg_ok, 1)

            def low_part(h):
                dve.wait_ge(high, h + 1)
                nc.vector.tensor_tensor(ol[:, h, :], o_ps[h % 2][:, :], oh[:, h, :].bitcast(F32), ALU.subtract
                                        ).then_inc(low, 1)

            maximum(0)
            for n, (h, q) in enumerate(jobs):
                j = slice(n % 2, n % 2 + 1)
                dve.wait_ge(exp_ok, n + 1)
                nc.vector.reciprocal(inv[:, j], total[:, j]).then_inc(inv_ok, 1)
                dve.wait_ge(inv_ok, n + 1)
                nc.vector.tensor_scalar(p[:, n % 2, :], p[:, n % 2, :], inv[:, j], None, ALU.mult).then_inc(probs_ok, 1)
                if n + 1 < len(jobs):
                    maximum(n + 1)
                dve.wait_ge(turned[1], n + 1)
                if h >= 2:
                    dve.wait_ge(mixed, h - 1)
                nc.vector.tensor_copy(pt[h % 2][:, 3:6, q * P:(q + 1) * P],
                                      t_ps[1][:, :3 * P].rearrange("p (i t) -> p i t", i=3)).then_inc(copied[1], 1)
                if q == 0 and h:
                    low_part(h - 1)
            low_part(HEADS - 1)



def clear(nc, name, ap):
    with Stage(nc, name) as st:
        block = st.block()

        @block.gpsimd
        def _(pool):
            nc.gpsimd.memset(ap, 0.0)


def constant(nc, name, value, where):
    c = where.enter_context(nc.sbuf_tensor(name, [P, P], F32))
    with Stage(nc, f"{name}_fill") as st:
        block = st.block()

        @block.vector
        def _(dve):
            nc.vector.memset(c[:, :], value)
    return c


def activated(nc, dst, func, spans, shift=0):
    def evac_act(act, i, ps, slot):
        for (t0, n), b in zip(spans, ps):
            ins = nc.scalar.activation(dst[:, bass.ds(i + shift, 1), t0:t0 + n], b[:, :n], func)
        return ins
    return evac_act


def rms_mod(nc, t, name, x, spans, mods, o, hh, hl):
    conds = [1 if t0 < CTX else 0 for t0, _ in spans]
    normed(nc, t, name, x, KD, spans, t["over_d"], 1e-6, False,
           [lambda k, j=j: mods[:, o + KD + k, j:j + 1] for j in conds],
           [lambda k, j=j: mods[:, o + k, j:j + 1] for j in conds], hh, hl)


A_U, A_V, A_QKV, A_GATE, A_AB = 0, 4, 8, 20, 24


def second(nc, d, t, out, x_dram, x2, tail, keep):
    both = ((0, CTX, 1), (CTX, LAT, 0))
    gains1, gains2 = cols_of(t, "norm1_g_2"), cols_of(t, "norm2_g_2")
    with ExitStack() as mem:
        mods = t["mods2"]
        branches, tall, hidden = ExitStack(), ExitStack(), ExitStack()
        ones = constant(nc, "ones", 1.0, mem)
        y_a = keep("y_a", [P, GW, T], where=branches)
        o = keep("o_gdn", [P, GW, T], where=branches)
        hh = keep("h2_h", [P, KD, T], F32R, where=hidden)
        hl = keep("h2_l", [P, KD, T], F32R, where=hidden)
        rms_mod(nc, t, "rms_a", x2, SEGS, mods, 0, hh, hl)
        with ExitStack() as part:
            a_uv = keep("a_uv", [P, 2 * GW, T], where=part)
            a_u, a_v = a_uv[:, :GW, :], a_uv[:, GW:, :]
            vtok = keep("a_vtok", [P, TT, GW * P], where=part)
            dense(nc, "a_uv_mm", d["ab_w"], 8, KD, hh, hl, SEGS, first=A_U, evac_act=activated(nc, a_uv, ACT.Gelu, SEGS),
                  warm=ACT.Gelu, also=[(x_dram, x2[:, :, :])], side=Gemv(d["ada_w"], d["vec_2"], mods, 72, 2))
            tail.close()
            over = constant(nc, "over_512", 1.0 / 512, part)
            normed(nc, t, "a_ln", a_v, GW, SEGS, over, 1e-6, True, [lambda k: col(t, "a_ln_g_2", k)] * 2,
                   [lambda k: col(t, "a_ln_b_2", k)] * 2, None, None, out=a_v)
            to_tokens(nc, "a_tok", [([a_v[:, f, i * P:(i + 1) * P] for f in range(GW)], vtok[:, i, :])
                                    for i in range(TT)], t["mask"][:, MASKS["ident"], :])
            gmlp(nc, t, a_u, vtok, y_a)
        gate_dram = nc.dram_tensor("b_gate_kept", (P, GW, T), F32, kind="Internal").ap()
        with ExitStack() as part:
            gate = keep("b_gate", [P, GW, T], where=part)
            dense(nc, "b_gate_mm", d["ab_w"], 4, KD, hh, hl, SEGS, first=A_GATE,
                  evac_act=activated(nc, gate, ACT.Silu, SEGS), warm=ACT.Silu)
            qkv = keep("qkv", [P, 12, T], where=tall, side="right")
            p_ab = keep("p_ab", [P, 1, T], where=tall, side="right")
            dense(nc, "qkv_mm", d["ab_w"], 12, KD, hh, hl, SEGS, first=A_QKV,
                  evac=three_taps(nc, t, "b_conv_w_2", 12, lambda i, t0, n: qkv[:, bass.ds(i, 1), t0:t0 + n], SEGS),
                  side=Gemv(d["ada_w"], d["vec_2"], mods, 48, 2), also=[(gate_dram, gate[:, :, :])])
        dense(nc, "ab_mm", d["ab_w"], 1, KD, hh, hl, SEGS, first=A_AB, evac_act=activated(nc, p_ab, ACT.Copy, SEGS))
        hidden.close()
        with Stage(nc, "v_silu") as st:
            block = st.block()

            @block.scalar
            def _(act):
                nc.scalar.activation(qkv[:, 8:12, :], qkv[:, 8:12, :], ACT.Silu)
        unit_norm(nc, t, "qk_unit", qkv[:, 0:8, :], 8, SEGS, ones[:, :], 1.0, 1e-6,
                  lambda f: float(HV ** -0.5) if f < GW else 1.0, before=ACT.Silu)
        with ExitStack() as part:
            gdn(nc, t, qkv, p_ab[:, 0, :], o, part)
        tall.close()
        late = ExitStack()
        x2 = keep("x_b", [P, KD, T], where=late, side="right")
        hh = keep("h_h", [P, KD, T], F32R, where=late, side="right")
        hl = keep("h_l", [P, KD, T], F32R, where=late, side="right")
        with ExitStack() as part:
            gate = keep("b_gate_back", [P, GW, T], where=part)
            unit_norm(nc, t, "o_rms", o, GW, SEGS, ones[:, :], 1.0 / HV, 1e-6, lambda f: col(t, "b_norm_g_2", 0),
                      also=[(gate[:, :, :], gate_dram), (x2[:, :, :], x_dram)])
            gated(nc, "mix2", [y_a[:, f, :] for f in range(GW)] + [o[:, f, :] for f in range(GW)],
                  [None] * GW + [gate[:, f, :] for f in range(GW)], hh, hl, T)
        branches.close()
        dense(nc, "ab_out_mm", d["ab_w_out"], KD, KD, hh, hl, SEGS, evac_dve=into_residual(nc, x2, mods, 16, both),
              side=Gemv(d["ada_w"], d["vec_2"], mods, 88, 1))
        modulation(nc, t, "mods2", 48, cols_of(t, "ada_b_2")[:, 48:], (56, 80), (gains1[:, KD:], gains2[:, KD:]))
        rms_mod(nc, t, "rms_f0", x2, SEGS, mods, 24, hh, hl)
        ffn(nc, t, "f0", 0, x2, hh, hl, SEGS, both, mods, 40)

        rms_mod(nc, t, "rms_c", x2, SEGS, mods, 48, hh, hl)
        with ExitStack() as part:
            ckv = keep("c_ckv", [P, 3, T], where=part)
            kr = ckv[:, 2, :]
            qs = keep("c_qs", [P, 12, LAT], where=part)
            qn, qr = qs[:, :HEADS, :], qs[:, HEADS:, :]
            with ExitStack() as low:
                cq = keep("c_cq", [P, 3, LAT], where=low)
                cq_h = keep("c_cq_h", [P, 3, LAT], F32R, where=low)
                cq_l = keep("c_cq_l", [P, 3, LAT], F32R, where=low)
                over = constant(nc, "over_384", 1.0 / 384, low)
                shifted = [(0, LAT)]

                def cq_out(act, i, ps, slot):
                    return nc.scalar.activation(cq[:, bass.ds(i, 1), :], ps[0][:, :], ACT.Copy)
                dense(nc, "cq_mm", d["mla_w"], 3, KD, hh, hl, LAT_ONLY, evac_act=cq_out)
                normed(nc, t, "cq_rms", cq, 3, shifted, over, 1e-6, False, [lambda k: col(t, "mla_q_norm_g_2", k)],
                       None, cq_h, cq_l)
                dense(nc, "q_mm", d["mla_uq"], 12, 3, cq_h, cq_l, shifted, evac_act=activated(nc, qs, ACT.Copy, shifted))
            v = keep("c_vtok", [P, TT, HEADS * P], where=part)
            kn = keep("c_kn", [P, HEADS, T], where=part)
            with ExitStack() as low:
                ckv_h = keep("c_ckv_h", [P, 2, T], F32R, where=low)
                ckv_l = keep("c_ckv_l", [P, 2, T], F32R, where=low)
                over = constant(nc, "over_256", 1.0 / 256, low)
                dense(nc, "ckv_mm", d["mla_w"], 3, KD, hh, hl, SEGS, first=3, evac_act=activated(nc, ckv, ACT.Copy, SEGS))
                normed(nc, t, "ckv_rms", ckv, 2, SEGS, over, 1e-6, False, [lambda k: col(t, "mla_kv_norm_g_2", k)] * 2,
                       None, ckv_h, ckv_l)
                dense(nc, "kn_mm", d["mla_ukv"], HEADS, 2, ckv_h, ckv_l, SEGS, evac_act=activated(nc, kn, ACT.Copy, SEGS))
                values(nc, d["mla_ukv"], HEADS, ckv_h, ckv_l, v)
            rotate(nc, t, [qr[:, f, :] for f in range(HEADS // 2)] + [kr[:, CTX:]])
            attention(nc, t, qn, qr, kn, kr, v, hh[:, :, :LAT], hl[:, :, :LAT])
        dense(nc, "c_out_mm", d["mla_w_out"], KD, KD, hh, hl, ((0, LAT),),
              evac_dve=into_residual(nc, x2, mods, 64, both[1:]))
        rms_mod(nc, t, "rms_f1", x2, LAT_ONLY, mods, 72, hh, hl)
        ffn(nc, t, "f1", 1, x2, hh, hl, LAT_ONLY, both[1:], mods, 88)
        normed(nc, t, "final", x2, KD, LAT_ONLY, t["over_d"], 1e-6, False, [lambda k: col(t, "final_g_2", k)],
               None, None, None, out=x2, store=lambda t0, n: out[:, :, t0 - CTX:t0 - CTX + n])
        late.close()


def build(nc, d, out):
    with ExitStack() as mem:
        t = setup(nc, d, mem)
        t["dram"] = d

        def keep(name, shape, dt=F32, where=mem, side=None):
            t[name] = where.enter_context(nc.sbuf_tensor(name, shape, dt, side=side))
            return t[name]

        tail = ExitStack()
        x_dram = nc.dram_tensor("x_kept", (P, KD, T), F32, kind="Internal").ap()
        mods = keep("mods", [P, 24, 2])
        mods2 = keep("mods2", [P, 96, 2])
        x2 = keep("x2", [P, KD, T], side="right", where=tail)
        gemv_mods(nc, "mod", d["mod_w"], 16, d["vec_1"], mods,
                  also=[(x2[:, :, :CTX], d["ctx"]), (x2[:, :, CTX:], d["x"])])
        modulation(nc, t, "mods", 0, cols_of(t, "mod_b")[:, :16], (8,))
        with ExitStack() as first:
            o_hgrn = keep("o_hgrn", [P, NR, LAT], where=first)
            w_up, a_up = (keep(name, [P, D_RWKV], where=first) for name in ("w_up", "a_up"))
            hidden = ExitStack()
            hh = keep("hh", [P, KD, T], F32R, where=hidden)
            hl = keep("hl", [P, KD, T], F32R, where=hidden)
            normed(nc, t, "ln0", x2, KD, SEGS, t["over_d"], 1e-5, True,
                   [lambda k, j=j: mods[:, 8 + k, j:j + 1] for j in (1, 0)],
                   [lambda k, j=j: mods[:, k, j:j + 1] for j in (1, 0)], hh, hl,
                   also=[(w_up[:, :], d["w_up"]), (a_up[:, :], d["a_up"])])
            tail.close()
            with ExitStack() as part:
                p_hgrn = keep("p_hgrn", [P, 12, T], where=part)

                def copy_out(act, i, ps, slot):
                    for (t0, n), b in zip(SEGS, ps):
                        ins = nc.scalar.activation(p_hgrn[:, bass.ds(i, 1), t0:t0 + n], b[:, :n], ACT.Copy)
                    return ins
                dense(nc, "p_hgrn_mm", d["w_in"], 12, KD, hh, hl, SEGS, evac_act=copy_out, first=O_HGRN,
                      side=Gemv(d["ada_w"], d["vec_2"], mods2, 0, 2))
                hgrn(nc, t, p_hgrn, o_hgrn, part)
            branches = ExitStack()
            pooled = keep("pooled", [P, 2, LAT], where=branches, side="right")
            with ExitStack() as part:
                p_pool = keep("p_pool", [P, 2, POOL_ROWS, GRID + 2 * POOL_PAD], where=part)
                clear(nc, "pool_clear", p_pool[:, :, :, :])

                def pool_out(act, i, ps, slot):
                    return nc.scalar.activation(
                        p_pool[:, bass.ds(i, 1), :, POOL_PAD:POOL_PAD + GRID].rearrange("p a r c -> p (a r) c"),
                        ps[0][:, :].rearrange("p (r c) -> p r c", c=GRID), ACT.Copy)
                dense(nc, "pool_mm", d["w_in"], 2, KD, hh, hl, LAT_ONLY, evac_act=pool_out, first=O_POOL,
                      side=Gemv(d["ada_w"], d["vec_2"], mods2, 24, 1))
                pool_branch(nc, t, p_pool, pooled)

            gate_dram = nc.dram_tensor("gate_kept", (P, KD, LAT), F32, kind="Internal").ap()
            with ExitStack() as part:
                gate = keep("gate", [P, KD, LAT], where=part)

                def gate_out(act, i, ps, slot):
                    return nc.scalar.activation(gate[:, bass.ds(i, 1), :], ps[0][:, :], ACT.Silu)
                dense(nc, "gate_mm", d["w_in"], KD, KD, hh, hl, LAT_ONLY, evac_act=gate_out, first=O_GATE,
                      warm=ACT.Silu, side=Gemv(d["mod_w"], d["vec_1"], mods, 16, 1))
                u = keep("u", [P, N_RWKV_IN, T], where=branches, side="right")
                dense(nc, "u_mm", d["w_in"], N_RWKV_IN, KD, hh, hl, SEGS, first=O_RWKV,
                      evac=three_taps(nc, t, "rwkv_shift", N_RWKV_IN,
                                      lambda i, t0, n: u[:, bass.ds(i, 1), t0:t0 + n], SEGS),
                      side=Gemv(d["ada_w"], d["vec_2"], mods2, 26, 2), also=[(gate_dram, gate[:, :, :])])
            hidden.close()
            y = keep("y_rwkv", [P, NR, LAT], where=first)
            with ExitStack() as part:
                rwkv(nc, t, u, y, part)
            hh = keep("mix_h", [P, KD, LAT], F32R, where=first)
            hl = keep("mix_l", [P, KD, LAT], F32R, where=first)
            parts = [pooled[:, f, :] for f in range(2)] + [y[:, f, :] for f in range(NR)] + \
                [o_hgrn[:, f, :] for f in range(NR)]
            gate = keep("gate_back", [P, KD, LAT], where=first)
            load(nc, "gate_load", [(gate[:, :, :], gate_dram)])
            x2 = keep("x2b", [P, KD, T], where=first)
            gated(nc, "mix", parts, [gate[:, k, :] for k in range(KD)], hh, hl, LAT,
                  also=[(x2[:, :, CTX:], d["x"])], factor=ALPHA)
            branches.close()
            modulation(nc, t, "mods", 16, cols_of(t, "mod_b")[:, 16:], ())
            dense(nc, "w_out_mm", d["w_out"], KD, KD, hh, hl, ((0, LAT),),
                  evac_dve=into_residual(nc, x2, mods, 16, [(CTX, LAT, 0)]))
            x3 = keep("x3", [P, KD, T], where=tail, side="right")
            modulation(nc, t, "mods2", 0, cols_of(t, "ada_b_2")[:, :48], (8, 32),
                       (cols_of(t, "norm1_g_2")[:, :KD], cols_of(t, "norm2_g_2")[:, :KD]))
            normed(nc, t, "ln1", x2, KD, LAT_ONLY, t["over_d"], 1e-5, True,
                   [lambda k: col(t, "ln_g", k)], [lambda k: col(t, "ln_b", k)], None, None, out=x3,
                   also=[(x3[:, :, :CTX], d["ctx_2"])])
        second(nc, d, t, out, x_dram, x3, tail, keep)


def kernel(**inputs):
    import concourse.bacc as bacc
    from concourse.bass_utils import run_bass_kernel_spmd

    arrays = lay_out(inputs)
    nc = bacc.Bacc("TRN2", target_bir_lowering=False, num_devices=1)
    dram = {name: nc.dram_tensor(f"in_{name}", a.shape, mybir.dt.from_np(a.dtype), kind="ExternalInput").ap()
            for name, a in arrays.items()}
    out = nc.dram_tensor("out_y", (P, KD, LAT), F32, kind="ExternalOutput").ap()
    build(nc, dram, out)
    r = run_bass_kernel_spmd(nc, [{f"in_{k}": v for k, v in arrays.items()}], core_ids=[0])
    y = r.results[0]["out_y"]
    return np.ascontiguousarray(y.transpose(2, 1, 0).reshape(1, LAT, D))
```
